# Optimizing a Trainium2 kernel written in Bass

```python
import jax, jax.numpy as jnp
from jax import lax
import numpy as np

D_MODEL = 1024
BATCH = 1
SEQ = 1024
DEPTH = 1

GRID_W = 64
EPS = 1e-6
D_MIX = D_MODEL
NA_HEAD_DIM = 64
NA_WIDTH = D_MIX // 2
NA_HEADS = NA_WIDTH // NA_HEAD_DIM
NA_KH = 8
NA_KW = 16
DN_HEAD_DIM = 128
DN_WIDTH = D_MIX - NA_WIDTH
DN_HEADS = DN_WIDTH // DN_HEAD_DIM
DN_CONV = 5
DN_CHUNK = 64
IN_SIZES = (NA_WIDTH,) * 4 + (DN_WIDTH,) * 4 + (DN_HEADS,) * 4
D_IN = sum(IN_SIZES)


def _rmsnorm(x, w):
    xf = x.astype(jnp.float32)
    y = xf * lax.rsqrt(jnp.mean(xf * xf, axis=-1, keepdims=True) + EPS) * w.astype(jnp.float32)
    return y.astype(x.dtype)

def _l2norm(t):
    return t * lax.rsqrt(jnp.sum(t * t, axis=-1, keepdims=True) + EPS)

def _split_proj(p):
    offsets = [int(o) for o in np.cumsum(IN_SIZES)[:-1]]
    return jnp.split(p, offsets, axis=-1)

def _neighbourhood_attention(q, k, v, rpb):
    B, L, H, Dh = q.shape
    rows = L // GRID_W
    kh = min(NA_KH, rows)
    to_grid = lambda t: t.reshape(B, rows, GRID_W, H, Dh).transpose(0, 3, 1, 2, 4)
    qg, kg, vg = to_grid(q), to_grid(k), to_grid(v)
    cols = np.arange(GRID_W)
    cs = np.clip(cols - NA_KW // 2, 0, GRID_W - NA_KW)
    col_idx = cs[:, None] + np.arange(NA_KW)[None, :]
    col_bias = rpb[:, :, col_idx - cols[:, None] + NA_KW - 1]
    scale = Dh ** -0.5

    def row_fn(r):
        rs = jnp.clip(r - kh // 2, 0, rows - kh)
        q_r = lax.dynamic_index_in_dim(qg, r, axis=2, keepdims=False)
        k_sel = jnp.take(lax.dynamic_slice_in_dim(kg, rs, kh, axis=2), col_idx, axis=3)
        v_sel = jnp.take(lax.dynamic_slice_in_dim(vg, rs, kh, axis=2), col_idx, axis=3)
        dr = rs + jnp.arange(kh) - r + NA_KH - 1
        bias = jnp.take(col_bias, dr, axis=1).transpose(0, 2, 1, 3)
        s = jnp.einsum('bhwd,bhiwjd->bhwij', q_r, k_sel).astype(jnp.float32) * scale + bias.astype(jnp.float32)
        p = jax.nn.softmax(s.reshape(B, H, GRID_W, kh * NA_KW), axis=-1).reshape(s.shape).astype(v.dtype)
        return jnp.einsum('bhwij,bhiwjd->bhwd', p, v_sel)

    o = lax.map(row_fn, jnp.arange(rows))
    return o.transpose(1, 0, 3, 2, 4).reshape(B, L, H * Dh)

def _centred_depthwise_conv(x, w):
    c = x.shape[-1]
    return lax.conv_general_dilated(
        x, w[:, None, :].astype(x.dtype), window_strides=(1,),
        padding=[(DN_CONV // 2, DN_CONV // 2)],
        dimension_numbers=('NWC', 'WIO', 'NWC'), feature_group_count=c)

def _gated_delta_chunked(q, k, v, g, beta):
    B, H, L, Dk = q.shape
    Dv = v.shape[-1]
    C = DN_CHUNK
    N = L // C
    q = q * (Dk ** -0.5)
    ch = lambda t: t.reshape((B, H, N, C) + t.shape[3:])
    q, k, v, g, beta = ch(q), ch(k), ch(v), ch(g), ch(beta)
    g = jnp.cumsum(g, axis=-1)
    tri = np.tril(np.ones((C, C), dtype=bool))
    strict = np.tril(np.ones((C, C), dtype=bool), -1)
    diff = g[..., :, None] - g[..., None, :]
    decay = jnp.where(tri, jnp.exp(jnp.where(tri, diff, 0.0)), 0.0)
    kb = k * beta[..., None]
    a_mat = jnp.where(strict, jnp.einsum('bhncd,bhnsd->bhncs', kb, k) * decay, 0.0) + jnp.eye(C, dtype=jnp.float32)
    rhs = jnp.concatenate([v * beta[..., None], kb * jnp.exp(g)[..., None]], axis=-1)
    sol = lax.linalg.triangular_solve(a_mat, rhs, left_side=True, lower=True, unit_diagonal=True)
    u, w = sol[..., :Dv], sol[..., Dv:]
    intra = jnp.einsum('bhncd,bhnsd->bhncs', q, k) * decay

    def step(S, inp):
        q_c, k_c, u_c, w_c, g_c, a_c = inp
        v_new = u_c - jnp.einsum('bhcd,bhde->bhce', w_c, S)
        o = jnp.einsum('bhcd,bhde->bhce', q_c * jnp.exp(g_c)[..., None], S) + jnp.einsum('bhcs,bhse->bhce', a_c, v_new)
        g_last = g_c[..., -1]
        S = S * jnp.exp(g_last)[..., None, None] + jnp.einsum(
            'bhcd,bhce->bhde', k_c * jnp.exp(g_last[..., None] - g_c)[..., None], v_new)
        return S, o

    xs = tuple(jnp.moveaxis(t, 2, 0) for t in (q, k, u, w, g, intra))
    S0 = jnp.zeros((B, H, Dk, Dv), jnp.float32)
    _, o = lax.scan(step, S0, xs)
    return jnp.moveaxis(o, 0, 2).reshape(B, H, L, Dv)

def _layer(x, norm_w, w_in, qk_gain_q, qk_gain_k, rpb, conv_w, a_log, dt_bias, dn_norm_w, w_out):
    B, L, _ = x.shape
    h = _rmsnorm(x, norm_w)
    proj = jnp.einsum('bld,de->ble', h, w_in)
    aq, ak, av, az, dq, dk, dv, dz, b_f, a_f, b_b, a_b = _split_proj(proj)
    heads = lambda t, n: t.reshape(B, L, n, -1)

    aq = _rmsnorm(heads(aq, NA_HEADS), qk_gain_q)
    ak = _rmsnorm(heads(ak, NA_HEADS), qk_gain_k)
    attn = _neighbourhood_attention(aq, ak, heads(av, NA_HEADS), rpb) * jax.nn.silu(az)

    qkv = jax.nn.silu(_centred_depthwise_conv(jnp.concatenate([dq, dk, dv], axis=-1), conv_w))
    dq, dk, dv = jnp.split(qkv, 3, axis=-1)
    to_bhld = lambda t: heads(t, DN_HEADS).astype(jnp.float32).transpose(0, 2, 1, 3)
    dq, dk, dv = _l2norm(to_bhld(dq)), _l2norm(to_bhld(dk)), to_bhld(dv)

    def gates(b, a, d):
        beta = jax.nn.sigmoid(b.astype(jnp.float32))
        g = -jnp.exp(a_log[d].astype(jnp.float32)) * jax.nn.softplus(a.astype(jnp.float32) + dt_bias[d].astype(jnp.float32))
        return g.transpose(0, 2, 1), beta.transpose(0, 2, 1)

    g_f, beta_f = gates(b_f, a_f, 0)
    g_b, beta_b = gates(b_b, a_b, 1)
    flip = lambda t: jnp.flip(t, axis=2)
    o_f = _gated_delta_chunked(dq, dk, dv, g_f, beta_f)
    o_b = flip(_gated_delta_chunked(flip(dq), flip(dk), flip(dv), flip(g_b), flip(beta_b)))
    o = (o_f + o_b).transpose(0, 2, 1, 3)
    o = o * lax.rsqrt(jnp.mean(o * o, axis=-1, keepdims=True) + EPS) * dn_norm_w.astype(jnp.float32)
    o = o * jax.nn.silu(heads(dz, DN_HEADS).astype(jnp.float32))
    delta = o.reshape(B, L, DN_WIDTH).astype(x.dtype)

    y = jnp.einsum('ble,ed->bld', jnp.concatenate([attn, delta], axis=-1), w_out)
    return x + y

def first_inputs(seed: int = 0) -> dict:
    key = jax.random.key(seed)
    ks = jax.random.split(key, 12)
    f32 = jnp.float32
    x = jax.random.normal(ks[0], (BATCH, SEQ, D_MODEL), f32)
    norm_w = 1.0 + 0.02 * jax.random.normal(ks[1], (DEPTH, D_MODEL), f32)
    w_in = jax.random.normal(ks[2], (DEPTH, D_MODEL, D_IN), f32) * D_MODEL ** -0.5
    qk_gain_q = 1.0 + 0.02 * jax.random.normal(ks[3], (DEPTH, NA_HEAD_DIM), f32)
    qk_gain_k = 1.0 + 0.02 * jax.random.normal(ks[4], (DEPTH, NA_HEAD_DIM), f32)
    rpb = 0.02 * jax.random.normal(ks[5], (DEPTH, NA_HEADS, 2 * NA_KH - 1, 2 * NA_KW - 1), f32)
    conv_w = jax.random.normal(ks[6], (DEPTH, DN_CONV, 3 * DN_WIDTH), f32) * DN_CONV ** -0.5
    a_log = jnp.log(jax.random.uniform(ks[7], (DEPTH, 2, DN_HEADS), f32, 1.0, 16.0))
    u = jax.random.uniform(ks[8], (DEPTH, 2, DN_HEADS), f32)
    dt = jnp.exp(u * (jnp.log(0.1) - jnp.log(0.001)) + jnp.log(0.001))
    dt_bias = dt + jnp.log(-jnp.expm1(-dt))
    dn_norm_w = 1.0 + 0.02 * jax.random.normal(ks[9], (DEPTH, DN_HEAD_DIM), f32)
    w_out = jax.random.normal(ks[10], (DEPTH, D_MIX, D_MODEL), f32) * D_MIX ** -0.5
    return {'x': x, 'norm_w': norm_w, 'w_in': w_in, 'qk_gain_q': qk_gain_q, 'qk_gain_k': qk_gain_k,
            'rpb': rpb, 'conv_w': conv_w, 'a_log': a_log, 'dt_bias': dt_bias,
            'dn_norm_w': dn_norm_w, 'w_out': w_out}

def first_block(x, norm_w, w_in, qk_gain_q, qk_gain_k, rpb, conv_w, a_log, dt_bias, dn_norm_w, w_out):
    for l in range(DEPTH):
        x = _layer(x, norm_w[l], w_in[l], qk_gain_q[l], qk_gain_k[l], rpb[l], conv_w[l],
                   a_log[l], dt_bias[l], dn_norm_w[l], w_out[l])
    return x


CHUNK = 64
Q_BLOCK = 128
SB_HEADS = 8
SB_HEAD_DIM = D_MODEL // SB_HEADS
SB_WIDTH = SB_HEADS * SB_HEAD_DIM
RET_HEADS = 4
RET_KEY_DIM = D_MODEL // RET_HEADS
RET_VAL_DIM = D_MODEL // RET_HEADS
RET_QK_WIDTH = RET_HEADS * RET_KEY_DIM
RET_WIDTH = RET_HEADS * RET_VAL_DIM
ROPE_BASE = 10000.0
SPLIT_SIZES = (SB_WIDTH, SB_WIDTH, SB_WIDTH, SB_WIDTH,
               RET_QK_WIDTH, RET_QK_WIDTH, RET_WIDTH, RET_WIDTH,
               D_MODEL, D_MODEL)
IN_COLS = sum(SPLIT_SIZES)
SPLIT_POINTS = tuple(int(v) for v in np.cumsum(SPLIT_SIZES)[:-1])


def rms_norm(x, gain):
    xf = x.astype(jnp.float32)
    y = xf * lax.rsqrt(jnp.mean(xf * xf, axis=-1, keepdims=True) + EPS)
    return (y * gain.astype(jnp.float32)).astype(x.dtype)

def split_heads(t, n_heads):
    b, s, w = t.shape
    return t.reshape(b, s, n_heads, w // n_heads).transpose(0, 2, 1, 3)

def merge_heads(t):
    b, h, s, d = t.shape
    return t.transpose(0, 2, 1, 3).reshape(b, s, h * d)

def rotary(t):
    s, d = t.shape[2], t.shape[3]
    inv_freq = ROPE_BASE ** (-jnp.arange(0, d, 2, dtype=jnp.float32) / d)
    ang = jnp.arange(s, dtype=jnp.float32)[:, None] * inv_freq[None, :]
    cos, sin = jnp.cos(ang), jnp.sin(ang)
    tf = t.astype(jnp.float32)
    t1, t2 = tf[..., : d // 2], tf[..., d // 2:]
    out = jnp.concatenate([t1 * cos - t2 * sin, t1 * sin + t2 * cos], axis=-1)
    return out.astype(t.dtype)

def stick_breaking_attention(q, k, v):
    b, h, s, d = q.shape
    nb = s // Q_BLOCK
    qb = q.reshape(b, h, nb, Q_BLOCK, d).transpose(2, 0, 1, 3, 4)
    kpos = jnp.arange(s)
    scale = d ** -0.5

    def block(args):
        qi, i = args
        z = jnp.einsum('bhqd,bhkd->bhqk', qi, k).astype(jnp.float32) * scale
        qpos = i * Q_BLOCK + jnp.arange(Q_BLOCK)
        mask = kpos[None, :] < qpos[:, None]
        log_keep = jnp.where(mask, jax.nn.log_sigmoid(-z), 0.0)
        suffix = lax.cumsum(log_keep, axis=3, reverse=True) - log_keep
        w = jnp.where(mask, jnp.exp(jax.nn.log_sigmoid(z) + suffix), 0.0)
        return jnp.einsum('bhqk,bhkd->bhqd', w.astype(v.dtype), v)

    out = lax.map(block, (qb, jnp.arange(nb)))
    return out.transpose(1, 2, 0, 3, 4).reshape(b, h, s, d)

def chunkwise_retention(q, k, v):
    dtype = v.dtype
    q, k, v = (a.astype(jnp.float32) for a in (q, k, v))
    b, h, s, dk = q.shape
    dv = v.shape[-1]
    n = s // CHUNK
    log_gamma = jnp.log1p(-jnp.exp2(-5.0 - jnp.arange(h, dtype=jnp.float32)))
    qc = q.reshape(b, h, n, CHUNK, dk)
    kc = k.reshape(b, h, n, CHUNK, dk)
    vc = v.reshape(b, h, n, CHUNK, dv)
    idx = jnp.arange(CHUNK, dtype=jnp.float32)
    intra_decay = jnp.exp(log_gamma[:, None, None] * jnp.abs(idx[:, None] - idx[None, :]))
    scores = jnp.einsum('bhnqd,bhnkd->bhnqk', qc, kc) * intra_decay[None, :, None]
    intra = jnp.einsum('bhnqk,bhnke->bhnqe', scores, vc)
    q_decay = jnp.exp(log_gamma[:, None] * (idx + 1.0))[None, :, :, None]
    k_decay = jnp.exp(log_gamma[:, None] * (CHUNK - 1.0 - idx))[None, :, :, None]
    chunk_decay = jnp.exp(log_gamma * CHUNK)[None, :, None, None]

    def step(state, inp):
        qi, ki, vi = inp
        out = jnp.einsum('bhqd,bhde->bhqe', qi * q_decay, state)
        state = state * chunk_decay + jnp.einsum('bhkd,bhke->bhde', ki * k_decay, vi)
        return state, out

    init = jnp.zeros((b, h, dk, dv), jnp.float32)
    xs = (qc.transpose(2, 0, 1, 3, 4), kc.transpose(2, 0, 1, 3, 4), vc.transpose(2, 0, 1, 3, 4))
    _, inter = lax.scan(step, init, xs)
    out = intra + inter.transpose(1, 2, 0, 3, 4)
    return out.reshape(b, h, s, dv).astype(dtype)

def second_inputs(seed: int = 0) -> dict:
    key = jax.random.key(seed)
    ks = jax.random.split(key, 10)
    f32 = jnp.float32
    x = jax.random.normal(ks[0], (BATCH, SEQ, D_MODEL), f32)
    norm_gain = 1.0 + 0.05 * jax.random.normal(ks[1], (DEPTH, D_MODEL), f32)
    w_in = jax.random.normal(ks[2], (DEPTH, D_MODEL, IN_COLS), f32) * D_MODEL ** -0.5
    b_merge = 0.01 * jax.random.normal(ks[3], (DEPTH, 2, D_MODEL), f32)
    sb_q_gain = 1.0 + 0.05 * jax.random.normal(ks[4], (DEPTH, SB_HEAD_DIM), f32)
    sb_k_gain = 1.0 + 0.05 * jax.random.normal(ks[5], (DEPTH, SB_HEAD_DIM), f32)
    ret_out_gain = 1.0 + 0.05 * jax.random.normal(ks[6], (DEPTH, RET_HEADS, RET_VAL_DIM), f32)
    w_branch_sb = jax.random.normal(ks[7], (DEPTH, SB_WIDTH, D_MODEL), f32) * SB_WIDTH ** -0.5
    w_branch_ret = jax.random.normal(ks[8], (DEPTH, RET_WIDTH, D_MODEL), f32) * RET_WIDTH ** -0.5
    w_out = jax.random.normal(ks[9], (DEPTH, D_MODEL, D_MODEL), f32) * D_MODEL ** -0.5
    return {"x": x, "norm_gain": norm_gain, "w_in": w_in, "b_merge": b_merge,
            "sb_q_gain": sb_q_gain, "sb_k_gain": sb_k_gain, "ret_out_gain": ret_out_gain,
            "w_branch_sb": w_branch_sb, "w_branch_ret": w_branch_ret, "w_out": w_out}

def second_block(x, norm_gain, w_in, b_merge, sb_q_gain, sb_k_gain, ret_out_gain,
              w_branch_sb, w_branch_ret, w_out):
    for layer in range(DEPTH):
        h = rms_norm(x, norm_gain[layer])
        proj = jnp.einsum('bsd,dc->bsc', h, w_in[layer])
        (sb_q, sb_k, sb_v, sb_g, r_q, r_k, r_v, r_g, m_sb, m_ret) = jnp.split(proj, SPLIT_POINTS, axis=-1)

        qa = rms_norm(split_heads(sb_q, SB_HEADS), sb_q_gain[layer])
        ka = rms_norm(split_heads(sb_k, SB_HEADS), sb_k_gain[layer])
        va = split_heads(sb_v, SB_HEADS)
        out_a = merge_heads(stick_breaking_attention(qa, ka, va)) * jax.nn.silu(sb_g)

        qb = rotary(split_heads(r_q, RET_HEADS))
        kb = rotary(split_heads(r_k, RET_HEADS)) * (RET_KEY_DIM ** -0.5)
        vb = split_heads(r_v, RET_HEADS)
        ret = chunkwise_retention(qb, kb, vb)
        ret = rms_norm(ret, ret_out_gain[layer][None, :, None, :])
        out_b = merge_heads(ret) * jax.nn.silu(r_g)

        p_a = jnp.einsum('bsw,wd->bsd', out_a, w_branch_sb[layer])
        p_b = jnp.einsum('bsw,wd->bsd', out_b, w_branch_ret[layer])
        merged = (jax.nn.sigmoid(m_sb + b_merge[layer, 0]) * p_a
                  + jax.nn.sigmoid(m_ret + b_merge[layer, 1]) * p_b)
        x = x + jnp.einsum('bsd,de->bse', merged, w_out[layer])
    return x


def setup_inputs(seed=0):
    out = dict(first_inputs(seed))
    for name, value in second_inputs(seed + 1).items():
        if name != "x":
            out[name + "_2"] = value
    return out


def reference(
    x, norm_w, w_in, qk_gain_q, qk_gain_k, rpb, conv_w, a_log, dt_bias, dn_norm_w, w_out,
    norm_gain_2, w_in_2, b_merge_2, sb_q_gain_2, sb_k_gain_2, ret_out_gain_2, w_branch_sb_2,
    w_branch_ret_2, w_out_2,
):
    x = first_block(
        x, norm_w, w_in, qk_gain_q, qk_gain_k, rpb, conv_w, a_log, dt_bias, dn_norm_w, w_out,
    )
    return second_block(
        x, norm_gain_2, w_in_2, b_merge_2, sb_q_gain_2, sb_k_gain_2, ret_out_gain_2,
        w_branch_sb_2, w_branch_ret_2, w_out_2,
    )


_drawn_inputs = setup_inputs


def setup_inputs(seed=0):
    import zlib

    import numpy as np

    out = dict(_drawn_inputs(seed))
    spreads = {}
    factors = {'norm_w': 3.753,
     'qk_gain_q': 8.0,
     'qk_gain_k': 8.0,
     'rpb': 41.444,
     'dn_norm_w': 16.819,
     'b_merge_2': 64.0,
     'sb_q_gain_2': 64.0,
     'sb_k_gain_2': 64.0,
     'ret_out_gain_2': 33.24,
     'norm_gain_2': 4.203}
    for name, (base, spread) in spreads.items():
        noise = np.random.default_rng([zlib.crc32(name.encode()), seed]).standard_normal(out[name].shape)
        drawn = base * np.exp(spread * noise) if base else spread * noise
        out[name] = __import__('jax').numpy.asarray(drawn.astype(out[name].dtype))
    for name, factor in factors.items():
        out[name] = (out[name] * factor).astype(out[name].dtype)
    return out
```

```python
import numpy as np
import concourse.bass as bass
from concourse import mybir
from concourse.alu_op_type import AluOpType as ALU
from contextlib import ExitStack

F32 = mybir.dt.float32
F32R = mybir.dt.float32r
ACT = mybir.ActivationFunctionType
AX = mybir.AxisListType

EPS = 1e-6
NEG = -1.0e30


class Queue:

    def __init__(self, sem, chained):
        self.sem, self.chained = sem, chained
        self.n = 0
        self.seen = {}
        self.items = []

    def put(self, fn, after=(), sig=True, free=False):
        waits = []
        own = [(self.sem, self.n)] if self.chained and not free and self.n else []
        for sem, v in [*after, *own]:
            if self.seen.get(id(sem), 0) < v:
                self.seen[id(sem)] = v
                waits.append((sem, v))
        self.items.append((waits, fn, sig))
        if sig:
            self.n += 1
        return (self.sem, self.n)

    def last(self):
        return (self.sem, self.n)

    def play(self, eng):
        for waits, fn, sig in self.items:
            best = {}
            for sem, v in waits:
                if id(sem) not in best or best[id(sem)][1] < v:
                    best[id(sem)] = (sem, v)
            for sem, v in best.values():
                eng.wait_ge(sem, v)
            ins = fn(eng)
            if sig is True:
                ins.then_inc(self.sem, 1)
            elif sig:
                ins.then_inc(sig, 16)


class Slot:

    def __init__(self, sem):
        self.sem, self.n = sem, 0

    def token(self):
        return (self.sem, self.n)


def build(nc, x, norm_w, w_in, gq, gk, rpb, conv_w, a_log, dt_bias, dn_w, w_out,
          gain2, w_in2, b_merge, sbq, sbk, ret_gain, w_sb, w_ret, w_out2,
          masks, cossin, retmask, retcol, out):
    ctx = ExitStack()
    with ctx:
        def sb(name, shape, dt=F32):
            return ctx.enter_context(nc.sbuf_tensor(name, shape, dt))

        def semaphore(name):
            return ctx.enter_context(nc.semaphore(name))

        def scratch(name, shape):
            return nc.dram_tensor(name, shape, F32, kind="Internal").ap()

        mix_d = scratch("mix_d", [1024, 1024])
        x1_d = scratch("x1_d", [1024, 1024])
        oa_d = scratch("oa_d", [1024, 1024])
        ob_d = scratch("ob_d", [1024, 1024])
        sig_d = scratch("sig_d", [2, 1024, 1024])
        dz_d = scratch("dz_d", [1024, 512])

        HH = sb("HH", [128, 8, 1024], F32R)
        HL = sb("HL", [128, 8, 1024], F32R)
        NSLOT = 12
        WH = sb("WH", [128, NSLOT, 1024], F32R)
        NRAW = 4
        RAW = sb("RAW", [128, NRAW, 512])
        TM = sb("TM", [128, 3, 4096])
        WKW = 10160
        WK = sb("WK", [128, WKW])
        PS = ctx.enter_context(nc.psum_tensor("PS", [128, 4096], F32))

        def bank(n, w=512, o=0):
            return PS[:, n * 512 + o:n * 512 + o + w]

        pe = Queue(semaphore("s_pe"), False)
        act = Queue(semaphore("s_act"), True)
        dve = Queue(semaphore("s_dve"), True)
        pool = Queue(semaphore("s_pool"), True)
        sp = Queue(semaphore("s_sp"), False)
        slots = []

        def slot(name):
            s = Slot(semaphore(name))
            slots.append(s)
            return s

        def mm(o, l, r, start, stop, after=(), sig=False):
            return pe.put(lambda e: e.matmul(o, l, r, start=start, stop=stop), after, sig)

        def tr(o, i, after=(), sig=False):
            p = i.shape[0]
            b = i.base_partition() if callable(i.base_partition) else i.base_partition
            idn = ident[b:b + p, b:b + p] if p < 128 else ident
            return pe.put(lambda e: e.transpose(o, i, idn), after, sig)

        def af(o, i, func, after=(), **kw):
            return act.put(lambda e: e.activation(o, i, func, **kw), after)

        def tt(q, o, a, b, op, after=()):
            return q.put(lambda e: e.tensor_tensor(o, a, b, op), after)

        def ts(q, o, a, s1, s2, op0, op1=None, after=()):
            if op1 is None:
                return q.put(lambda e: e.tensor_scalar(o, a, s1, None, op0), after)
            return q.put(lambda e: e.tensor_scalar(o, a, s1, s2, op0, op1), after)

        def stt(o, a, s, b, op0, op1, after=()):
            return dve.put(lambda e: e.scalar_tensor_tensor(out=o, in0=a, scalar=s, in1=b, op0=op0, op1=op1), after)

        def red(o, i, op, after=(), axis=AX.X):
            return dve.put(lambda e: e.tensor_reduce(o, i, axis, op), after)

        def recip(o, i, after=()):
            return dve.put(lambda e: e.reciprocal(o, i), after)

        def mset(q, o, v, after=()):
            return q.put(lambda e: e.memset(o, v), after)

        def dma(q, s, o, i, after=()):
            if q is sp:
                sp.put(lambda e: e.dma_start(o, i), after, s.sem)
                sp.n -= 1
            else:
                q.put(lambda e: e.dma_start(o, i), after, s.sem)
                q.n -= 1
            s.n += 16
            return s.token()

        class Area:
            def __init__(self, at):
                self.at = at

            def take(self, n):
                a = self.at
                self.at += n
                assert self.at <= WKW, self.at
                return WK[:, a:a + n]

        keep = Area(0)
        ident = keep.take(128)
        one = keep.take(1)
        half = keep.take(1)
        nw = keep.take(8)
        nw2 = keep.take(8)
        naq, nak, sq_, sk_ = (keep.take(1) for _ in range(4))
        ss = keep.take(64)
        rs = keep.take(64)
        base = keep.at

        c_const = slot("c_const")
        dma(sp, c_const, ident, masks[0])
        dma(sp, c_const, nw, norm_w)
        dma(sp, c_const, nw2, gain2)
        for b in (0, 64):
            dma(sp, c_const, naq[b:b + 64, :], gq)
            dma(sp, c_const, nak[b:b + 64, :], gk)
        dma(sp, c_const, sq_, sbq)
        dma(sp, c_const, sk_, sbk)
        t_const = c_const.token()
        mset(dve, one, 1.0)
        t_one = mset(dve, half, -0.5)
        ts(dve, naq, naq, 0.125, None, ALU.mult, after=[t_const])
        t_gain = ts(dve, sq_, sq_, 128.0 ** -0.5, None, ALU.mult)

        def rsqrt(cols, n, after=()):
            a, r = ss[:, cols[0]:cols[1]], rs[:, cols[0]:cols[1]]
            ts(pool, a, a, 1.0 / n, EPS, ALU.mult, ALU.add, after=[*after, t_one])
            return tt(pool, r, a, half.to_broadcast([128, cols[1] - cols[0]]), ALU.pow)

        def seg(w, k):
            return w[k * 128:(k + 1) * 128, :]

        blocks = []
        w_segs = w_in[:, 0:4096].rearrange("r (s c) -> r s c", c=512)
        w2_segs = w_in2.rearrange("r (s c) -> r s c", c=1024)

        def add_block(width, src):
            blocks.append((width, src))

        for p in range(4):
            add_block(512, lambda k, p=p: w_segs[k * 128:(k + 1) * 128, 0:4, p * 128:(p + 1) * 128])
        add_block(16, lambda k: w_in[k * 128:(k + 1) * 128, 4096:4112])
        add_block(512, lambda k: w_segs[k * 128:(k + 1) * 128, 7, :])
        for h in range(4):
            add_block(384, lambda k, h=h: w_segs[k * 128:(k + 1) * 128, 4:7, h * 128:(h + 1) * 128])
        for cb in range(2):
            add_block(512, lambda k, cb=cb: w_out[k * 128:(k + 1) * 128, cb * 512:(cb + 1) * 512])
        for h in range(8):
            add_block(512, lambda k, h=h: w2_segs[k * 128:(k + 1) * 128, 0:4, h * 128:(h + 1) * 128])
        for h in range(4):
            for s in (4, 6):
                add_block(512, lambda k, h=h, s=s: w2_segs[k * 128:(k + 1) * 128, s:s + 2, h * 256:(h + 1) * 256])
        for s in (8, 9):
            for cb in range(2):
                add_block(512, lambda k, s=s, cb=cb: w2_segs[k * 128:(k + 1) * 128, s, cb * 512:(cb + 1) * 512])
        for w in (w_sb, w_ret, w_out2):
            for cb in range(2):
                add_block(512, lambda k, w=w, cb=cb: w[k * 128:(k + 1) * 128, cb * 512:(cb + 1) * 512])

        tiles = [(b, k) for b in range(len(blocks)) for k in range(8)]
        c_raw = [slot(f"c_raw{i}") for i in range(NRAW)]
        raw_free = [[] for _ in range(NRAW)]
        wh_free = [[] for _ in range(NSLOT)]
        ready = {}
        prepped = [0]
        loaded = [0]

        def load_next():
            n = loaded[0]
            if n >= len(tiles):
                return
            b, k = tiles[n]
            width, src = blocks[b]
            d = RAW[:, n % NRAW, 0:width]
            s = src(k)
            if len(s.shape) == 3:
                d = d.rearrange("p (s c) -> p s c", c=s.shape[2])
            dma(sp, c_raw[n % NRAW], d, s, after=raw_free[n % NRAW])
            loaded[0] += 1

        def prep_next():
            n = prepped[0]
            if n >= len(tiles):
                return
            width = blocks[tiles[n][0]][0]
            r, w = RAW[:, n % NRAW, 0:width], WH[:, n % NSLOT, :]
            arrived = (c_raw[n % NRAW].sem, 16 * (n // NRAW + 1))
            hi = af(w[:, 0:width], r, ACT.Copy, after=[arrived, *wh_free[n % NSLOT]])
            lo = tt(dve, w[:, 512:512 + width], r, w[:, 0:width].bitcast(F32), ALU.subtract, after=[hi])
            ready[n] = lo
            raw_free[n % NRAW] = [lo]
            prepped[0] += 1
            load_next()

        for _ in range(NRAW):
            load_next()

        side = []
        rate = [1]

        def spawn(g):
            side.append(g)

        def pump(n=1):
            for _ in range(n * rate[0]):
                for g in list(side):
                    try:
                        next(g)
                    except StopIteration:
                        side.remove(g)

        def drain():
            while side:
                pump()

        c_side = []

        def fence():
            marks = [q.last() for q in (pe, act, dve, pool)] + [s.token() for s in slots if s.n and s not in c_raw]
            marks = [m for m in marks if m[1]]
            return marks

        cur = [0]
        mb = [0]
        mfree = [[], []]

        def token_groups(consume, after_tile, width=512):
            b = cur[0]
            cur[0] += 1
            assert blocks[b][0] == width
            while prepped[0] < 8 * b + 8:
                prep_next()
            for t in range(8):
                tile_tokens = after_tile(t)
                m = mb[0] % 2
                mb[0] += 1
                ps = bank(m, width)
                for k in range(8):
                    n = 8 * b + k
                    w = WH[:, n % NSLOT, :]
                    aft = [ready[n]]
                    if k == 0:
                        aft += mfree[m] + tile_tokens
                    hh, hl = HH[:, k, t * 128:(t + 1) * 128], HL[:, k, t * 128:(t + 1) * 128]
                    mm(ps, hh, w[:, 0:width], k == 0, False, after=aft)
                    mm(ps, hh, w[:, 512:512 + width], False, False)
                    tok = mm(ps, hl, w[:, 0:width], False, k == 7, sig=(k == 7 or t == 7))
                    if t == 7:
                        wh_free[n % NSLOT] = [tok]
                        prep_next() if prepped[0] < 8 * b + 16 and prepped[0] - NSLOT < 8 * b + k + 1 else None
                    pump()
                mfree[m] = consume(t, ps, tok)
                if t < 7 and prepped[0] < 8 * b + 8 + NSLOT - 8:
                    prep_next()

        def channel_groups(consume, after_tile):
            b = cur[0]
            cur[0] += 1
            while prepped[0] < 8 * b + 8:
                prep_next()
            g = 0
            for c in range(3):
                for th in range(2):
                    m = mb[0] % 2
                    mb[0] += 1
                    ps = bank(m)
                    for k in range(8):
                        n = 8 * b + k
                        w = WH[:, n % NSLOT, :]
                        wh, wl = w[:, c * 128:(c + 1) * 128], w[:, 512 + c * 128:512 + (c + 1) * 128]
                        hh, hl = HH[:, k, th * 512:(th + 1) * 512], HL[:, k, th * 512:(th + 1) * 512]
                        aft = [ready[n]]
                        if k == 0:
                            aft += mfree[m] + after_tile
                        mm(ps, wh, hh, k == 0, False, after=aft)
                        mm(ps, wh, hl, False, False)
                        tok = mm(ps, wl, hh, False, k == 7, sig=(k == 7 or g == 5))
                        if g == 5:
                            wh_free[n % NSLOT] = [tok]
                            prep_next() if prepped[0] < 8 * b + 16 and prepped[0] - NSLOT < 8 * b + k + 1 else None
                        pump()
                    mfree[m] = consume(c, th, ps, tok)
                    if g < 5 and prepped[0] < 8 * b + 8 + NSLOT - 8:
                        prep_next()
                    g += 1

        def to_stationary(t, src, after, scale=None, tmp=None):
            dst = slice(t * 128, (t + 1) * 128)
            for half_ in range(2):
                m = mb[0] % 2
                mb[0] += 1
                ps = bank(m)
                for j in range(4):
                    k = half_ * 4 + j
                    tok = tr(ps[:, j * 128:(j + 1) * 128], src[:, k * 128:(k + 1) * 128],
                             after=[*after, *mfree[m], t_const], sig=(j == 3))
                hh, hl = HH[:, half_ * 4:half_ * 4 + 4, dst], HL[:, half_ * 4:half_ * 4 + 4, dst]
                p4 = ps.rearrange("p (k c) -> p k c", c=128)
                if scale is None:
                    hi = af(hh, p4, ACT.Copy, after=[tok])
                    lo = tt(dve, hl, p4, hh.bitcast(F32), ALU.subtract, after=[hi])
                    mfree[m] = [lo]
                else:
                    sc = scale[:, half_ * 4:half_ * 4 + 4].unsqueeze(2).to_broadcast([128, 4, 128])
                    t4 = tmp.rearrange("p (k c) -> p k c", c=128)
                    a = tt(dve, t4, p4, sc, ALU.mult, after=[tok])
                    mfree[m] = [a]
                    hi = af(hh, t4, ACT.Copy, after=[a])
                    lo = tt(dve, hl, t4, hh.bitcast(F32), ALU.subtract, after=[hi])
            return lo

        area = Area(base)
        junk = area.take(1024)
        tmp = area.take(512)
        c_x = [slot(f"c_x{i}") for i in range(8)]

        def xt(t):
            return TM[:, t // 4, (t % 4) * 1024:(t % 4 + 1) * 1024]

        for t in range(8):
            dma(sp, c_x[t], xt(t), x[t * 128:(t + 1) * 128, :])
        for t in range(8):
            s = af(junk, xt(t), ACT.Square, after=[c_x[t].token()], accum_out=ss[:, t:t + 1])
        r = rsqrt((0, 8), 1024, after=[s])
        ht = {}
        for t in range(8):
            a = ts(dve, xt(t), xt(t), rs[:, t:t + 1], None, ALU.mult, after=[r])
            ht[t] = to_stationary(t, xt(t), [a], nw, tmp)

        for _ in range(8):
            prep_next()

        area = Area(base)
        tab = [area.take(23 * 64).rearrange("p (j c) -> p j c", c=64) for _ in range(2)]
        qT = area.take(1024)
        kT = area.take(1024)
        S = [area.take(576) for _ in range(2)]
        PT = [area.take(640) for _ in range(2)]
        nm = area.take(2)
        sums = area.take(2)
        rinv = area.take(2)
        sqt = area.take(256)
        c_tab = [slot("c_tab0"), slot("c_tab1")]
        c_mix = [slot(f"c_mix{i}") for i in range(3)]
        mark = fence()
        dve.put(lambda e: e.memset(nm, 0.0), mark)
        act.put(lambda e: e.activation(sums, nm, ACT.Copy), [*mark, dve.last()])
        mset(pool, rinv, 0.0, after=[*mark, dve.last()])
        w_start = [dve.last(), act.last(), pool.last()]
        tm_free = [list(fence()) for _ in range(3)]
        tab_free = [list(w_start) for _ in range(2)]

        def load_table(h):
            T = tab[h % 2]
            tok = None
            for ro in range(2):
                src = rpb[h, 1 - ro:15 - ro, :, :].rearrange("j w c -> w j c")
                tok = dma(sp, c_tab[h % 2], T[ro * 64:(ro + 1) * 64, 0:14, :], src, after=tab_free[h % 2])
            F = T[:, 0:14, :]
            for ro in range(2):
                Fh = T[ro * 64:(ro + 1) * 64, 0:14, :]
                a = pool.put(lambda e, Fh=Fh: e.affine_select(
                    out=Fh[:, :, 0:48], in_=Fh[:, :, 0:48], pattern=[[0, 14], [1, 48]], compare_op=ALU.is_ge,
                    fill=NEG, base=8, channel_multiplier=-1), [tok])
                a = pool.put(lambda e, Fh=Fh: e.affine_select(
                    out=Fh[:, :, 16:64], in_=Fh[:, :, 16:64], pattern=[[0, 14], [-1, 48]], compare_op=ALU.is_ge,
                    fill=NEG, base=7 - 16, channel_multiplier=1))
            a = pool.put(lambda e: e.tensor_copy(T[:, 14:23, :], T[:, 2:11, :]))
            a = mset(pool, T[64:128, 14, :], NEG)
            a = mset(pool, T[0:64, 22, :], NEG)
            return a

        def transposed(dst, src, gain, after, bk, free):
            for g in range(2):
                for j in range(4):
                    tok = tr(bank(bk)[:, j * 128:(j + 1) * 128], src(g * 4 + j), after=[*after, *free], sig=(j == 3))
                if gain is None:
                    free = [af(dst[:, g * 512:(g + 1) * 512], bank(bk), ACT.Copy, after=[tok])]
                else:
                    free = [af(dst[:, g * 512:(g + 1) * 512], bank(bk), ACT.Copy, after=[tok, t_gain], scale=gain)]
                yield free

        def silu_in_place(z, e, after=()):
            a = af(e, z, ACT.Exp, after=after, scale=-1.0)
            ts(dve, e, e, 1.0, None, ALU.add, after=[a])
            recip(e, e)
            return tt(dve, z, z, e, ALU.mult)

        state = {"pe_na": [], "table": {}}
        state["table"][0] = load_table(0)
        state["table"][1] = load_table(1)
        done = {}

        def na_side(p, buf, ev):
            B = TM[:, buf, :].rearrange("p (t c) -> p t c", c=512)
            qk = B[:, :, 0:256].rearrange("p t (g d) -> p t g d", d=64)
            r = rsqrt((0, 32), 64, after=[ev])
            yield
            sc = rs[:, 0:32].rearrange("p (t g) -> p t g", g=4)
            for t in range(0, 8, 4):
                a = tt(dve, qk[:, t:t + 4].rearrange("p t g d -> p (t g) d"),
                       qk[:, t:t + 4].rearrange("p t g d -> p (t g) d"),
                       sc[:, t:t + 4].rearrange("p t g -> p (t g)").unsqueeze(2).to_broadcast([128, 16, 64]),
                       ALU.mult, after=[r]) if False else None
            for t in range(8):
                a = tt(dve, qk[:, t], qk[:, t], sc[:, t].unsqueeze(2).to_broadcast([128, 4, 64]), ALU.mult, after=[r])
            yield
            while p and not done.get(("na", p - 1)):
                yield
            free = state["pe_na"]
            for dst, o, g in ((qT, 0, naq), (kT, 128, nak)):
                for f in transposed(dst, lambda t, o=o: B[:, t, o:o + 128], g, [a, *w_start], 4, free):
                    free = f
                    yield
            qk_tok = free[0]
            z, e = B[:, :, 384:512], B[:, :, 0:128]
            sz = silu_in_place(z, e, after=[pe.last()])
            yield
            pt_tok = {}
            for h in range(2):
                hd = 2 * p + h
                tok_tab = state["table"][hd]
                T = tab[hd % 2]
                P = slice(h * 64, h * 64 + 64)
                for i in range(8):
                    n = h * 8 + i
                    Sb, Pb = S[n % 2], PT[n % 2]
                    inner = 2 <= i <= 5
                    k0 = i - 2 if inner else (0 if i < 2 else 4)
                    nk = 576 if inner else 512
                    q = qT[P, i * 128:(i + 1) * 128]
                    tok = mm(PS[:, 1024:1536], q, kT[P, k0 * 128:k0 * 128 + 512], True, True,
                             after=[qk_tok, *state.get("s_free", [])], sig=True)
                    if inner:
                        tok = mm(PS[:, 1536:1600], q, kT[P, k0 * 128 + 512:k0 * 128 + 576], True, True,
                                 after=state.get("c_free", []), sig=True)
                    yield
                    j0 = 14 if inner else 2 * k0 - 2 * i + 7 - 1
                    tb = T[:, j0:j0 + nk // 64, :].rearrange("p j c -> p (j c)")
                    a = tt(dve, Sb[:, 0:nk], PS[:, 1024:1024 + nk], tb, ALU.add, after=[tok, tok_tab, *state.get(("s", n % 2), [])])
                    state["s_free"] = [a]
                    if i == 7:
                        tab_free[hd % 2] = [a]
                    b = dve.put(lambda e, Sb=Sb, nk=nk, n=n: e.tensor_reduce(
                        nm[:, n % 2:n % 2 + 1], Sb[:, 0:nk], AX.X, ALU.max, negate=True), [*state.get(("e", n % 2), [])])
                    ex = af(Sb[:, 0:nk], Sb[:, 0:nk], ACT.Exp, after=[b], bias=nm[:, n % 2:n % 2 + 1],
                            accum_out=sums[:, n % 2:n % 2 + 1])
                    state[("e", n % 2)] = [ex]
                    ri = recip(rinv[:, n % 2:n % 2 + 1], sums[:, n % 2:n % 2 + 1], after=[ex])
                    yield
                    for j in range(4):
                        tok = tr(bank(4)[:, j * 128:(j + 1) * 128], Sb[:, j * 128:(j + 1) * 128],
                                 after=[ex, *state.get("pt_free", [])], sig=(j == 3))
                    if inner:
                        tok = tr(PS[0:64, 1664:1792], Sb[:, 512:576], after=[*state["s_free"]], sig=True)
                    state[("s", n % 2)] = [tok]
                    yield
                    c = af(Pb[:, 0:512], bank(4), ACT.Copy, after=[tok, *pt_tok.get(n % 2, [])])
                    state["pt_free"] = [c]
                    if inner:
                        c = af(Pb[0:64, 512:640], PS[0:64, 1664:1792], ACT.Copy)
                    yield
                    V = B[:, :, 256 + h * 64:256 + h * 64 + 64]
                    O = PS[:, 1920:1984]
                    for j in range(4):
                        tok = mm(O, Pb[:, j * 128:(j + 1) * 128], V[:, k0 + j, :], j == 0, (j == 3) and not inner,
                                 after=[c, *state["s_free"]], sig=(j == 3))
                    if inner:
                        tok = mm(O, Pb[0:64, 512:640], V[0:64, k0 + 4, :], False, True, sig=True)
                    pt_tok[n % 2] = [tok]
                    yield
                    o = stt(B[:, i, 128 + h * 64:128 + h * 64 + 64], O, rinv[:, n % 2:n % 2 + 1],
                            B[:, i, 384 + h * 64:384 + h * 64 + 64], ALU.mult, ALU.mult, after=[tok, sz])
                    state["c_free"] = [o]
                    state["s_free"] = [o]
                    yield
                if hd + 2 < 8:
                    state["table"][hd + 2] = load_table(hd + 2)
            state["pe_na"] = [pe.last()]
            w = dma(sp, c_mix[buf], mix_d.rearrange("(t p) c -> p t c", p=128)[:, :, p * 128:(p + 1) * 128],
                    B[:, :, 128:256], after=[o])
            tm_free[buf] = [w, pe.last(), o]
            done[("na", p)] = True

        def na_consume(buf):
            B = TM[:, buf, :].rearrange("p (t c) -> p t c", c=512)

            def f(t, ps, tok):
                a = af(B[:, t, :], ps, ACT.Copy, after=[tok, *tm_free[buf]])
                q = B[:, t, 0:256]
                tt(dve, sqt, q, q, ALU.mult, after=[a, *w_start, *state.get("rs_free", [])])
                red(ss[:, t * 4:t * 4 + 4], sqt.rearrange("p (g d) -> p g d", d=64), ALU.add)
                return [a]
            return f

        rate[0] = 1
        for p in range(4):
            buf = p % 2
            if p >= 2:
                while not done.get(("na", p - 2)):
                    pump()
            if p:
                state["rs_free"] = [state["used"]]
            token_groups(na_consume(buf), lambda t: [ht[t]])
            ev = dve.last()
            g = na_side(p, buf, ev)
            next(g)
            next(g)
            state["used"] = dve.last()
            spawn(g)
        w_tok = [ht[7]]

        drain()
        area = Area(base)
        mark = fence()
        MK = TM[:, 0, 3088:3088 + 14 * 64].bitcast(mybir.dt.bfloat16).rearrange("p (l d c) -> p l d c", l=7, d=2)
        tri = area.take(256).rearrange("p (d c) -> p d c", d=2)
        onesq = area.take(128)
        dnw = area.take(128)
        cw = area.take(60).rearrange("p (g j) -> p g j", j=5)
        cst = area.take(16)
        gt_in = area.take(128).rearrange("p (t c) -> p t c", c=16)
        G, g_, beta, kdf, eGL, bg = (area.take(64) for _ in range(6))
        gtmp = area.take(64)
        sets = [[area.take(512) for _ in range(7)] for _ in range(2)]
        St = area.take(256).rearrange("p (d c) -> p d c", d=2)
        Vn = area.take(256).rearrange("p (d c) -> p d c", d=2)
        OA = area.take(1024).rearrange("p (t c) -> p t c", c=128)
        mset(dve, onesq, 1.0, after=mark)
        mset(pool, gtmp, 0.0, after=mark)
        af(cst, gt_in[:, 0, :], ACT.Copy, after=mark) if False else act.put(
            lambda e: e.activation(G[:, 0:1], onesq[:, 0:1], ACT.Copy), [*mark, dve.last()])
        c_dn = slot("c_dn")
        dn_mark = [dve.last(), act.last(), pool.last()]
        mk32 = TM[:, 2, 0:14 * 128].rearrange("p (m c) -> p m c", c=128)
        dma(sp, c_dn, mk32, masks[1:15].rearrange("m p c -> p m c"), after=dn_mark + tm_free[2])
        dma(sp, c_dn, tri, masks[15:17].rearrange("m p c -> p m c"), after=dn_mark)
        dma(sp, c_dn, dnw, dn_w.to_broadcast([128, 128]), after=dn_mark)
        dma(sp, c_dn, cw, conv_w, after=dn_mark)
        dma(sp, c_dn, cst[:, 0:8], a_log.to_broadcast([128, 8]), after=dn_mark)
        dma(sp, c_dn, cst[:, 8:16], dt_bias.to_broadcast([128, 8]), after=dn_mark)
        mkt = dve.put(lambda e: e.tensor_copy(MK.rearrange("p l d c -> p (l d) c"), mk32), [c_dn.token(), *tm_free[0]])
        tm_free[2] = [mkt]
        t_dn = c_dn.token()

        def gt_consume(t, ps, tok):
            return [af(gt_in[:, t, :], ps, ACT.Copy, after=[tok, *dn_mark])]

        token_groups(gt_consume, lambda t: [], width=16)
        gv = gt_in.rearrange("p t (d k h) -> p d k h t", d=2, k=2)

        def col(a, d):
            return a[:, d * 32:(d + 1) * 32].rearrange("p (h t) -> p h t", t=8)

        for d in range(2):
            a = af(col(beta, d), gv[:, d, 0], ACT.Exp, scale=-1.0)
        ts(dve, beta, beta, 1.0, None, ALU.add, after=[a])
        recip(beta, beta)
        al = af(cst[:, 0:8], cst[:, 0:8], ACT.Exp, after=[t_dn])
        for d in range(2):
            db = cst[:, 8 + 4 * d:12 + 4 * d].unsqueeze(2).to_broadcast([128, 4, 8])
            a = tt(dve, col(g_, d), gv[:, d, 1], db, ALU.add, after=[t_dn, al])
        a = af(gtmp, g_, ACT.Abs, after=[a, pool.last()])
        a = af(gtmp, gtmp, ACT.Exp, scale=-1.0)
        a = af(gtmp, gtmp, ACT.Ln, bias=1.0)
        stt(g_, g_, 0.0, gtmp, ALU.max, ALU.add, after=[a])
        for d in range(2):
            ab = cst[:, 4 * d:4 * d + 4].unsqueeze(2).to_broadcast([128, 4, 8])
            tt(dve, col(g_, d), col(g_, d), ab, ALU.mult)
        gg = ts(dve, g_, g_, -1.0, None, ALU.mult)
        p5 = bank(5)
        for d in range(2):
            mm(p5[:, 32 * d:32 * d + 32], tri[:, d, :], g_[:, 32 * d:32 * d + 32], True, True, after=[gg, t_dn])
        tok = mm(p5[:, 64:128], onesq, g_, True, True, sig=True)
        a = af(G, p5[:, 0:64], ACT.Copy, after=[tok])
        a = af(bg, G, ACT.Exp)
        b = af(eGL, p5[:, 64:128], ACT.Exp)
        c = tt(dve, kdf, p5[:, 64:128], G, ALU.subtract, after=[b])
        tt(dve, bg, bg, beta, ALU.mult)
        b = af(kdf, kdf, ACT.Exp, after=[c])
        dn_free5 = [b]
        t_gates = [b, dve.last()]

        c_dz = [slot("c_dz0"), slot("c_dz1")]
        Z2 = TM[:, 1, :].rearrange("p (t c) -> p t c", c=512)

        def dz_consume(t, ps, tok):
            z = Z2[:, t, :]
            a = af(z, ps, ACT.Copy, after=[tok, *tm_free[1]])
            e = TM[:, 0, 0:512]
            b = af(e, z, ACT.Exp, scale=-1.0, after=tm_free[0])
            ts(dve, e, e, 1.0, None, ALU.add, after=[b])
            recip(e, e)
            c = tt(dve, z, z, e, ALU.mult)
            tm_free[0] = [c]
            return [a]

        token_groups(dz_consume, lambda t: [])
        w = dma(sp, c_dz[0], dz_d.rearrange("(t p) c -> p t c", p=128), Z2, after=[dve.last()])
        tm_free[1] = [w]
        dz_written = w

        def raw_buf():
            return TM[:, 0, 0:3 * 1028].rearrange("p (g t) -> p g t", t=1028)

        out_free = {1: tm_free[1], 2: tm_free[2]}

        def dn_consume(h):
            R = raw_buf()

            def f(c, th, ps, tok):
                a = []
                if c == 0 and th == 0:
                    mset(pool, R[:, :, 0:2], 0.0, after=tm_free[0])
                    a = [mset(pool, R[:, :, 1026:1028], 0.0)]
                    dn_st["pad"] = a
                return [af(R[:, c, 2 + th * 512:2 + (th + 1) * 512], ps, ACT.Copy, after=[tok, *tm_free[0]])]
            return f

        dn_st = {"pb": {0: [], 1: [], 2: []}, "free5": dn_free5, "free7": []}

        def dn_prepare(h, ob, ev):
            R = raw_buf()
            C = TM[:, ob, 0:3072].rearrange("p (g t) -> p g t", t=1024)
            while h >= 2 and not done.get(("dn", h - 2)):
                yield
            for c in range(3):
                w = cw[:, c * 4 + h, :]
                ts(dve, C[:, c, :], R[:, c, 0:1024], w[:, 0:1], None, ALU.mult,
                   after=[*ev, *dn_st["pad"], t_dn, *out_free[ob]])
                for j in range(1, 5):
                    a = stt(C[:, c, :], R[:, c, j:j + 1024], w[:, j:j + 1], C[:, c, :], ALU.mult, ALU.add)
                    yield
            E = TM[:, 0, 0:3072].rearrange("p (g t) -> p g t", t=1024)
            for c in range(3):
                s = silu_in_place(C[:, c, :], E[:, c, :], after=[a])
                yield
            qt = TM[:, 0, 0:1024].rearrange("p (t c) -> p t c", c=128)
            kt0 = TM[:, 0, 1024:2048].rearrange("p (t c) -> p t c", c=128)
            kt = TM[:, ob, 2048:3072].rearrange("p (t c) -> p t c", c=128)
            vt = TM[:, ob, 3072:4096].rearrange("p (t c) -> p t c", c=128)
            bk = 2
            free = dn_st["pb"][2]
            for c, dst in ((0, qt), (1, kt0), (2, vt)):
                for f in transposed(dst.rearrange("p t c -> p (t c)"), lambda t, c=c: C[:, c, t * 128:(t + 1) * 128],
                                    None, [s], bk, free):
                    free = f
                    yield
            e = TM[:, 0, 2048:3072].rearrange("p (t c) -> p t c", c=128)
            for n, src in ((0, qt), (1, kt0)):
                tt(dve, e, src, src, ALU.mult, after=free)
                a = red(ss[:, 32 + n * 8:40 + n * 8], e, ALU.add)
                yield
            r = rsqrt((32, 48), 1.0, after=[a])
            a = ts(dve, rs[:, 32:40], rs[:, 32:40], 128.0 ** -0.5, None, ALU.mult, after=[r])
            yield
            a = tt(dve, qt, qt, rs[:, 32:40].unsqueeze(2).to_broadcast([128, 8, 128]), ALU.mult)
            a = tt(dve, kt, kt0, rs[:, 40:48].unsqueeze(2).to_broadcast([128, 8, 128]), ALU.mult, after=[pe.last()])
            yield
            for c, src in ((0, qt), (1, kt)):
                for f in transposed(C[:, c, :], lambda t, src=src: src[:, t, :], None, [a], bk, free):
                    free = f
                    yield
            dn_st["pb"][2] = free
            dn_st[("in", h)] = [free[0], a]
            tm_free[0] = [pe.last(), a, free[0]]
            done[("prep", h)] = True

        def half_inverse(h, ob, j, ss_):
            while not done.get(("prep", h)) or (j >= 2 and not done.get(("rec", h, j - 2))) or (
                    j < 2 and h and not done.get(("rec", h - 1, j + 2))):
                yield
            AT, X, XT, Y, aT, E, TB = sets[ss_]
            b0, b1 = (3, 4) if ss_ == 0 else (5, 6)
            A, Bk = bank(b0), bank(b1)
            u4 = lambda a: a.rearrange("p (u c) -> p u c", c=128)
            d4 = lambda a: a.rearrange("p (d s c) -> p d s c", d=2, s=2)
            chunks = [2 * j, 2 * j + 1, 6 - 2 * j, 7 - 2 * j]
            cols = [d * 32 + h * 8 + c for d, c in zip((0, 0, 1, 1), chunks)]
            kT_ = TM[:, ob, 1024:2048]
            qT_ = TM[:, ob, 0:1024]
            kt = TM[:, ob, 2048:3072]
            vt = TM[:, ob, 3072:4096]
            cs = lambda a, c: a[:, c * 128:(c + 1) * 128]
            src = dn_st[("in", h)]
            fr = [*dn_st.get(("set", ss_), dn_free5), *t_gates]
            for u in range(4):
                a = ts(pool, u4(TB)[:, u, :], tri[:, u // 2, :], g_[:, cols[u]:cols[u] + 1], None, ALU.mult, after=fr)
                b = ts(pool, u4(Y)[:, u, :], ident, beta[:, cols[u]:cols[u] + 1], None, ALU.mult)
            yield
            gr = mm(A, onesq, TB, True, True, after=[b, *fr], sig=True)
            br = mm(Bk, onesq, Y, True, True, sig=True)
            yield
            for u in range(4):
                a = ts(dve, u4(E)[:, u, :], u4(A)[:, u, :], G[:, cols[u]:cols[u] + 1], 0.0, ALU.subtract, ALU.min,
                       after=[gr, *fr])
            e = af(E, E, ACT.Exp, after=[a])
            qe = af(TB, A, ACT.Exp)
            tri4 = tri.unsqueeze(2).to_broadcast([128, 2, 2, 128])
            yield
            e = tt(dve, d4(E), d4(E), tri4, ALU.mult, after=[e])
            beta_row = af(X, Bk, ACT.Copy, after=[br])
            yield
            for u in range(4):
                kk = mm(u4(A)[:, u, :], cs(kT_, chunks[u]), cs(kT_, chunks[u]), True, True, after=[qe, e, *src],
                        sig=(u == 3))
            for u in range(4):
                kq = mm(u4(Bk)[:, u, :], cs(kT_, chunks[u]), cs(qT_, chunks[u]), True, True, after=[beta_row],
                        sig=(u == 3))
            yield
            a = tt(dve, aT, Bk, E, ALU.mult, after=[kq])
            tt(dve, AT, A, E, ALU.mult, after=[kk])
            stt(AT, AT, -1.0, X, ALU.mult, ALU.mult, after=[beta_row])
            yield
            mk = lambda l: MK[:, l].unsqueeze(2).to_broadcast([128, 2, 2, 128])
            tt(dve, d4(XT), d4(AT), MK[:, 6].unsqueeze(2).to_broadcast([128, 2, 2, 128]), ALU.mult, after=[mkt])
            a = tt(dve, u4(XT), u4(XT), ident.unsqueeze(1).to_broadcast([128, 4, 128]), ALU.add)
            yield
            for u in range(4):
                t_ = tr(u4(A)[:, u, :], u4(XT)[:, u, :], after=[a], sig=(u == 3))
            a = xe = af(X, A, ACT.Copy, after=[t_])
            yield
            for l in range(6):
                for u in range(4):
                    y = mm(u4(A)[:, u, :], u4(AT)[:, u, :], u4(X)[:, u, :], True, True, after=[a, xe, dve.last()] if u == 0 else (), sig=(u == 3))
                yield
                ym = tt(dve, d4(Y), d4(A), mk(l), ALU.mult, after=[y])
                yield
                for u in range(4):
                    zt = mm(u4(Bk)[:, u, :], u4(Y)[:, u, :], u4(XT)[:, u, :], True, True, after=[ym], sig=(u == 3))
                if l < 5:
                    for u in range(4):
                        z = mm(u4(A)[:, u, :], u4(XT)[:, u, :], u4(Y)[:, u, :], True, True, sig=(u == 3))
                else:
                    z = zt
                yield
                a = tt(dve, XT, XT, Bk, ALU.add, after=[z])
                if l < 5:
                    a = tt(dve, X, X, A, ALU.add, after=[z])
                yield
            for u in range(4):
                vb = ts(pool, u4(Y)[:, u, :], cs(vt, chunks[u]), beta[:, cols[u]:cols[u] + 1], None, ALU.mult, after=[z, *src])
                kb = ts(pool, u4(E)[:, u, :], cs(kt, chunks[u]), bg[:, cols[u]:cols[u] + 1], None, ALU.mult, after=[a])
            for d in range(2):
                c0 = chunks[2 * d]
                qg = tt(dve, AT[:, d * 256:(d + 1) * 256], TB[:, d * 256:(d + 1) * 256],
                        qT_[:, c0 * 128:(c0 + 2) * 128], ALU.mult, after=[z])
            yield
            for u in range(4):
                uu = mm(u4(A)[:, u, :], u4(XT)[:, u, :], u4(Y)[:, u, :], True, True, after=[kb, a], sig=(u == 3))
            for u in range(4):
                ww = mm(u4(Bk)[:, u, :], u4(E)[:, u, :], u4(XT)[:, u, :], True, True, sig=(u == 3))
            yield
            ue = af(X, A, ACT.Copy, after=[uu])
            we = af(Y, Bk, ACT.Copy, after=[ww], scale=-1.0)
            for u in range(4):
                kd = ts(pool, u4(XT)[:, u, :], cs(kt, chunks[u]), kdf[:, cols[u]:cols[u] + 1], None, ALU.mult, after=[ww])
            yield
            dn_st[("out", h, j)] = [ue, we, kd, qg]
            done[("pre", h, j)] = True

        def recursion(h, ob):
            D3 = bank(7)
            ws = D3[:, 0:256].rearrange("p (d c) -> p d c", d=2)
            oo = D3[:, 256:512].rearrange("p (d c) -> p d c", d=2)
            while h and not done.get(("dn", h - 1)):
                yield
            mset(dve, St, 0.0, after=dn_mark)
            s_tok = [dve.last()]
            for j in range(4):
                while not done.get(("pre", h, j)):
                    yield
                AT, X, XT, Y, aT, E, TB = sets[j % 2]
                u4 = lambda a: a.rearrange("p (u c) -> p u c", c=128)
                pre = dn_st[("out", h, j)]
                for s in range(2):
                    us = (s, 3 - s)
                    chs = (2 * j + s, 7 - 2 * j - s)
                    for d in range(2):
                        w = mm(ws[:, d, :], u4(Y)[:, us[d], :], St[:, d, :], True, True,
                               after=[*pre, *s_tok, *dn_st["free7"]], sig=(d == 1))
                    yield
                    v = tt(dve, Vn, ws, u4(X)[:, s:4 - s:3 - 2 * s, :], ALU.add, after=[w])
                    yield
                    for d in range(2):
                        mm(oo[:, d, :], u4(AT)[:, us[d], :], St[:, d, :], True, False, after=[v])
                        mm(oo[:, d, :], u4(aT)[:, us[d], :], Vn[:, d, :], False, True)
                    for d in range(2):
                        w = mm(ws[:, d, :], u4(XT)[:, us[d], :], Vn[:, d, :], True, True, sig=(d == 1))
                    yield
                    for d in range(2):
                        cl = d * 32 + h * 8 + chs[d]
                        a = stt(St[:, d, :], St[:, d, :], eGL[:, cl:cl + 1], ws[:, d, :], ALU.mult, ALU.add, after=[w])
                    s_tok = [a]
                    for d in range(2):
                        o = OA[:, chs[d], :]
                        if j < 2:
                            a = dve.put(lambda e, o=o, d=d: e.tensor_copy(o, oo[:, d, :]), dn_st.get("oa_free", dn_mark))
                        else:
                            a = tt(dve, o, o, oo[:, d, :], ALU.add)
                    dn_st["free7"] = [a]
                    yield
                dn_st[("set", j % 2)] = [pe.last(), a]
                done[("rec", h, j)] = True
            out_free[ob] = [pe.last(), a]
            done[("dn", h)] = True
            zt = TM[:, ob, 0:1024].rearrange("p (t c) -> p t c", c=128)
            e = TM[:, ob, 1024:2048].rearrange("p (t c) -> p t c", c=128)
            lz = dma(sp, c_dz[1], zt, dz_d.rearrange("(t p) c -> p t c", p=128)[:, :, h * 128:(h + 1) * 128],
                     after=[dz_written, pool.last(), *out_free[ob]])
            tt(dve, e, OA, OA, ALU.mult, after=[pe.last(), pool.last()])
            a = red(ss[:, 48:56], e, ALU.add)
            r = rsqrt((48, 56), 128, after=[a])
            out_free[ob] = [dve.last()]
            yield
            tt(dve, OA, OA, rs[:, 48:56].unsqueeze(2).to_broadcast([128, 8, 128]), ALU.mult, after=[r])
            tt(dve, OA, OA, dnw.unsqueeze(1).to_broadcast([128, 8, 128]), ALU.mult)
            a = tt(dve, OA, OA, zt, ALU.mult, after=[lz])
            out_free[ob] = [a]
            w = dma(sp, c_mix[2], mix_d.rearrange("(t p) c -> p t c", p=128)[:, :, 512 + h * 128:512 + (h + 1) * 128],
                    OA, after=[a])
            dn_st["oa_free"] = [w]
            done[("dnall", h)] = True
            yield

        def dn_head(h):
            ob = 1 + h % 2
            for j in range(0, 4):
                yield from half_inverse(h, ob, j, j % 2)

        def lane(s):
            for h in range(4):
                for j in (s, s + 2):
                    yield from half_inverse(h, 1 + h % 2, j, s)

        def rec_lane():
            for h in range(4):
                while h and not done.get(("dnall", h - 1)):
                    yield
                yield from recursion(h, 1 + h % 2)

        spawn(lane(0))
        spawn(lane(1))
        spawn(rec_lane())
        for h in range(4):
            while h and not done.get(("prep", h - 1)):
                pump()
            channel_groups(dn_consume(h), [])
            ev = [act.last()]
            spawn(dn_prepare(h, 1 + h % 2, ev))
        drain()

        area = Area(base)
        mark = fence()
        ring = [area.take(1024) for _ in range(2)]
        h2 = [area.take(1024) for _ in range(2)]
        tmp = area.take(512)
        junk = area.take(1024)
        c_ring = [slot("c_ring0"), slot("c_ring1")]
        c_x1 = slot("c_x1out")
        ring_free = [list(mark), list(mark)]
        nring = [0]

        def feed(src):
            i = nring[0] % 2
            nring[0] += 1
            tok = dma(sp, c_ring[i], ring[i], src, after=ring_free[i])
            return ring[i], tok, i

        for t in range(8):
            dma(sp, c_x[t], xt(t), x[t * 128:(t + 1) * 128, :], after=mark)
        for t in range(8):
            buf, tok, i = feed(mix_d[t * 128:(t + 1) * 128, :])
            ht[t] = to_stationary(t, buf, [tok, *mark])
            ring_free[i] = [pe.last()]
        last_w = {}

        def wo_consume(cb):
            def f(t, ps, tok):
                o = xt(t)[:, cb * 512:(cb + 1) * 512]
                a = tt(dve, o, ps, o, ALU.add, after=[tok, c_x[t].token()])
                if cb:
                    dma(sp, c_x1, x1_d[t * 128:(t + 1) * 128, :], xt(t), after=[a])
                    s = af(junk, xt(t), ACT.Square, after=[a, *mark], accum_out=ss[:, t:t + 1])
                    r = rsqrt((t, t + 1), 1024, after=[s])
                    b = ts(dve, h2[t % 2], xt(t), rs[:, t:t + 1], None, ALU.mult, after=[r, *last_w.get(t % 2, mark)])
                    late.append((t, b, tok))
                return [a]
            return f

        late = []
        token_groups(wo_consume(0), lambda t: [ht[t]])

        def wo_tile_hook(t):
            while late:
                t0, b, tok = late.pop(0)
                pend.append((t0, b))
            if len(pend) > 0:
                t0, b = pend.pop(0)
                ht[t0] = to_stationary(t0, h2[t0 % 2], [b, *mark], nw2, tmp)
                last_w[t0 % 2] = [pe.last()]
            return []

        pend = []
        token_groups(wo_consume(1), wo_tile_hook)
        wo_tile_hook(8)

        area = Area(base)
        mark = fence()
        qT = area.take(1024)
        kT = area.take(1024)
        L = area.take(1024)
        Pm = area.take(1025)
        Sx = area.take(1024)
        WT = area.take(1024)
        sqt = area.take(256)
        sm = area.take(128)
        sm2 = area.take(1)
        c_sb = slot("c_sb")
        c_oa = [slot(f"c_oa{i}") for i in range(3)]
        mset(dve, sqt, 0.0, after=mark)
        mset(pool, sm2, 0.0, after=mark)
        act.put(lambda e: e.activation(L[:, 0:1], sqt[:, 0:1], ACT.Copy), [*mark, dve.last()])
        dma(sp, c_sb, sm, masks[17], after=mark)
        w_start = [dve.last(), act.last(), pool.last(), c_sb.token()]
        tm_free = [list(mark) for _ in range(3)]
        state = {"rs_free": [], "b4": [], "z": [], "b5": [], "qk": []}

        def norm_consume(buf, dh, ng, cols):
            B = TM[:, buf, :].rearrange("p (t c) -> p t c", c=512)

            def f(t, ps, tok):
                a = af(B[:, t, :], ps, ACT.Copy, after=[tok, *tm_free[buf]])
                q = B[:, t, 0:256]
                tt(dve, sqt, q, q, ALU.mult, after=[a, *w_start, *state["rs_free"]])
                red(ss[:, cols + t * ng:cols + t * ng + ng], sqt.rearrange("p (g d) -> p g d", d=dh), ALU.add)
                return [a]
            return f

        def sb_side(h, buf, ev):
            B = TM[:, buf, :].rearrange("p (t c) -> p t c", c=512)
            qk = B[:, :, 0:256].rearrange("p t (g d) -> p t g d", d=128)
            r = rsqrt((0, 16), 128, after=[ev])
            yield
            sc = rs[:, 0:16].rearrange("p (t g) -> p t g", g=2)
            for t in range(8):
                a = tt(dve, qk[:, t], qk[:, t], sc[:, t].unsqueeze(2).to_broadcast([128, 2, 128]), ALU.mult, after=[r])
            yield
            while h and not done.get(("sb", h - 1)):
                yield
            free = state["b4"]
            for dst, o, g in ((qT, 0, sq_), (kT, 128, sk_)):
                for f in transposed(dst, lambda t, o=o: B[:, t, o:o + 128], g, [a, *w_start, *state["qk"]], 4, free):
                    free = f
                    yield
            state["b4"] = free
            qk_tok = free[0]
            sz = silu_in_place(B[:, :, 384:512], B[:, :, 0:128], after=[pe.last()])
            yield
            for i in range(8):
                nk = (i + 1) * 128
                zp = PS[:, 1024:1024 + nk]
                for c in range(0, nk, 512):
                    w = min(512, nk - c)
                    tok = mm(PS[:, 1024 + c:1024 + c + w], qT[:, i * 128:(i + 1) * 128], kT[:, c:c + w], True, True,
                             after=[qk_tok, *state["z"]], sig=True)
                yield
                l = L[:, 0:nk]
                a = af(l, zp, ACT.Abs, after=[tok, *state.get("L", [])])
                a = af(l, l, ACT.Exp, scale=-1.0)
                a = af(l, l, ACT.Ln, bias=1.0)
                yield
                pm = Pm[:, 0:nk]
                stt(pm, zp, 0.0, l, ALU.max, ALU.add, after=[a])
                b = tt(dve, l, zp, pm, ALU.subtract, after=[a])
                state["z"] = [b]
                tt(dve, Pm[:, nk - 128:nk], Pm[:, nk - 128:nk], sm, ALU.mult)
                mset(dve, Pm[:, nk:nk + 1], 0.0)
                dve.put(lambda e, nk=nk: e.tensor_tensor_scan(
                    Sx[:, 0:nk][:, ::-1], one.to_broadcast([128, nk]), Pm[:, 1:nk + 1][:, ::-1], 0.0, ALU.mult, ALU.add))
                b = tt(dve, l, l, Sx[:, 0:nk], ALU.subtract)
                yield
                a = af(l, l, ACT.Exp, after=[b])
                a = tt(dve, L[:, nk - 128:nk], L[:, nk - 128:nk], sm, ALU.mult, after=[a])
                yield
                free = state["b4"]
                for g in range(0, i + 1, 4):
                    n = min(4, i + 1 - g)
                    for jj in range(n):
                        tok = tr(bank(4)[:, jj * 128:(jj + 1) * 128], L[:, (g + jj) * 128:(g + jj + 1) * 128],
                                 after=[a, *free], sig=(jj == n - 1))
                    free = [af(WT[:, g * 128:(g + n) * 128], bank(4, n * 128), ACT.Copy, after=[tok, *state.get("WT", [])])]
                    yield
                state["b4"] = free
                state["L"] = [tok]
                O = bank(5, 128)
                for jj in range(i + 1):
                    tok = mm(O, WT[:, jj * 128:(jj + 1) * 128], B[:, jj, 256:384], jj == 0, jj == i,
                             after=[free[0], *state["b5"]], sig=(jj == i))
                state["WT"] = [tok]
                yield
                o = tt(dve, B[:, i, 128:256], O, B[:, i, 384:512], ALU.mult, after=[tok, sz])
                state["b5"] = [o]
                yield
            state["qk"] = [pe.last()]
            w = dma(sp, c_oa[buf], oa_d.rearrange("(t p) c -> p t c", p=128)[:, :, h * 128:(h + 1) * 128],
                    B[:, :, 128:256], after=[o])
            tm_free[buf] = [w, pe.last(), o]
            done[("sb", h)] = True

        for h in range(8):
            buf = h % 3
            if h >= 3:
                while not done.get(("sb", h - 3)):
                    pump()
            if h:
                state["rs_free"] = [state["used"]]
            token_groups(norm_consume(buf, 128, 2, 0), lambda t: [ht[t]])
            g = sb_side(h, buf, dve.last())
            next(g)
            next(g)
            state["used"] = dve.last()
            spawn(g)
        drain()

        area = Area(base)
        mark = fence()
        CS = area.take(2048).rearrange("p (s t c) -> p s t c", s=2, c=128)
        RQ = area.take(2048).rearrange("p (d t) -> p d t", d=2)
        RK = area.take(2048).rearrange("p (d t) -> p d t", d=2)
        tq = [area.take(256).rearrange("p (g c) -> p g c", g=2) for _ in range(4)]
        Sr = [area.take(512).rearrange("p (d e) -> p d e", d=2) for _ in range(2)]
        aTr = area.take(128)
        rm = area.take(512).rearrange("p (h c) -> p h c", h=4)
        rc = area.take(8)
        grow = area.take(256)
        brow = area.take(512)
        c_rt = slot("c_rt")
        c_gr = slot("c_gr")
        c_ob = slot("c_ob")
        mset(dve, aTr, 0.0, after=mark)
        mset(pool, tq[2], 0.0, after=mark)
        act.put(lambda e: e.activation(Sr[0][:, 0, 0:1], aTr[:, 0:1], ACT.Copy), [*mark, dve.last()])
        dma(sp, c_rt, CS, cossin.rearrange("s (t p) c -> p s t c", p=128), after=mark)
        dma(sp, c_rt, rm, retmask.rearrange("h p c -> p h c"), after=mark)
        dma(sp, c_rt, rc, retcol, after=mark)
        w_start = [dve.last(), act.last(), pool.last(), c_rt.token()]
        tm_free = [list(mark) for _ in range(3)]
        state = {"b4": [], "b5": [], "b6": [], "qk": []}
        gam = [1.0 - 2.0 ** (-5.0 - h) for h in range(4)]

        def plain_consume(buf):
            B = TM[:, buf, :].rearrange("p (t c) -> p t c", c=512)

            def f(t, ps, tok):
                return [af(B[:, t, :], ps, ACT.Copy, after=[tok, *tm_free[buf]])]
            return f

        def ret_side(h, bx, by, ev):
            BX = TM[:, bx, :].rearrange("p (t c) -> p t c", c=512)
            BY = TM[:, by, :].rearrange("p (t c) -> p t c", c=512)
            gr = dma(sp, c_gr, grow, ret_gain[h:h + 1, :].to_broadcast([128, 256]), after=[*w_start, *state.get("grow", [])])
            for t in range(8):
                v = BX[:, t, :].rearrange("p (g s c) -> p g s c", g=2, s=2)
                t1, t2 = v[:, :, 0, :], v[:, :, 1, :]
                c = CS[:, 0, t, :].unsqueeze(1).to_broadcast([128, 2, 128])
                s = CS[:, 1, t, :].unsqueeze(1).to_broadcast([128, 2, 128])
                tt(dve, tq[0], t1, c, ALU.mult, after=[*ev, *w_start])
                a = tt(dve, tq[1], t2, s, ALU.mult)
                b = tt(pool, tq[2], t1, s, ALU.mult, after=[*ev, *w_start])
                b = tt(pool, tq[3], t2, c, ALU.mult)
                tt(dve, t1, tq[0], tq[1], ALU.subtract, after=[b])
                b = tt(pool, t2, tq[2], tq[3], ALU.add, after=[a])
                yield
            rope = [b, dve.last()]
            while h and not done.get(("ret", h - 1)):
                yield
            free = state["b4"]
            for dst, o in ((RQ, 0), (RK, 256)):
                for dh in range(2):
                    for f in transposed(dst[:, dh, :], lambda t, o=o, dh=dh: BX[:, t, o + dh * 128:o + dh * 128 + 128],
                                        None, [*rope, *w_start, *state["qk"]], 4, free):
                        free = f
                        yield
            state["b4"] = free
            tr_done = [pe.last(), free[0]]
            kd = ts(dve, BX[:, :, 256:512], BX[:, :, 256:512], rc[:, 4 + h:5 + h], None, ALU.mult, after=tr_done)
            sz = silu_in_place(BY[:, :, 256:512], BX[:, :, 0:256], after=tr_done)
            yield
            s_tok = [mset(dve, Sr[0], 0.0, after=w_start)]
            for c in range(8):
                cc = slice(c * 128, (c + 1) * 128)
                S0, S1 = Sr[c % 2], Sr[(c + 1) % 2]
                b5, b6 = bank(5, 128), bank(5, 256, 256)
                for dh in range(2):
                    tok = mm(b5, RK[:, dh, cc], RQ[:, dh, cc], dh == 0, dh == 1, after=[*tr_done, *state["b5"]],
                             sig=(dh == 1))
                yield
                a = tt(dve, aTr, b5, rm[:, h, :], ALU.mult, after=[tok, *state.get("a", [])])
                yield
                o = bank(6, 256)
                for dh in range(2):
                    mm(o, RQ[:, dh, cc], S0[:, dh, :], dh == 0, False, after=[*s_tok, *state["b6"]])
                tok = mm(o, aTr, BY[:, c, 0:256], False, True, after=[a], sig=True)
                state["a"] = [tok]
                state["b5"] = [a]
                if c < 7:
                    for dh in range(2):
                        u = mm(bank(7)[:, dh * 256:(dh + 1) * 256], BX[:, c, 256 + dh * 128:256 + (dh + 1) * 128],
                               BY[:, c, 0:256], True, True, after=[kd, *s_tok], sig=(dh == 1))
                yield
                oe = ts(dve, BX[:, c, 0:256], o, rc[:, h:h + 1], None, ALU.mult, after=[tok])
                state["b6"] = [oe]
                if c < 7:
                    a = stt(S1, S0, gam[h] ** 128, bank(7).rearrange("p (d e) -> p d e", d=2), ALU.mult, ALU.add, after=[u])
                    s_tok = [a]
                yield
            state["qk"] = [pe.last()]
            pe_done = pe.last()
            O = BX[:, :, 0:256]
            e = BX[:, :, 256:512]
            tt(dve, e, O, O, ALU.mult, after=[pe_done])
            a = red(ss[:, 0:8], e, ALU.add)
            r = rsqrt((0, 8), 256, after=[a])
            yield
            tt(dve, O, O, rs[:, 0:8].unsqueeze(2).to_broadcast([128, 8, 256]), ALU.mult, after=[r])
            a = tt(dve, O, O, grow.unsqueeze(1).to_broadcast([128, 8, 256]), ALU.mult, after=[gr])
            state["grow"] = [a]
            a = tt(dve, O, O, BY[:, :, 256:512], ALU.mult)
            w = dma(sp, c_ob, ob_d.rearrange("(t p) c -> p t c", p=128)[:, :, h * 256:(h + 1) * 256], O, after=[a])
            tm_free[bx] = [w, pe_done, a]
            tm_free[by] = [pe_done, a]
            done[("ret", h)] = True

        nb = 0
        for h in range(4):
            bx, by = nb % 3, (nb + 1) % 3
            nb += 2
            while h and not done.get(("ret", h - 1)):
                pump()
            token_groups(plain_consume(bx), lambda t: [])
            token_groups(plain_consume(by), lambda t: [])
            spawn(ret_side(h, bx, by, [act.last()]))
        c_br = slot("c_br")
        c_sg = [slot("c_sg0"), slot("c_sg1")]
        sgf = [[], []]
        fb = nb % 3
        sbufs = [TM[:, fb, i * 512:(i + 1) * 512] for i in range(2)]
        n_s = [0]
        br_free = [[]]

        def m_consume(g, cb, br):
            def f(t, ps, tok):
                i = n_s[0] % 2
                n_s[0] += 1
                s = sbufs[i]
                a = tt(dve, s, ps, brow, ALU.add, after=[tok, br, *tm_free[fb], *sgf[i]])
                br_free[0] = [a]
                b = af(s, s, ACT.Exp, after=[a], scale=-1.0)
                ts(dve, s, s, 1.0, None, ALU.add, after=[b])
                r = recip(s, s)
                w = dma(sp, c_sg[i], sig_d[g, t * 128:(t + 1) * 128, cb * 512:(cb + 1) * 512], s, after=[r])
                sgf[i] = [w]
                return [a]
            return f

        for g in range(2):
            for cb in range(2):
                br = dma(sp, c_br, brow, b_merge[g:g + 1, cb * 512:(cb + 1) * 512].to_broadcast([128, 512]),
                         after=[*w_start, *br_free[0]])
                token_groups(m_consume(g, cb, br), lambda t: [])
        drain()

        area = Area(base)
        mark = fence()
        ring = [area.take(1024) for _ in range(2)]
        sgt = [area.take(512) for _ in range(4)]
        ot = [area.take(512) for _ in range(4)]
        c_st = [slot(f"c_st{i}") for i in range(4)]
        c_ot = [slot(f"c_ot{i}") for i in range(4)]
        ring_free = [list(mark), list(mark)]
        nring[0] = 0
        c_ring[0], c_ring[1] = slot("c_ring2"), slot("c_ring3")
        sg_free = [list(mark) for _ in range(4)]
        ot_free = [list(mark) for _ in range(4)]
        n_g = [0]

        def merged(t):
            return TM[:, t // 4, (t % 4) * 1024:(t % 4 + 1) * 1024]

        def feed_small(src):
            i = n_g[0] % 4
            n_g[0] += 1
            tok = dma(sp, c_st[i], sgt[i], src, after=sg_free[i])
            return sgt[i], tok, i

        def restage(get):
            def hook(t):
                if t:
                    get(t - 1)
                return []
            return hook

        def stage(src_d):
            def get(t):
                buf, tok, i = feed(src_d[t * 128:(t + 1) * 128, :])
                ht[t] = to_stationary(t, buf, [tok, *mark])
                ring_free[i] = [pe.last()]
            return get

        def branch_consume(g, cb):
            def f(t, ps, tok):
                s, st, i = feed_small(sig_d[g, t * 128:(t + 1) * 128, cb * 512:(cb + 1) * 512])
                m = merged(t)[:, cb * 512:(cb + 1) * 512]
                if g == 0:
                    a = b = tt(dve, m, ps, s, ALU.mult, after=[tok, st, *mark])
                else:
                    a = tt(dve, s, ps, s, ALU.mult, after=[tok, st])
                    b = tt(dve, m, m, s, ALU.add)
                sg_free[i] = [b]
                mdone[t] = b
                return [a]
            return f

        mdone = {}
        ga, gb = stage(oa_d), stage(ob_d)
        for t in range(8):
            ga(t)
        tile_ready = lambda t: [ht[t]]
        token_groups(branch_consume(0, 0), tile_ready)
        token_groups(branch_consume(0, 1), restage(gb))
        gb(7)
        token_groups(branch_consume(1, 0), tile_ready)

        def gm(t):
            ht[t] = to_stationary(t, merged(t), [mdone[t]])

        token_groups(branch_consume(1, 1), restage(gm))
        gm(7)

        def final_consume(cb):
            def f(t, ps, tok):
                s, st, i = feed_small(x1_d[t * 128:(t + 1) * 128, cb * 512:(cb + 1) * 512])
                o = ot[n_o[0] % 4]
                j = n_o[0] % 4
                n_o[0] += 1
                a = tt(dve, o, ps, s, ALU.add, after=[tok, st, *ot_free[j]])
                sg_free[i] = [a]
                w = dma(sp, c_ot[j], out[t * 128:(t + 1) * 128, cb * 512:(cb + 1) * 512], o, after=[a])
                ot_free[j] = [w]
                return [a]
            return f

        n_o = [0]
        token_groups(final_consume(0), tile_ready)
        token_groups(final_consume(1), tile_ready)

        ends = [s.token() for s in slots]

        block = ctx.enter_context(nc.Block())

        @block.sync
        def _(eng):
            sp.play(eng)
            for sem, v in ends:
                eng.wait_ge(sem, v)

        @block.tensor
        def _(eng):
            pe.play(eng)

        @block.scalar
        def _(eng):
            eng.preload_act_table_set("natural_log_exp_and_others")
            act.play(eng)

        @block.vector
        def _(eng):
            dve.play(eng)

        @block.gpsimd
        def _(eng):
            pool.play(eng)


def constants():
    i = np.arange(128)
    eye = np.eye(128, dtype=np.float32)
    planes = [eye]
    for b in (2, 4, 8, 16, 32, 64):
        pair = (i[:, None] // (2 * b)) == (i[None, :] // (2 * b))
        low = pair & (i[:, None] // b % 2 == 1) & (i[None, :] // b % 2 == 0)
        planes += [low.astype(np.float32), low.T.astype(np.float32)]
    pair = (i[:, None] // 2) == (i[None, :] // 2)
    low = pair & (i[:, None] % 2 == 1) & (i[None, :] % 2 == 0)
    planes += [low.T.astype(np.float32), low.astype(np.float32)]
    planes += [(i[:, None] <= i[None, :]).astype(np.float32), (i[:, None] >= i[None, :]).astype(np.float32)]
    planes += [(i[:, None] > i[None, :]).astype(np.float32)]
    masks = np.stack(planes)
    inv = (10000.0 ** (-np.arange(0, 256, 2, dtype=np.float32) / np.float32(256))).astype(np.float32)
    ang = np.arange(1024, dtype=np.float32)[:, None] * inv[None, :]
    cs = np.stack([np.cos(ang), np.sin(ang)]).astype(np.float32)
    rm = np.zeros((4, 128, 128), np.float32)
    rc = np.zeros((128, 8), np.float32)
    for h in range(4):
        lg = np.log1p(-np.exp2(-5.0 - h))
        s, t = i[:, None], i[None, :]
        rm[h] = np.where(s // 64 <= t // 64, np.exp(lg * (np.abs(t - s) - (t + 1.0))), 0.0) / 16.0
        rc[:, h] = np.exp(lg * (i + 1.0))
        rc[:, 4 + h] = np.exp(lg * (127.0 - i)) / 16.0
    return masks, cs, rm, rc


def kernel(**inputs):
    import concourse.bacc as bacc
    from concourse.bass_utils import run_bass_kernel_spmd

    a = {k: np.asarray(v)[0] for k, v in inputs.items()}
    masks, cs, rm, rc = constants()
    pad = np.pad(a["rpb"], ((0, 0), (0, 0), (48, 48)))
    tabs = np.stack([pad[:, :, 63 - w:127 - w] for w in range(64)], axis=2)
    arrays = {
        "x": a["x"],
        "norm_w": a["norm_w"].reshape(8, 128).T,
        "w_in": a["w_in"],
        "gq": a["qk_gain_q"][:, None],
        "gk": a["qk_gain_k"][:, None],
        "rpb": tabs,
        "conv_w": a["conv_w"].reshape(5, 12, 128).transpose(2, 1, 0),
        "a_log": a["a_log"].reshape(1, 8),
        "dt_bias": a["dt_bias"].reshape(1, 8),
        "dn_w": a["dn_norm_w"][None, :],
        "w_out": a["w_out"],
        "gain2": a["norm_gain_2"].reshape(8, 128).T,
        "w_in2": a["w_in_2"],
        "b_merge": a["b_merge_2"],
        "sbq": a["sb_q_gain_2"][:, None],
        "sbk": a["sb_k_gain_2"][:, None],
        "ret_gain": a["ret_out_gain_2"],
        "w_sb": a["w_branch_sb_2"],
        "w_ret": a["w_branch_ret_2"],
        "w_out2": a["w_out_2"],
        "masks": masks, "cossin": cs, "retmask": rm, "retcol": rc,
    }
    nc = bacc.Bacc("TRN2", target_bir_lowering=False, num_devices=1)
    given, args = {}, []
    for name, v in arrays.items():
        v = np.ascontiguousarray(v)
        given[f"in_{name}"] = v
        args.append(nc.dram_tensor(f"in_{name}", v.shape, mybir.dt.from_np(v.dtype), kind="ExternalInput").ap())
    args.append(nc.dram_tensor("out_0", [1024, 1024], F32, kind="ExternalOutput").ap())
    build(nc, *args)
    r = run_bass_kernel_spmd(nc, [given], core_ids=[0])
    return np.asarray(r.results[0]["out_0"]).reshape(1, 1024, 1024)
```

```python
import numpy as np
import concourse.bass as bass
from concourse import mybir
from concourse.alu_op_type import AluOpType as ALU
from contextlib import ExitStack

F32 = mybir.dt.float32
F32R = mybir.dt.float32r
ACT = mybir.ActivationFunctionType
AX = mybir.AxisListType

EPS = 1e-6
NEG = -1.0e30


class Queue:

    def __init__(self, sem, chained, clock, tail):
        self.sem, self.chained = sem, chained
        self.clock, self.tail = clock, tail
        self.n = 0
        self.t = 0.0
        self.seen = {}
        self.items = []

    def put(self, fn, after=(), sig=True, free=False, cost=100.0):
        waits = []
        start = max([self.t] + [self.clock.get((id(m), v), 0.0) for m, v in after])
        self.t = start + cost
        own = [(self.sem, self.n)] if self.chained and not free and self.n else []
        for sem, v in [*after, *own]:
            if self.seen.get(id(sem), 0) < v:
                self.seen[id(sem)] = v
                waits.append((sem, v))
        self.items.append((waits, fn, sig))
        if sig:
            self.n += 1
            self.clock[(id(self.sem), self.n)] = self.t + self.tail
        if self.chained:
            self.clock["side"] = max(self.clock.get("side", 0.0), self.t + self.tail)
        return (self.sem, self.n)

    def last(self):
        return (self.sem, self.n)

    def play(self, eng):
        for waits, fn, sig in self.items:
            best = {}
            for sem, v in waits:
                if id(sem) not in best or best[id(sem)][1] < v:
                    best[id(sem)] = (sem, v)
            for sem, v in best.values():
                eng.wait_ge(sem, v)
            ins = fn(eng)
            if sig is True:
                ins.then_inc(self.sem, 1)
            elif sig:
                ins.then_inc(sig, 16)


class Slot:

    def __init__(self, sem):
        self.sem, self.n = sem, 0

    def token(self):
        return (self.sem, self.n)


def build(nc, x, norm_w, w_in, gq, gk, rpb, conv_w, a_log, dt_bias, dn_w, w_out,
          gain2, w_in2, b_merge, sbq, sbk, ret_gain, w_sb, w_ret, w_out2,
          masks, cossin, retmask, retcol, out):
    ctx = ExitStack()
    with ctx:
        def sb(name, shape, dt=F32):
            return ctx.enter_context(nc.sbuf_tensor(name, shape, dt))

        def semaphore(name):
            return ctx.enter_context(nc.semaphore(name))

        def scratch(name, shape):
            return nc.dram_tensor(name, shape, F32, kind="Internal").ap()

        mix_d = scratch("mix_d", [1024, 1024])
        x1_d = scratch("x1_d", [1024, 1024])
        oa_d = scratch("oa_d", [1024, 1024])
        ob_d = scratch("ob_d", [1024, 1024])
        sig_d = scratch("sig_d", [2, 1024, 1024])
        dz_d = scratch("dz_d", [1024, 512])

        HH = sb("HH", [128, 8, 1024], F32R)
        HL = sb("HL", [128, 8, 1024], F32R)
        NSLOT = 12
        WH = sb("WH", [128, NSLOT, 1024], F32R)
        NRAW = 4
        RAW = sb("RAW", [128, NRAW, 512])
        TM = sb("TM", [128, 3, 4096])
        WKW = 10160
        WK = sb("WK", [128, WKW])
        PS = ctx.enter_context(nc.psum_tensor("PS", [128, 4096], F32))

        def bank(n, w=512, o=0):
            return PS[:, n * 512 + o:n * 512 + o + w]

        clock = {}
        pe = Queue(semaphore("s_pe"), False, clock, 200.0)
        act = Queue(semaphore("s_act"), True, clock, 100.0)
        dve = Queue(semaphore("s_dve"), True, clock, 100.0)
        pool = Queue(semaphore("s_pool"), True, clock, 100.0)
        sp = Queue(semaphore("s_sp"), False, clock, 0.0)

        def width(a):
            n = 1
            for d in a.shape[1:]:
                n *= d
            return n
        slots = []

        def slot(name):
            s = Slot(semaphore(name))
            slots.append(s)
            return s

        def mm(o, l, r, start, stop, after=(), sig=False):
            passes = 4 if l.dtype == F32 else 1
            return pe.put(lambda e: e.matmul(o, l, r, start=start, stop=stop), after, sig,
                          cost=passes * max(64, width(r)) / 2.4)

        def tr(o, i, after=(), sig=False):
            p = i.shape[0]
            b = i.base_partition() if callable(i.base_partition) else i.base_partition
            idn = ident[b:b + p, b:b + p] if p < 128 else ident
            return pe.put(lambda e: e.transpose(o, i, idn), after, sig, cost=60)

        def af(o, i, func, after=(), par=False, **kw):
            return act.put(lambda e: e.activation(o, i, func, **kw), after, free=par, cost=70 + 0.83 * width(o))

        def tt(q, o, a, b, op, after=()):
            c = 150 + 160 * width(o) if op == ALU.pow else 70 + (1.04 if q is dve else 2.4) * width(o)
            return q.put(lambda e: e.tensor_tensor(o, a, b, op), after, cost=c)

        def ts(q, o, a, s1, s2, op0, op1=None, after=(), par=False):
            c = 70 + (1.04 if q is dve else 5.0) * width(o)
            if op1 is None:
                return q.put(lambda e: e.tensor_scalar(o, a, s1, None, op0), after, free=par, cost=c)
            return q.put(lambda e: e.tensor_scalar(o, a, s1, s2, op0, op1), after, free=par, cost=c)

        def stt(o, a, s, b, op0, op1, after=()):
            return dve.put(lambda e: e.scalar_tensor_tensor(out=o, in0=a, scalar=s, in1=b, op0=op0, op1=op1), after,
                           cost=70 + 1.04 * width(o))

        def red(o, i, op, after=(), axis=AX.X):
            return dve.put(lambda e: e.tensor_reduce(o, i, axis, op), after, cost=70 + 1.04 * width(i))

        def recip(o, i, after=()):
            return dve.put(lambda e: e.reciprocal(o, i), after, cost=70 + 6.3 * width(o))

        def mset(q, o, v, after=()):
            return q.put(lambda e: e.memset(o, v), after)

        def dma(q, s, o, i, after=()):
            if q is sp:
                sp.put(lambda e: e.dma_start(o, i), after, s.sem)
                sp.n -= 1
            else:
                q.put(lambda e: e.dma_start(o, i), after, s.sem)
                q.n -= 1
            s.n += 16
            clock[(id(s.sem), s.n)] = q.t + 2000.0 + width(o) * 128 * 4 / 200.0
            return s.token()

        class Area:
            def __init__(self, at, end=WKW):
                self.at, self.end = at, end

            def take(self, n):
                a = self.at
                self.at += n
                assert self.at <= self.end, self.at
                return WK[:, a:a + n]

        keep = Area(0)
        ident = keep.take(128)
        one = keep.take(1)
        half = keep.take(1)
        nw = keep.take(8)
        nw2 = keep.take(8)
        naq, nak, sq_, sk_ = (keep.take(1) for _ in range(4))
        ss = keep.take(128)
        rs = keep.take(128)
        base = keep.at
        tail = WK[:, WKW - 512:WKW]

        c_const = slot("c_const")
        dma(sp, c_const, ident, masks[0])
        dma(sp, c_const, nw, norm_w)
        dma(sp, c_const, nw2, gain2)
        for b in (0, 64):
            dma(sp, c_const, naq[b:b + 64, :], gq)
            dma(sp, c_const, nak[b:b + 64, :], gk)
        dma(sp, c_const, sq_, sbq)
        dma(sp, c_const, sk_, sbk)
        t_const = c_const.token()
        mset(dve, one, 1.0)
        t_one = mset(dve, half, -0.5)
        ts(dve, naq, naq, 0.125, None, ALU.mult, after=[t_const])
        t_gain = ts(dve, sq_, sq_, 128.0 ** -0.5, None, ALU.mult)

        def rsqrt(cols, n, after=()):
            a, r = ss[:, cols[0]:cols[1]], rs[:, cols[0]:cols[1]]
            ts(pool, a, a, 1.0 / n, EPS, ALU.mult, ALU.add, after=[*after, t_one])
            return tt(pool, r, a, half.to_broadcast([128, cols[1] - cols[0]]), ALU.pow)

        def seg(w, k):
            return w[k * 128:(k + 1) * 128, :]

        blocks = []
        w_segs = w_in[:, 0:4096].rearrange("r (s c) -> r s c", c=512)
        w2_segs = w_in2.rearrange("r (s c) -> r s c", c=1024)

        def add_block(width, src):
            blocks.append((width, src))

        for p in range(4):
            add_block(512, lambda k, p=p: w_segs[k * 128:(k + 1) * 128, 0:4, p * 128:(p + 1) * 128])
        add_block(16, lambda k: w_in[k * 128:(k + 1) * 128, 4096:4112])
        add_block(512, lambda k: w_segs[k * 128:(k + 1) * 128, 7, :])
        for h in range(4):
            add_block(384, lambda k, h=h: w_segs[k * 128:(k + 1) * 128, 4:7, h * 128:(h + 1) * 128])
        for cb in range(2):
            add_block(512, lambda k, cb=cb: w_out[k * 128:(k + 1) * 128, cb * 512:(cb + 1) * 512])
        for h in range(8):
            add_block(512, lambda k, h=h: w2_segs[k * 128:(k + 1) * 128, 0:4, h * 128:(h + 1) * 128])
        for cb in range(2):
            add_block(512, lambda k, cb=cb: w2_segs[k * 128:(k + 1) * 128, 8, cb * 512:(cb + 1) * 512])
        for h in range(4):
            for s in (4, 6):
                add_block(512, lambda k, h=h, s=s: w2_segs[k * 128:(k + 1) * 128, s:s + 2, h * 256:(h + 1) * 256])
        for cb in range(2):
            add_block(512, lambda k, cb=cb: w2_segs[k * 128:(k + 1) * 128, 9, cb * 512:(cb + 1) * 512])
        for w in (w_sb, w_ret, w_out2):
            for cb in range(2):
                add_block(512, lambda k, w=w, cb=cb: w[k * 128:(k + 1) * 128, cb * 512:(cb + 1) * 512])

        tiles = [(b, k) for b in range(len(blocks)) for k in range(8)]
        c_raw = [slot(f"c_raw{i}") for i in range(NRAW)]
        raw_free = [[] for _ in range(NRAW)]
        wh_free = [[] for _ in range(NSLOT)]
        ready = {}
        prepped = [0]
        loaded = [0]

        def load_next():
            n = loaded[0]
            if n >= len(tiles):
                return
            b, k = tiles[n]
            width, src = blocks[b]
            d = RAW[:, n % NRAW, 0:width]
            s = src(k)
            if len(s.shape) == 3:
                d = d.rearrange("p (s c) -> p s c", c=s.shape[2])
            dma(sp, c_raw[n % NRAW], d, s, after=raw_free[n % NRAW])
            loaded[0] += 1

        def prep_next():
            n = prepped[0]
            if n >= len(tiles):
                return
            width = blocks[tiles[n][0]][0]
            r, w = RAW[:, n % NRAW, 0:width], WH[:, n % NSLOT, :]
            arrived = (c_raw[n % NRAW].sem, 16 * (n // NRAW + 1))
            hi = af(w[:, 0:width], r, ACT.Copy, after=[arrived, *wh_free[n % NSLOT]])
            lo = tt(dve, w[:, 512:512 + width], r, w[:, 0:width].bitcast(F32), ALU.subtract, after=[hi])
            ready[n] = lo
            raw_free[n % NRAW] = [lo]
            prepped[0] += 1
            load_next()

        for _ in range(NRAW):
            load_next()

        side = []

        class Stream:
            def __init__(self, gen):
                self.gen, self.wake = gen, 0.0

            def step(self):
                ran = False
                while self.wake <= pe.t:
                    clock["side"] = 0.0
                    try:
                        said = next(self.gen)
                    except StopIteration:
                        side.remove(self)
                        return True
                    if said == "idle":
                        return ran
                    ran = True
                    self.wake = clock["side"]
                return ran

        def spawn(g):
            side.append(Stream(g))

        def pump(idle=False):
            ran = [s.step() for s in list(side)]
            if idle and not any(ran):
                later = [s.wake for s in side if s.wake > pe.t]
                assert later, "streams wait for each other"
                pe.t = min(later)

        def drain():
            while side:
                pump(True)

        def fence():
            marks = [q.last() for q in (pe, act, dve, pool)] + [s.token() for s in slots if s.n and s not in c_raw]
            marks = [m for m in marks if m[1]]
            return marks

        cur = [0]
        mb = [0]
        mfree = [[] for _ in range(8)]
        ring_banks = list(range(8))

        def next_bank():
            mb[0] += 1
            return ring_banks[mb[0] % len(ring_banks)]

        def use_banks(banks, after=()):
            for b in banks:
                if b not in ring_banks:
                    mfree[b] = list(after)
            ring_banks[:] = banks

        def token_groups(consume, after_tile, width=512):
            b = cur[0]
            cur[0] += 1
            assert blocks[b][0] == width
            while prepped[0] < 8 * b + 8:
                prep_next()
            for t in range(8):
                tile_tokens = after_tile(t)
                m = next_bank()
                ps = bank(m, width)
                for k in range(8):
                    n = 8 * b + k
                    w = WH[:, n % NSLOT, :]
                    aft = [ready[n]]
                    if k == 0:
                        aft += mfree[m] + tile_tokens
                    hh, hl = HH[:, k, t * 128:(t + 1) * 128], HL[:, k, t * 128:(t + 1) * 128]
                    mm(ps, hh, w[:, 0:width], k == 0, False, after=aft)
                    mm(ps, hh, w[:, 512:512 + width], False, False)
                    tok = mm(ps, hl, w[:, 0:width], False, k == 7, sig=(k == 7 or t == 7))
                    if t == 7:
                        wh_free[n % NSLOT] = [tok]
                        prep_next() if prepped[0] < 8 * b + 16 and prepped[0] - NSLOT < 8 * b + k + 1 else None
                    pump()
                mfree[m] = consume(t, ps, tok)
                if t < 7 and prepped[0] < 8 * b + 8 + NSLOT - 8:
                    prep_next()

        def channel_groups(consume, after_tile):
            b = cur[0]
            cur[0] += 1
            while prepped[0] < 8 * b + 8:
                prep_next()
            g = 0
            for c in range(3):
                for th in range(2):
                    m = next_bank()
                    ps = bank(m)
                    for k in range(8):
                        n = 8 * b + k
                        w = WH[:, n % NSLOT, :]
                        wh, wl = w[:, c * 128:(c + 1) * 128], w[:, 512 + c * 128:512 + (c + 1) * 128]
                        hh, hl = HH[:, k, th * 512:(th + 1) * 512], HL[:, k, th * 512:(th + 1) * 512]
                        aft = [ready[n]]
                        if k == 0:
                            aft += mfree[m] + after_tile
                        mm(ps, wh, hh, k == 0, False, after=aft)
                        mm(ps, wh, hl, False, False)
                        tok = mm(ps, wl, hh, False, k == 7, sig=(k == 7 or g == 5))
                        if g == 5:
                            wh_free[n % NSLOT] = [tok]
                            prep_next() if prepped[0] < 8 * b + 16 and prepped[0] - NSLOT < 8 * b + k + 1 else None
                        pump()
                    mfree[m] = consume(c, th, ps, tok)
                    if g < 5 and prepped[0] < 8 * b + 8 + NSLOT - 8:
                        prep_next()
                    g += 1

        def to_stationary(t, src, after, scale=None, tmp=None):
            dst = slice(t * 128, (t + 1) * 128)
            for half_ in range(2):
                m = next_bank()
                ps = bank(m)
                for j in range(4):
                    k = half_ * 4 + j
                    tok = tr(ps[:, j * 128:(j + 1) * 128], src[:, k * 128:(k + 1) * 128],
                             after=[*after, *mfree[m], t_const], sig=(j == 3))
                hh, hl = HH[:, half_ * 4:half_ * 4 + 4, dst], HL[:, half_ * 4:half_ * 4 + 4, dst]
                p4 = ps.rearrange("p (k c) -> p k c", c=128)
                if scale is None:
                    hi = af(hh, p4, ACT.Copy, after=[tok])
                    lo = tt(dve, hl, p4, hh.bitcast(F32), ALU.subtract, after=[hi])
                    mfree[m] = [lo]
                else:
                    sc = scale[:, half_ * 4:half_ * 4 + 4].unsqueeze(2).to_broadcast([128, 4, 128])
                    t4 = tmp.rearrange("p (k c) -> p k c", c=128)
                    a = tt(dve, t4, p4, sc, ALU.mult, after=[tok])
                    mfree[m] = [a]
                    hi = af(hh, t4, ACT.Copy, after=[a])
                    lo = tt(dve, hl, t4, hh.bitcast(F32), ALU.subtract, after=[hi])
            return lo

        act.put(lambda e: e.preload_act_table_set("natural_log_exp_and_others"), sig=False)

        area = Area(base)
        junk = area.take(1024)
        tmp = area.take(512)
        c_x = [slot(f"c_x{i}") for i in range(8)]

        def xt(t):
            return TM[:, t // 4, (t % 4) * 1024:(t % 4 + 1) * 1024]

        for t in range(8):
            dma(sp, c_x[t], xt(t), x[t * 128:(t + 1) * 128, :])
        for t in range(8):
            s = af(junk, xt(t), ACT.Square, after=[c_x[t].token()], accum_out=ss[:, t:t + 1])
        r = rsqrt((0, 8), 1024, after=[s])
        ht = {}
        for t in range(8):
            a = ts(dve, xt(t), xt(t), rs[:, t:t + 1], None, ALU.mult, after=[r])
            ht[t] = to_stationary(t, xt(t), [a], nw, tmp)

        for _ in range(8):
            prep_next()

        area = Area(base, WKW - 512)
        tab = [area.take(23 * 64).rearrange("p (j c) -> p j c", c=64) for _ in range(2)]
        qT = area.take(1024)
        kT = area.take(1024)
        S = [area.take(576) for _ in range(2)]
        PT = [area.take(640) for _ in range(2)]
        acc = area.take(2)
        nm = area.take(2)
        sums = area.take(2)
        rinv = area.take(2)
        sqt = area.take(256)
        c_tab = [slot("c_tab0"), slot("c_tab1")]
        c_mix = [slot(f"c_mix{i}") for i in range(3)]
        mark = fence()
        dve.put(lambda e: e.memset(nm, 0.0), mark)
        act.put(lambda e: e.activation(sums, nm, ACT.Copy), [*mark, dve.last()])
        mset(pool, rinv, 0.0, after=[*mark, dve.last()])
        w_start = [dve.last(), act.last(), pool.last()]
        tm_free = [list(fence()) for _ in range(3)]
        tab_free = [list(w_start) for _ in range(2)]
        for b_ in range(2, 8):
            w_start += mfree[b_]

        def load_table(h):
            T = tab[h % 2]
            tok = None
            for ro in range(2):
                src = rpb[h, 1 - ro:15 - ro, :, :].rearrange("j w c -> w j c")
                tok = dma(pool, c_tab[h % 2], T[ro * 64:(ro + 1) * 64, 0:14, :], src, after=tab_free[h % 2])
            F = T[:, 0:14, :]
            for ro in range(2):
                Fh = T[ro * 64:(ro + 1) * 64, 0:14, :]
                a = pool.put(lambda e, Fh=Fh: e.affine_select(
                    out=Fh[:, :, 0:48], in_=Fh[:, :, 0:48], pattern=[[0, 14], [1, 48]], compare_op=ALU.is_ge,
                    fill=NEG, base=8, channel_multiplier=-1), [tok])
                a = pool.put(lambda e, Fh=Fh: e.affine_select(
                    out=Fh[:, :, 16:64], in_=Fh[:, :, 16:64], pattern=[[0, 14], [-1, 48]], compare_op=ALU.is_ge,
                    fill=NEG, base=7 - 16, channel_multiplier=1))
            a = pool.put(lambda e: e.tensor_copy(T[:, 14:23, :], T[:, 2:11, :]))
            a = mset(pool, T[64:128, 14, :], NEG)
            a = mset(pool, T[0:64, 22, :], NEG)
            return a

        def transposed(dst, src, gain, after, bk, free):
            for g in range(2):
                for j in range(4):
                    tok = tr(bank(bk)[:, j * 128:(j + 1) * 128], src(g * 4 + j), after=[*after, *free], sig=(j == 3))
                if gain is None:
                    free = [af(dst[:, g * 512:(g + 1) * 512], bank(bk), ACT.Copy, after=[tok])]
                else:
                    free = [af(dst[:, g * 512:(g + 1) * 512], bank(bk), ACT.Copy, after=[tok, t_gain], scale=gain)]
                yield free

        def exp_ln_set():
            act.put(lambda e: e.preload_act_table_set("natural_log_exp_and_others"), sig=False, cost=1300)

        def silu_in_place(z, e, after=()):
            a = af(z, z, ACT.Silu, after=after)
            if e:
                exp_ln_set()
            return a

        state = {"pe_na": [[], []], "table": {}}
        state["table"][0] = load_table(0)
        state["table"][1] = load_table(1)
        done = {}

        def na_side(p, buf, ev):
            B = TM[:, buf, :].rearrange("p (t c) -> p t c", c=512)
            qk = B[:, :, 0:256].rearrange("p t (g d) -> p t g d", d=64)
            c0 = (p % 3) * 32
            r = rsqrt((c0, c0 + 32), 64, after=[ev])
            sc = rs[:, c0:c0 + 32].rearrange("p (t g) -> p t g", g=4)
            for t in range(8):
                a = tt(dve, qk[:, t], qk[:, t], sc[:, t].unsqueeze(2).to_broadcast([128, 4, 64]), ALU.mult, after=[r])
            yield
            while p and not (done.get(("na", p - 1, 0)) and done.get(("na", p - 1, 1))):
                yield "idle"
            free = [*state.get("pt_free0", []), *state["pe_na"][0], *state["pe_na"][1]]
            for dst, o, g in ((qT, 0, naq), (kT, 128, nak)):
                for f in transposed(dst, lambda t, o=o: B[:, t, o:o + 128], g, [a, *w_start], 4, free):
                    free = f
                    yield
            state["pt_free0"] = free
            sz = silu_in_place(B[:, :, 384:512], True, after=[pe.last()])
            state[("qk", p)] = [free[0], sz]
            done[("naqk", p)] = True

        def na_head(p, buf, h):
            B = TM[:, buf, :].rearrange("p (t c) -> p t c", c=512)
            while not done.get(("naqk", p)):
                yield "idle"
            qk_tok, sz = state[("qk", p)]
            hd = 2 * p + h
            tok_tab = state["table"][hd]
            T = tab[h]
            P = slice(h * 64, h * 64 + 64)
            Sb, Pb = S[h], PT[h]
            sbk = 2 + 3 * h if h == 0 else 5
            c0 = sbk * 512
            ptb = 4 if h == 0 else 7
            key = lambda n: n + str(h)
            for i in range(8):
                inner = 2 <= i <= 5
                k0 = i - 2 if inner else (0 if i < 2 else 4)
                nk = 576 if inner else 512
                q = qT[P, i * 128:(i + 1) * 128]
                tok = mm(PS[:, c0:c0 + 512], q, kT[P, k0 * 128:k0 * 128 + 512], True, True,
                         after=[qk_tok, *state.get(key("s_free"), [])], sig=True)
                if inner:
                    tok = mm(PS[:, c0 + 512:c0 + 576], q, kT[P, k0 * 128 + 512:k0 * 128 + 576], True, True, sig=True)
                j0 = 14 if inner else 2 * k0 - 2 * i + 7 - 1
                tb = T[:, j0:j0 + nk // 64, :].rearrange("p j c -> p (j c)")
                b = dve.put(lambda e, Sb=Sb, nk=nk, tb=tb, c0=c0: e.tensor_tensor_reduce(
                    out=Sb[:, 0:nk], in0=PS[:, c0:c0 + nk], in1=tb, scale=-1.0, scalar=3.0e38, op0=ALU.add,
                    op1=ALU.min, accum_out=nm[:, h:h + 1]), [tok, tok_tab, *state.get(key("s"), []), *state.get(key("e"), [])],
                    cost=70 + 1.04 * nk)
                if i == 7:
                    tab_free[h] = [b]
                ex = af(Sb[:, 0:nk], Sb[:, 0:nk], ACT.Exp, after=[b], bias=nm[:, h:h + 1], scale=-1.0,
                        accum_out=sums[:, h:h + 1])
                state[key("e")] = [ex]
                recip(rinv[:, h:h + 1], sums[:, h:h + 1], after=[ex])
                yield
                for j in range(4):
                    tok = tr(bank(ptb)[:, j * 128:(j + 1) * 128], Sb[:, j * 128:(j + 1) * 128],
                             after=[ex, b, *state.get("pt_free" + str(h), [])], sig=(j == 3))
                if inner:
                    tok = tr(PS[0:64, c0 + 640:c0 + 768], Sb[:, 512:576], sig=True)
                state[key("s")] = [tok]
                c = af(Pb[:, 0:512], bank(ptb), ACT.Copy, after=[tok, *state.get(key("pt"), [])])
                state["pt_free" + str(h)] = [c]
                if inner:
                    c = af(Pb[0:64, 512:640], PS[0:64, c0 + 640:c0 + 768], ACT.Copy, par=True)
                yield
                V = B[:, :, 256 + h * 64:256 + h * 64 + 64]
                O = PS[:, c0 + 896:c0 + 960]
                for j in range(4):
                    tok = mm(O, Pb[:, j * 128:(j + 1) * 128], V[:, k0 + j, :], j == 0, (j == 3) and not inner,
                             after=[c, b], sig=(j == 3))
                if inner:
                    tok = mm(O, Pb[0:64, 512:640], V[0:64, k0 + 4, :], False, True, sig=True)
                state[key("pt")] = [tok]
                o = stt(B[:, i, 128 + h * 64:128 + h * 64 + 64], O, rinv[:, h:h + 1],
                        B[:, i, 384 + h * 64:384 + h * 64 + 64], ALU.mult, ALU.mult, after=[tok, sz])
                state[key("s_free")] = [o]
                yield
            if hd + 2 < 8:
                state["table"][hd + 2] = load_table(hd + 2)
            state["pe_na"][h] = [pe.last(), o]
            done[("na", p, h)] = True
            if done.get(("na", p, 1 - h)):
                w = dma(pool, c_mix[buf], mix_d.rearrange("(t p) c -> p t c", p=128)[:, :, p * 128:(p + 1) * 128],
                        B[:, :, 128:256], after=[o])
                tm_free[buf] = [w, pe.last(), o]
                done[("naw", p)] = True

        def na_consume(buf, p):
            B = TM[:, buf, :].rearrange("p (t c) -> p t c", c=512)

            def f(t, ps, tok):
                a = af(B[:, t, :], ps, ACT.Copy, after=[tok, *tm_free[buf]])
                q = B[:, t, 0:256]
                tt(dve, sqt, q, q, ALU.mult, after=[a, *w_start])
                c0 = (p % 3) * 32 + t * 4
                red(ss[:, c0:c0 + 4], sqt.rearrange("p (g d) -> p g d", d=64), ALU.add)
                return [a]
            return f

        use_banks([0, 1])
        for p in range(4):
            buf = p % 3
            if p >= 3:
                while not done.get(("naw", p - 3)):
                    pump(True)
            token_groups(na_consume(buf, p), lambda t: [ht[t]])
            spawn(na_side(p, buf, dve.last()))
            spawn(na_head(p, buf, 0))
            spawn(na_head(p, buf, 1))
        w_tok = [ht[7]]

        gt_in = tail[:, 0:128].rearrange("p (t c) -> p t c", c=16)

        def gt_consume(t, ps, tok):
            return [af(gt_in[:, t, :], ps, ACT.Copy, after=[tok])]

        token_groups(gt_consume, lambda t: [], width=16)
        c_dz = [slot("c_dz0"), slot("c_dz1")]
        while not done.get(("naw", 1)):
            pump(True)
        Z2 = TM[:, 1, :].rearrange("p (t c) -> p t c", c=512)

        def dz_consume(t, ps, tok):
            return [af(Z2[:, t, :], ps, ACT.Copy, after=[tok, *tm_free[1]])]

        token_groups(dz_consume, lambda t: [])
        drain()
        area = Area(base)
        mark = fence()
        MK = TM[:, 0, 3088:3088 + 14 * 64].bitcast(mybir.dt.bfloat16).rearrange("p (l d c) -> p l d c", l=7, d=2)
        tri = area.take(256).rearrange("p (d c) -> p d c", d=2)
        onesq = area.take(128)
        dnw = area.take(128)
        cw = area.take(60).rearrange("p (g j) -> p g j", j=5)
        cst = area.take(16)
        G, g_, beta, kdf, eGL, bg = (area.take(64) for _ in range(6))
        gtmp = area.take(64)
        OA = area.take(1024).rearrange("p (t c) -> p t c", c=128)
        sets = [[area.take(512) for _ in range(6)] for _ in range(2)]
        St = area.take(256).rearrange("p (d c) -> p d c", d=2)
        Vn = area.take(256).rearrange("p (d c) -> p d c", d=2)
        sets[0].append(area.take(512))
        sets[1].append(area.take(512))
        mset(dve, onesq, 1.0, after=mark)
        mset(pool, gtmp, 0.0, after=mark)
        act.put(lambda e: e.activation(G[:, 0:1], onesq[:, 0:1], ACT.Copy), [*mark, dve.last()])
        c_dn = slot("c_dn")
        dn_mark = [dve.last(), act.last(), pool.last()]
        mk32 = TM[:, 2, 0:14 * 128].rearrange("p (m c) -> p m c", c=128)
        dma(pool, c_dn, mk32, masks[1:15].rearrange("m p c -> p m c"), after=dn_mark + tm_free[2])
        dma(pool, c_dn, tri, masks[15:17].rearrange("m p c -> p m c"), after=dn_mark)
        dma(pool, c_dn, dnw, dn_w.to_broadcast([128, 128]), after=dn_mark)
        dma(pool, c_dn, cw, conv_w, after=dn_mark)
        dma(pool, c_dn, cst[:, 0:8], a_log.to_broadcast([128, 8]), after=dn_mark)
        dma(pool, c_dn, cst[:, 8:16], dt_bias.to_broadcast([128, 8]), after=dn_mark)
        mkt = dve.put(lambda e: e.tensor_copy(MK.rearrange("p l d c -> p (l d) c"), mk32), [c_dn.token(), *tm_free[0]])
        tm_free[2] = [mkt]
        t_dn = c_dn.token()
        a = af(Z2, Z2, ACT.Silu)
        w = dma(pool, c_dz[0], dz_d.rearrange("(t p) c -> p t c", p=128), Z2, after=[a])
        exp_ln_set()
        tm_free[1] = [w]
        dz_written = w
        gv = gt_in.rearrange("p t (d k h) -> p d k h t", d=2, k=2)

        def col(a, d):
            return a[:, d * 32:(d + 1) * 32].rearrange("p (h t) -> p h t", t=8)

        for d in range(2):
            a = af(col(beta, d), gv[:, d, 0], ACT.Exp, scale=-1.0)
        ts(dve, beta, beta, 1.0, None, ALU.add, after=[a])
        recip(beta, beta)
        al = af(cst[:, 0:8], cst[:, 0:8], ACT.Exp, after=[t_dn])
        for d in range(2):
            db = cst[:, 8 + 4 * d:12 + 4 * d].unsqueeze(2).to_broadcast([128, 4, 8])
            a = tt(dve, col(g_, d), gv[:, d, 1], db, ALU.add, after=[t_dn, al])
        a = af(gtmp, g_, ACT.Abs, after=[a, pool.last()])
        a = af(gtmp, gtmp, ACT.Exp, scale=-1.0)
        a = af(gtmp, gtmp, ACT.Ln, bias=1.0)
        stt(g_, g_, 0.0, gtmp, ALU.max, ALU.add, after=[a])
        for d in range(2):
            ab = cst[:, 4 * d:4 * d + 4].unsqueeze(2).to_broadcast([128, 4, 8])
            tt(dve, col(g_, d), col(g_, d), ab, ALU.mult)
        gg = ts(dve, g_, g_, -1.0, None, ALU.mult)
        p5 = bank(5)
        for d in range(2):
            mm(p5[:, 32 * d:32 * d + 32], tri[:, d, :], g_[:, 32 * d:32 * d + 32], True, True, after=[gg, t_dn])
        tok = mm(p5[:, 64:128], onesq, g_, True, True, sig=True)
        a = af(G, p5[:, 0:64], ACT.Copy, after=[tok])
        a = af(bg, G, ACT.Exp)
        b = af(eGL, p5[:, 64:128], ACT.Exp)
        c = tt(dve, kdf, p5[:, 64:128], G, ALU.subtract, after=[b])
        tt(dve, bg, bg, beta, ALU.mult)
        b = af(kdf, kdf, ACT.Exp, after=[c])
        dn_free5 = [b]
        t_gates = [b, dve.last()]

        def raw_buf():
            return TM[:, 0, 0:3 * 1028].rearrange("p (g t) -> p g t", t=1028)

        out_free = {1: tm_free[1], 2: tm_free[2]}

        def dn_consume(h):
            R = raw_buf()

            def f(c, th, ps, tok):
                a = []
                if c == 0 and th == 0:
                    mset(pool, R[:, :, 0:2], 0.0, after=tm_free[0])
                    a = [mset(pool, R[:, :, 1026:1028], 0.0)]
                    dn_st["pad"] = a
                return [af(R[:, c, 2 + th * 512:2 + (th + 1) * 512], ps, ACT.Copy, after=[tok, *tm_free[0]])]
            return f

        dn_st = {"pb": {0: [], 1: [], 2: []}, "free5": dn_free5, "free7": []}

        def dn_prepare(h, ob, ev):
            R = raw_buf()
            C = TM[:, ob, 0:3072].rearrange("p (g t) -> p g t", t=1024)
            while h >= 2 and not done.get(("dn", h - 2)):
                yield "idle"
            for c in range(3):
                w = cw[:, c * 4 + h, :]
                ts(dve, C[:, c, :], R[:, c, 0:1024], w[:, 0:1], None, ALU.mult,
                   after=[*ev, *dn_st["pad"], t_dn, *out_free[ob]])
                for j in range(1, 5):
                    a = stt(C[:, c, :], R[:, c, j:j + 1024], w[:, j:j + 1], C[:, c, :], ALU.mult, ALU.add)
                    yield
            s = silu_in_place(C, True, after=[a])
            yield
            qt = TM[:, 0, 0:1024].rearrange("p (t c) -> p t c", c=128)
            kt0 = TM[:, 0, 1024:2048].rearrange("p (t c) -> p t c", c=128)
            kt = TM[:, ob, 2048:3072].rearrange("p (t c) -> p t c", c=128)
            vt = TM[:, ob, 3072:4096].rearrange("p (t c) -> p t c", c=128)
            bk = 2
            free = dn_st["pb"][2]
            for c, dst in ((0, qt), (1, kt0), (2, vt)):
                for f in transposed(dst.rearrange("p t c -> p (t c)"), lambda t, c=c: C[:, c, t * 128:(t + 1) * 128],
                                    None, [s], bk, free):
                    free = f
                    yield
            e = TM[:, 0, 2048:3072].rearrange("p (t c) -> p t c", c=128)
            for n, src in ((0, qt), (1, kt0)):
                tt(dve, e, src, src, ALU.mult, after=free)
                a = red(ss[:, 32 + n * 8:40 + n * 8], e, ALU.add)
                yield
            r = rsqrt((32, 48), 1.0, after=[a])
            a = ts(dve, rs[:, 32:40], rs[:, 32:40], 128.0 ** -0.5, None, ALU.mult, after=[r])
            yield
            a = tt(dve, qt, qt, rs[:, 32:40].unsqueeze(2).to_broadcast([128, 8, 128]), ALU.mult)
            a = tt(dve, kt, kt0, rs[:, 40:48].unsqueeze(2).to_broadcast([128, 8, 128]), ALU.mult, after=[pe.last()])
            yield
            for c, src in ((0, qt), (1, kt)):
                for f in transposed(C[:, c, :], lambda t, src=src: src[:, t, :], None, [a], bk, free):
                    free = f
                    yield
            dn_st["pb"][2] = free
            dn_st[("in", h)] = [free[0], a]
            tm_free[0] = [pe.last(), a, free[0]]
            done[("prep", h)] = True

        def half_inverse(h, ob, j, ss_):
            while not done.get(("prep", h)) or (j >= 2 and not done.get(("rec", h, j - 2))) or (
                    j < 2 and h and not done.get(("rec", h - 1, j + 2))):
                yield "idle"
            AT, X, XT, Y, aT, E, TB = sets[ss_]
            b0, b1 = (3, 4) if ss_ == 0 else (5, 6)
            A, Bk = bank(b0), bank(b1)
            u4 = lambda a: a.rearrange("p (u c) -> p u c", c=128)
            d4 = lambda a: a.rearrange("p (d s c) -> p d s c", d=2, s=2)
            chunks = [2 * j, 2 * j + 1, 6 - 2 * j, 7 - 2 * j]
            cols = [d * 32 + h * 8 + c for d, c in zip((0, 0, 1, 1), chunks)]
            kT_ = TM[:, ob, 1024:2048]
            qT_ = TM[:, ob, 0:1024]
            kt = TM[:, ob, 2048:3072]
            vt = TM[:, ob, 3072:4096]
            cs = lambda a, c: a[:, c * 128:(c + 1) * 128]
            src = dn_st[("in", h)]
            fr = [*dn_st.get(("set", ss_), dn_free5), *t_gates]
            for u in range(4):
                a = af(u4(TB)[:, u, :], tri[:, u // 2, :], ACT.Copy, after=fr, par=u > 0, scale=g_[:, cols[u]:cols[u] + 1])
                b = af(u4(Y)[:, u, :], ident, ACT.Copy, par=True, scale=beta[:, cols[u]:cols[u] + 1])
            yield
            gr = mm(A, onesq, TB, True, True, after=[b, *fr], sig=True)
            br = mm(Bk, onesq, Y, True, True, sig=True)
            yield
            for u in range(4):
                a = ts(dve, u4(E)[:, u, :], u4(A)[:, u, :], G[:, cols[u]:cols[u] + 1], 0.0, ALU.subtract, ALU.min,
                       after=[gr, *fr], par=u > 0)
            e = af(E, E, ACT.Exp, after=[a])
            qe = af(TB, A, ACT.Exp)
            tri4 = tri.unsqueeze(2).to_broadcast([128, 2, 2, 128])
            yield
            e = tt(dve, d4(E), d4(E), tri4, ALU.mult, after=[e])
            beta_row = af(X, Bk, ACT.Copy, after=[br])
            yield
            for u in range(4):
                kk = mm(u4(A)[:, u, :], cs(kT_, chunks[u]), cs(kT_, chunks[u]), True, True, after=[qe, e, *src],
                        sig=(u == 3))
            for u in range(4):
                kq = mm(u4(Bk)[:, u, :], cs(kT_, chunks[u]), cs(qT_, chunks[u]), True, True, after=[beta_row],
                        sig=(u == 3))
            yield
            a = tt(dve, aT, Bk, E, ALU.mult, after=[kq])
            tt(dve, AT, A, E, ALU.mult, after=[kk])
            stt(AT, AT, -1.0, X, ALU.mult, ALU.mult, after=[beta_row])
            yield
            mk = lambda l: MK[:, l].unsqueeze(2).to_broadcast([128, 2, 2, 128])
            tt(dve, d4(XT), d4(AT), MK[:, 6].unsqueeze(2).to_broadcast([128, 2, 2, 128]), ALU.mult, after=[mkt])
            a = tt(dve, u4(XT), u4(XT), ident.unsqueeze(1).to_broadcast([128, 4, 128]), ALU.add)
            yield
            for u in range(4):
                t_ = tr(u4(A)[:, u, :], u4(XT)[:, u, :], after=[a], sig=(u == 3))
            a = xe = af(X, A, ACT.Copy, after=[t_])
            yield
            for l in range(6):
                for u in range(4):
                    y = mm(u4(A)[:, u, :], u4(AT)[:, u, :], u4(X)[:, u, :], True, True, after=[a, xe] if u == 0 else (), sig=(u == 3))
                if l:
                    o_, i_, z_ = late_xt
                    tt(dve, o_, o_, i_, ALU.add, after=[z_])
                yield
                ym = tt(dve, d4(Y), d4(A), mk(l), ALU.mult, after=[y])
                yield
                if l < 5:
                    for u in range(4):
                        z = mm(u4(A)[:, u, :], u4(XT)[:, u, :], u4(Y)[:, u, :], True, True, after=[ym], sig=(u == 3))
                    xa = tt(dve, X, X, A, ALU.add, after=[z])
                for u in range(4):
                    z = mm(u4(Bk)[:, u, :], u4(Y)[:, u, :], u4(XT)[:, u, :], True, True, after=[ym], sig=(u == 3))
                if l < 5:
                    a = xa
                    late_xt = (XT, Bk, z)
                else:
                    a = tt(dve, XT, XT, Bk, ALU.add, after=[z])
                yield
            for u in range(4):
                vb = af(u4(Y)[:, u, :], cs(vt, chunks[u]), ACT.Copy, after=[z, *src], par=u > 0, scale=beta[:, cols[u]:cols[u] + 1])
                kb = af(u4(E)[:, u, :], cs(kt, chunks[u]), ACT.Copy, after=[a], par=True, scale=bg[:, cols[u]:cols[u] + 1])
            for d in range(2):
                c0 = chunks[2 * d]
                qg = tt(dve, AT[:, d * 256:(d + 1) * 256], TB[:, d * 256:(d + 1) * 256],
                        qT_[:, c0 * 128:(c0 + 2) * 128], ALU.mult, after=[z])
            yield
            for u in range(4):
                uu = mm(u4(A)[:, u, :], u4(XT)[:, u, :], u4(Y)[:, u, :], True, True, after=[kb, a], sig=(u == 3))
            for u in range(4):
                ww = mm(u4(Bk)[:, u, :], u4(E)[:, u, :], u4(XT)[:, u, :], True, True, sig=(u == 3))
            yield
            ue = af(X, A, ACT.Copy, after=[uu])
            we = af(Y, Bk, ACT.Copy, after=[ww], scale=-1.0)
            for u in range(4):
                kd = af(u4(XT)[:, u, :], cs(kt, chunks[u]), ACT.Copy, after=[ww], par=u > 0, scale=kdf[:, cols[u]:cols[u] + 1])
            yield
            dn_st[("out", h, j)] = [ue, we, kd, qg]
            done[("pre", h, j)] = True

        def recursion(h, ob):
            D3 = bank(7)
            ws = D3[:, 0:256].rearrange("p (d c) -> p d c", d=2)
            oo = D3[:, 256:512].rearrange("p (d c) -> p d c", d=2)
            while h and not done.get(("dn", h - 1)):
                yield "idle"
            mset(dve, St, 0.0, after=dn_mark)
            s_tok = [dve.last()]
            for j in range(4):
                while not done.get(("pre", h, j)):
                    yield "idle"
                AT, X, XT, Y, aT, E, TB = sets[j % 2]
                u4 = lambda a: a.rearrange("p (u c) -> p u c", c=128)
                pre = dn_st[("out", h, j)]
                for s in range(2):
                    us = (s, 3 - s)
                    chs = (2 * j + s, 7 - 2 * j - s)
                    for d in range(2):
                        w = mm(ws[:, d, :], u4(Y)[:, us[d], :], St[:, d, :], True, True,
                               after=[*pre, *s_tok, *dn_st["free7"]], sig=(d == 1))
                    yield
                    v = tt(dve, Vn, ws, u4(X)[:, s:4 - s:3 - 2 * s, :], ALU.add, after=[w])
                    yield
                    for d in range(2):
                        mm(oo[:, d, :], u4(AT)[:, us[d], :], St[:, d, :], True, False, after=[v])
                        mm(oo[:, d, :], u4(aT)[:, us[d], :], Vn[:, d, :], False, True)
                    for d in range(2):
                        w = mm(ws[:, d, :], u4(XT)[:, us[d], :], Vn[:, d, :], True, True, sig=(d == 1))
                    yield
                    for d in range(2):
                        cl = d * 32 + h * 8 + chs[d]
                        a = stt(St[:, d, :], St[:, d, :], eGL[:, cl:cl + 1], ws[:, d, :], ALU.mult, ALU.add, after=[w])
                    s_tok = [a]
                    for d in range(2):
                        o = OA[:, chs[d], :]
                        if j < 2:
                            a = dve.put(lambda e, o=o, d=d: e.tensor_copy(o, oo[:, d, :]), dn_st.get("oa_free", dn_mark))
                        else:
                            a = tt(dve, o, o, oo[:, d, :], ALU.add)
                    dn_st["free7"] = [a]
                    yield
                dn_st[("set", j % 2)] = [pe.last(), a]
                done[("rec", h, j)] = True
            out_free[ob] = [pe.last(), a]
            done[("dn", h)] = True
            zt = TM[:, ob, 0:1024].rearrange("p (t c) -> p t c", c=128)
            e = TM[:, ob, 1024:2048].rearrange("p (t c) -> p t c", c=128)
            lz = dma(pool, c_dz[1], zt, dz_d.rearrange("(t p) c -> p t c", p=128)[:, :, h * 128:(h + 1) * 128],
                     after=[dz_written, pool.last(), *out_free[ob]])
            tt(dve, e, OA, OA, ALU.mult, after=[pe.last(), pool.last()])
            a = red(ss[:, 48:56], e, ALU.add)
            r = rsqrt((48, 56), 128, after=[a])
            out_free[ob] = [dve.last()]
            yield
            tt(dve, OA, OA, rs[:, 48:56].unsqueeze(2).to_broadcast([128, 8, 128]), ALU.mult, after=[r])
            tt(dve, OA, OA, dnw.unsqueeze(1).to_broadcast([128, 8, 128]), ALU.mult)
            a = tt(dve, OA, OA, zt, ALU.mult, after=[lz])
            out_free[ob] = [a]
            w = dma(pool, c_mix[2], mix_d.rearrange("(t p) c -> p t c", p=128)[:, :, 512 + h * 128:512 + (h + 1) * 128],
                    OA, after=[a])
            dn_st["oa_free"] = [w]
            done[("dnall", h)] = True
            yield

        def dn_head(h):
            ob = 1 + h % 2
            for j in range(0, 4):
                yield from half_inverse(h, ob, j, j % 2)

        def lane(s):
            for h in range(4):
                for j in (s, s + 2):
                    yield from half_inverse(h, 1 + h % 2, j, s)

        def rec_lane():
            for h in range(4):
                while h and not done.get(("dnall", h - 1)):
                    yield "idle"
                yield from recursion(h, 1 + h % 2)

        spawn(lane(0))
        spawn(lane(1))
        spawn(rec_lane())
        for h in range(4):
            while h and not done.get(("prep", h - 1)):
                pump(True)
            channel_groups(dn_consume(h), [])
            ev = [act.last()]
            spawn(dn_prepare(h, 1 + h % 2, ev))
        drain()

        area = Area(base)
        mark = fence()
        use_banks(list(range(8)), mark)
        ring = [area.take(1024) for _ in range(4)]
        h2 = [area.take(1024) for _ in range(2)]
        tmp = area.take(512)
        junk = area.take(1024)
        c_ring = [slot(f"c_ring{i}") for i in range(4)]
        c_x1 = slot("c_x1out")
        ring_free = [list(mark) for _ in range(4)]
        nring = [0]

        def feed(src):
            i = nring[0] % 4
            nring[0] += 1
            tok = dma(pool, c_ring[i], ring[i], src, after=ring_free[i])
            return ring[i], tok, i

        fed = {t: feed(mix_d[t * 128:(t + 1) * 128, :]) for t in range(4)}
        for t in range(8):
            if t >= 4:
                fed[t] = feed(mix_d[t * 128:(t + 1) * 128, :])
            buf, tok, i = fed.pop(t)
            ht[t] = to_stationary(t, buf, [tok, *mark])
            ring_free[i] = [pe.last()]
        c_x = [slot(f"c_xr{i}") for i in range(8)]
        for t in range(8):
            dma(pool, c_x[t], xt(t), x[t * 128:(t + 1) * 128, :], after=mark)
        last_w = {}

        def wo_consume(cb):
            def f(t, ps, tok):
                o = xt(t)[:, cb * 512:(cb + 1) * 512]
                a = tt(dve, o, ps, o, ALU.add, after=[tok, c_x[t].token()])
                if cb:
                    dma(pool, c_x1, x1_d[t * 128:(t + 1) * 128, :], xt(t), after=[a])
                    s = af(junk, xt(t), ACT.Square, after=[a, *mark], accum_out=ss[:, t:t + 1])
                    r = rsqrt((t, t + 1), 1024, after=[s])
                    b = ts(dve, h2[t % 2], xt(t), rs[:, t:t + 1], None, ALU.mult, after=[r, *last_w.get(t % 2, mark)])
                    late.append((t, b, tok))
                return [a]
            return f

        late = []
        token_groups(wo_consume(0), lambda t: [ht[t]])

        def wo_tile_hook(t):
            while late:
                t0, b, tok = late.pop(0)
                pend.append((t0, b))
            if len(pend) > 0:
                t0, b = pend.pop(0)
                ht[t0] = to_stationary(t0, h2[t0 % 2], [b, *mark], nw2, tmp)
                last_w[t0 % 2] = [pe.last()]
            return []

        pend = []
        token_groups(wo_consume(1), wo_tile_hook)
        wo_tile_hook(8)

        area = Area(base, WKW - 512)
        mark = fence()
        lanes = [dict(qT=area.take(1024), kT=area.take(1024), L=area.take(1024), P=area.take(1025)) for _ in range(2)]
        sqt = area.take(256)
        sm = area.take(128)
        c_sb = slot("c_sb")
        c_oa = [slot(f"c_oa{i}") for i in range(3)]
        mset(dve, sqt, 0.0, after=mark)
        mset(pool, tail, 0.0, after=mark)
        act.put(lambda e: e.activation(lanes[0]["L"][:, 0:1], sqt[:, 0:1], ACT.Copy), [*mark, dve.last()])
        dma(pool, c_sb, sm, masks[17], after=mark)
        w_start = [dve.last(), act.last(), pool.last(), c_sb.token()]
        use_banks([0, 1], mark)
        for b_ in range(2, 8):
            w_start += mfree[b_]
        tm_free = [list(mark) for _ in range(3)]
        state = {}

        def norm_consume(buf, dh, ng, cols):
            B = TM[:, buf, :].rearrange("p (t c) -> p t c", c=512)

            def f(t, ps, tok):
                a = af(B[:, t, :], ps, ACT.Copy, after=[tok, *tm_free[buf]])
                q = B[:, t, 0:256]
                tt(dve, sqt, q, q, ALU.mult, after=[a, *w_start])
                red(ss[:, cols + t * ng:cols + t * ng + ng], sqt.rearrange("p (g d) -> p g d", d=dh), ALU.add)
                return [a]
            return f

        def sb_side(h, buf, ev):
            ln = h % 2
            W = lanes[ln]
            qT, kT, L, Pm = W["qT"], W["kT"], W["L"], W["P"]
            z0, tb = (2, 4) if ln == 0 else (5, 7)
            st = lambda n: state.get((n, ln), [])
            B = TM[:, buf, :].rearrange("p (t c) -> p t c", c=512)
            qk = B[:, :, 0:256].rearrange("p t (g d) -> p t g d", d=128)
            c0 = (h % 3) * 16
            r = rsqrt((c0, c0 + 16), 128, after=[ev])
            sc = rs[:, c0:c0 + 16].rearrange("p (t g) -> p t g", g=2)
            for t in range(8):
                a = tt(dve, qk[:, t], qk[:, t], sc[:, t].unsqueeze(2).to_broadcast([128, 2, 128]), ALU.mult, after=[r])
            yield
            while h >= 2 and not done.get(("sb", h - 2)):
                yield "idle"
            free = st("tb")
            for dst, o, g in ((qT, 0, sq_), (kT, 128, sk_)):
                for f in transposed(dst, lambda t, o=o: B[:, t, o:o + 128], g, [a, *w_start, *st("qk")], tb, free):
                    free = f
                    yield
            state[("tb", ln)] = free
            qk_tok = free[0]
            sz = silu_in_place(B[:, :, 384:512], True, after=[pe.last()])
            for i in range(8):
                nk = (i + 1) * 128
                zp = PS[:, z0 * 512:z0 * 512 + nk]
                for c in range(0, nk, 512):
                    w = min(512, nk - c)
                    tok = mm(PS[:, z0 * 512 + c:z0 * 512 + c + w], qT[:, i * 128:(i + 1) * 128], kT[:, c:c + w], True, True,
                             after=[qk_tok, *st("z")], sig=True)
                l = L[:, 0:nk]
                a = af(l, zp, ACT.Abs, after=[tok, *st("L")])
                a = af(l, l, ACT.Exp, scale=-1.0)
                a = af(l, l, ACT.Ln, bias=1.0)
                pm = Pm[:, 0:nk]
                stt(pm, zp, 0.0, l, ALU.max, ALU.add, after=[a, *st("P")])
                b = tt(dve, l, zp, pm, ALU.subtract)
                state[("z", ln)] = [b]
                tt(dve, Pm[:, nk - 128:nk], Pm[:, nk - 128:nk], sm, ALU.mult)
                if i == 0:
                    mset(dve, Pm[:, 1024:1025], 0.0)
                if nk > 128 or nk == 128:
                    dve.put(lambda e, nk=nk: e.tensor_tensor_scan(
                        Pm[:, 1:nk][:, ::-1], one.to_broadcast([128, nk - 1]), Pm[:, 1:nk][:, ::-1], 0.0,
                        ALU.mult, ALU.add), cost=70 + 2.1 * nk)
                b = tt(dve, L[:, 0:nk - 1], L[:, 0:nk - 1], Pm[:, 1:nk], ALU.subtract)
                a = af(l, l, ACT.Exp, after=[b])
                a = tt(dve, L[:, nk - 128:nk], L[:, nk - 128:nk], sm, ALU.mult, after=[a])
                yield
                for g in range(0, i + 1, 4):
                    n = min(4, i + 1 - g)
                    for jj in range(n):
                        tok = tr(bank(tb)[:, jj * 128:(jj + 1) * 128], L[:, (g + jj) * 128:(g + jj + 1) * 128],
                                 after=[a, *st("tb")], sig=(jj == n - 1))
                    f = af(Pm[:, g * 128:(g + n) * 128], bank(tb, n * 128), ACT.Copy, after=[tok, a])
                    state[("tb", ln)] = [f]
                    yield
                state[("L", ln)] = [tok]
                O = bank(tb, 128)
                for jj in range(i + 1):
                    tok = mm(O, Pm[:, jj * 128:(jj + 1) * 128], B[:, jj, 256:384], jj == 0, jj == i,
                             after=[f], sig=(jj == i))
                state[("P", ln)] = [tok]
                o = tt(dve, B[:, i, 128:256], O, B[:, i, 384:512], ALU.mult, after=[tok, sz])
                state[("tb", ln)] = [o]
                yield
            state[("qk", ln)] = [pe.last()]
            w = dma(pool, c_oa[buf], oa_d.rearrange("(t p) c -> p t c", p=128)[:, :, h * 128:(h + 1) * 128],
                    B[:, :, 128:256], after=[o])
            tm_free[buf] = [w, pe.last(), o]
            done[("sb", h)] = True

        for h in range(8):
            buf = h % 3
            if h >= 3:
                while not done.get(("sb", h - 3)):
                    pump(True)
            token_groups(norm_consume(buf, 128, 2, (h % 3) * 16), lambda t: [ht[t]])
            spawn(sb_side(h, buf, dve.last()))

        brow = tail
        c_br = slot("c_br")
        c_sg = [slot(f"c_sg{i}") for i in range(4)]
        sgf = [[] for _ in range(4)]
        sbufs = [TM[:, 2, i * 512:(i + 1) * 512] for i in range(4)]
        n_s = [0]
        br_free = [[pool.last()]]

        def m_consume(g, cb, br):
            def f(t, ps, tok):
                i = n_s[0] % 4
                n_s[0] += 1
                s = sbufs[i]
                a = tt(dve, s, ps, brow, ALU.add, after=[tok, br, *tm_free[2], *sgf[i]])
                br_free[0] = [a]
                w = dma(pool, c_sg[i], sig_d[g, t * 128:(t + 1) * 128, cb * 512:(cb + 1) * 512], s, after=[a])
                sgf[i] = [w]
                return [a]
            return f

        def merge_gate(g):
            for cb in range(2):
                br = dma(pool, c_br, brow, b_merge[g:g + 1, cb * 512:(cb + 1) * 512].to_broadcast([128, 512]),
                         after=br_free[0])
                token_groups(m_consume(g, cb, br), lambda t: [])

        while not done.get(("sb", 5)):
            pump(True)
        merge_gate(0)
        drain()

        area = Area(base, WKW - 512)
        mark = fence()
        CS = area.take(2048).rearrange("p (s t c) -> p s t c", s=2, c=128)
        RQ = area.take(2048).rearrange("p (d t) -> p d t", d=2)
        RK = area.take(2048).rearrange("p (d t) -> p d t", d=2)
        tq = [area.take(256).rearrange("p (g c) -> p g c", g=2) for _ in range(4)]
        Sr = [area.take(512).rearrange("p (d e) -> p d e", d=2) for _ in range(2)]
        aTr = area.take(128)
        rm = area.take(512).rearrange("p (h c) -> p h c", h=4)
        rc = area.take(8)
        grow = area.take(256)
        c_rt = slot("c_rt")
        c_gr = slot("c_gr")
        c_ob = slot("c_ob")
        mset(dve, aTr, 0.0, after=mark)
        mset(pool, tq[2], 0.0, after=mark)
        act.put(lambda e: e.activation(Sr[0][:, 0, 0:1], aTr[:, 0:1], ACT.Copy), [*mark, dve.last()])
        dma(pool, c_rt, CS, cossin.rearrange("s (t p) c -> p s t c", p=128), after=mark)
        dma(pool, c_rt, rm, retmask.rearrange("h p c -> p h c"), after=mark)
        dma(pool, c_rt, rc, retcol, after=mark)
        w_start = [dve.last(), act.last(), pool.last(), c_rt.token()]
        tm_free = [list(mark) for _ in range(3)]
        state = {"b4": [], "b5": [], "b6": [], "qk": []}
        gam = [1.0 - 2.0 ** (-5.0 - h) for h in range(4)]

        def plain_consume(buf):
            B = TM[:, buf, :].rearrange("p (t c) -> p t c", c=512)

            def f(t, ps, tok):
                return [af(B[:, t, :], ps, ACT.Copy, after=[tok, *tm_free[buf]])]
            return f

        def ret_side(h, bx, by, ev):
            BX = TM[:, bx, :].rearrange("p (t c) -> p t c", c=512)
            BY = TM[:, by, :].rearrange("p (t c) -> p t c", c=512)
            gr = dma(pool, c_gr, grow, ret_gain[h:h + 1, :].to_broadcast([128, 256]), after=[*w_start, *state.get("grow", [])])
            for t in range(8):
                v = BX[:, t, :].rearrange("p (g s c) -> p g s c", g=2, s=2)
                t1, t2 = v[:, :, 0, :], v[:, :, 1, :]
                c = CS[:, 0, t, :].unsqueeze(1).to_broadcast([128, 2, 128])
                s = CS[:, 1, t, :].unsqueeze(1).to_broadcast([128, 2, 128])
                tt(dve, tq[0], t1, c, ALU.mult, after=[*ev, *w_start])
                a = tt(dve, tq[1], t2, s, ALU.mult)
                b = tt(pool, tq[2], t1, s, ALU.mult, after=[*ev, *w_start])
                b = tt(pool, tq[3], t2, c, ALU.mult)
                tt(dve, t1, tq[0], tq[1], ALU.subtract, after=[b])
                b = tt(pool, t2, tq[2], tq[3], ALU.add, after=[a])
                yield
            rope = [b, dve.last()]
            while h and not done.get(("ret", h - 1)):
                yield "idle"
            free = state["b4"]
            for dst, o in ((RQ, 0), (RK, 256)):
                for dh in range(2):
                    for f in transposed(dst[:, dh, :], lambda t, o=o, dh=dh: BX[:, t, o + dh * 128:o + dh * 128 + 128],
                                        None, [*rope, *w_start, *state["qk"]], 4, free):
                        free = f
                        yield
            state["b4"] = free
            tr_done = [pe.last(), free[0]]
            kd = ts(dve, BX[:, :, 256:512], BX[:, :, 256:512], rc[:, 4 + h:5 + h], None, ALU.mult, after=tr_done)
            sz = silu_in_place(BY[:, :, 256:512], False, after=tr_done)
            yield
            s_tok = [mset(dve, Sr[0], 0.0, after=w_start)]
            for c in range(8):
                cc = slice(c * 128, (c + 1) * 128)
                S0, S1 = Sr[c % 2], Sr[(c + 1) % 2]
                b5, b6 = bank(5, 128), bank(5, 256, 256)
                for dh in range(2):
                    tok = mm(b5, RK[:, dh, cc], RQ[:, dh, cc], dh == 0, dh == 1, after=[*tr_done, *state["b5"]],
                             sig=(dh == 1))
                yield
                a = tt(dve, aTr, b5, rm[:, h, :], ALU.mult, after=[tok, *state.get("a", [])])
                yield
                o = bank(6, 256)
                for dh in range(2):
                    mm(o, RQ[:, dh, cc], S0[:, dh, :], dh == 0, False, after=[*s_tok, *state["b6"]])
                tok = mm(o, aTr, BY[:, c, 0:256], False, True, after=[a], sig=True)
                state["a"] = [tok]
                state["b5"] = [a]
                if c < 7:
                    for dh in range(2):
                        u = mm(bank(7)[:, dh * 256:(dh + 1) * 256], BX[:, c, 256 + dh * 128:256 + (dh + 1) * 128],
                               BY[:, c, 0:256], True, True, after=[kd, *s_tok], sig=(dh == 1))
                yield
                oe = ts(dve, BX[:, c, 0:256], o, rc[:, h:h + 1], None, ALU.mult, after=[tok])
                state["b6"] = [oe]
                if c < 7:
                    a = stt(S1, S0, gam[h] ** 128, bank(7).rearrange("p (d e) -> p d e", d=2), ALU.mult, ALU.add, after=[u])
                    s_tok = [a]
                yield
            state["qk"] = [pe.last()]
            pe_done = pe.last()
            O = BX[:, :, 0:256]
            e = BX[:, :, 256:512]
            tt(dve, e, O, O, ALU.mult, after=[pe_done])
            a = red(ss[:, h % 2 * 8:h % 2 * 8 + 8], e, ALU.add)
            r = rsqrt((h % 2 * 8, h % 2 * 8 + 8), 256, after=[a])
            yield
            tt(dve, O, O, rs[:, h % 2 * 8:h % 2 * 8 + 8].unsqueeze(2).to_broadcast([128, 8, 256]), ALU.mult, after=[r])
            a = tt(dve, O, O, grow.unsqueeze(1).to_broadcast([128, 8, 256]), ALU.mult, after=[gr])
            state["grow"] = [a]
            a = tt(dve, O, O, BY[:, :, 256:512], ALU.mult, after=[sz])
            w = dma(pool, c_ob, ob_d.rearrange("(t p) c -> p t c", p=128)[:, :, h * 256:(h + 1) * 256], O, after=[a])
            tm_free[bx] = [w, pe_done, a]
            tm_free[by] = [pe_done, a]
            done[("ret", h)] = True

        for h in range(4):
            bx, by = 2 * h % 3, (2 * h + 1) % 3
            while h >= 2 and not done.get(("ret", h - 2)):
                pump(True)
            token_groups(plain_consume(bx), lambda t: [])
            while h and not done.get(("ret", h - 1)):
                pump(True)
            token_groups(plain_consume(by), lambda t: [])
            spawn(ret_side(h, bx, by, [act.last()]))
        sgf = [list(x) + tm_free[2] for x in sgf]
        merge_gate(1)
        drain()

        area = Area(base)
        mark = fence()
        use_banks(list(range(8)), mark)
        ring = [area.take(1024) for _ in range(4)]
        sgt = [area.take(512) for _ in range(4)]
        ot = [area.take(512) for _ in range(4)]
        c_st = [slot(f"c_st{i}") for i in range(4)]
        c_ot = [slot(f"c_ot{i}") for i in range(4)]
        ring_free = [list(mark) for _ in range(4)]
        nring[0] = 0
        c_ring[:] = [slot(f"c_ringb{i}") for i in range(4)]
        sg_free = [list(mark) for _ in range(4)]
        ot_free = [list(mark) for _ in range(4)]
        n_g = [0]

        def merged(t):
            return TM[:, t // 4, (t % 4) * 1024:(t % 4 + 1) * 1024]

        def feed_small(src):
            i = n_g[0] % 4
            n_g[0] += 1
            tok = dma(pool, c_st[i], sgt[i], src, after=sg_free[i])
            return sgt[i], tok, i

        fed = {}

        def restage(get, src, cb):
            def hook(t):
                for n in ((0, 1) if t == 0 else (t + 1,)):
                    if n < 8:
                        fed[n] = feed_small(src[n * 128:(n + 1) * 128, cb * 512:(cb + 1) * 512])
                if get is None:
                    return [ht[t]]
                if t:
                    get(t - 1)
                return []
            return hook

        def stage(src_d):
            ahead = {}

            def get(t):
                for n in range(t, min(8, t + 3)):
                    if n not in ahead:
                        ahead[n] = feed(src_d[n * 128:(n + 1) * 128, :])
                buf, tok, i = ahead[t]
                ht[t] = to_stationary(t, buf, [tok, *mark])
                ring_free[i] = [pe.last()]
            return get

        def branch_consume(g, cb):
            def f(t, ps, tok):
                s, st, i = fed.pop(t)
                m = merged(t)[:, cb * 512:(cb + 1) * 512]
                st = af(s, s, ACT.Sigmoid, after=[st])
                if g == 0:
                    a = b = tt(dve, m, ps, s, ALU.mult, after=[tok, st, *mark])
                else:
                    a = tt(dve, s, ps, s, ALU.mult, after=[tok, st])
                    b = tt(dve, m, m, s, ALU.add)
                sg_free[i] = [b]
                mdone[t] = b
                return [a]
            return f

        mdone = {}
        ga, gb = stage(oa_d), stage(ob_d)
        for t in range(8):
            ga(t)
        token_groups(branch_consume(0, 0), restage(None, sig_d[0], 0))
        token_groups(branch_consume(0, 1), restage(gb, sig_d[0], 1))
        gb(7)
        token_groups(branch_consume(1, 0), restage(None, sig_d[1], 0))

        def gm(t):
            ht[t] = to_stationary(t, merged(t), [mdone[t]])

        token_groups(branch_consume(1, 1), restage(gm, sig_d[1], 1))
        gm(7)

        def final_consume(cb):
            def f(t, ps, tok):
                s, st, i = fed.pop(t)
                o = ot[n_o[0] % 4]
                j = n_o[0] % 4
                n_o[0] += 1
                a = tt(dve, o, ps, s, ALU.add, after=[tok, st, *ot_free[j]])
                sg_free[i] = [a]
                w = dma(pool, c_ot[j], out[t * 128:(t + 1) * 128, cb * 512:(cb + 1) * 512], o, after=[a])
                ot_free[j] = [w]
                return [a]
            return f

        n_o = [0]
        token_groups(final_consume(0), restage(None, x1_d, 0))
        token_groups(final_consume(1), restage(None, x1_d, 1))

        ends = [s.token() for s in slots]

        block = ctx.enter_context(nc.Block())

        @block.sync
        def _(eng):
            sp.play(eng)
            for sem, v in ends:
                eng.wait_ge(sem, v)

        @block.tensor
        def _(eng):
            pe.play(eng)

        @block.scalar
        def _(eng):
            act.play(eng)

        @block.vector
        def _(eng):
            dve.play(eng)

        @block.gpsimd
        def _(eng):
            pool.play(eng)


def constants():
    i = np.arange(128)
    eye = np.eye(128, dtype=np.float32)
    planes = [eye]
    for b in (2, 4, 8, 16, 32, 64):
        pair = (i[:, None] // (2 * b)) == (i[None, :] // (2 * b))
        low = pair & (i[:, None] // b % 2 == 1) & (i[None, :] // b % 2 == 0)
        planes += [low.astype(np.float32), low.T.astype(np.float32)]
    pair = (i[:, None] // 2) == (i[None, :] // 2)
    low = pair & (i[:, None] % 2 == 1) & (i[None, :] % 2 == 0)
    planes += [low.T.astype(np.float32), low.astype(np.float32)]
    planes += [(i[:, None] <= i[None, :]).astype(np.float32), (i[:, None] >= i[None, :]).astype(np.float32)]
    planes += [(i[:, None] > i[None, :]).astype(np.float32)]
    masks = np.stack(planes)
    inv = (10000.0 ** (-np.arange(0, 256, 2, dtype=np.float32) / np.float32(256))).astype(np.float32)
    ang = np.arange(1024, dtype=np.float32)[:, None] * inv[None, :]
    cs = np.stack([np.cos(ang), np.sin(ang)]).astype(np.float32)
    rm = np.zeros((4, 128, 128), np.float32)
    rc = np.zeros((128, 8), np.float32)
    for h in range(4):
        lg = np.log1p(-np.exp2(-5.0 - h))
        s, t = i[:, None], i[None, :]
        rm[h] = np.where(s // 64 <= t // 64, np.exp(lg * (np.abs(t - s) - (t + 1.0))), 0.0) / 16.0
        rc[:, h] = np.exp(lg * (i + 1.0))
        rc[:, 4 + h] = np.exp(lg * (127.0 - i)) / 16.0
    return masks, cs, rm, rc


def kernel(**inputs):
    import concourse.bacc as bacc
    from concourse.bass_utils import run_bass_kernel_spmd

    a = {k: np.asarray(v)[0] for k, v in inputs.items()}
    masks, cs, rm, rc = constants()
    pad = np.pad(a["rpb"], ((0, 0), (0, 0), (48, 48)))
    tabs = np.stack([pad[:, :, 63 - w:127 - w] for w in range(64)], axis=2)
    arrays = {
        "x": a["x"],
        "norm_w": a["norm_w"].reshape(8, 128).T,
        "w_in": a["w_in"],
        "gq": a["qk_gain_q"][:, None],
        "gk": a["qk_gain_k"][:, None],
        "rpb": tabs,
        "conv_w": a["conv_w"].reshape(5, 12, 128).transpose(2, 1, 0),
        "a_log": a["a_log"].reshape(1, 8),
        "dt_bias": a["dt_bias"].reshape(1, 8),
        "dn_w": a["dn_norm_w"][None, :],
        "w_out": a["w_out"],
        "gain2": a["norm_gain_2"].reshape(8, 128).T,
        "w_in2": a["w_in_2"],
        "b_merge": a["b_merge_2"],
        "sbq": a["sb_q_gain_2"][:, None],
        "sbk": a["sb_k_gain_2"][:, None],
        "ret_gain": a["ret_out_gain_2"],
        "w_sb": a["w_branch_sb_2"],
        "w_ret": a["w_branch_ret_2"],
        "w_out2": a["w_out_2"],
        "masks": masks, "cossin": cs, "retmask": rm, "retcol": rc,
    }
    nc = bacc.Bacc("TRN2", target_bir_lowering=False, num_devices=1)
    given, args = {}, []
    for name, v in arrays.items():
        v = np.ascontiguousarray(v)
        given[f"in_{name}"] = v
        args.append(nc.dram_tensor(f"in_{name}", v.shape, mybir.dt.from_np(v.dtype), kind="ExternalInput").ap())
    args.append(nc.dram_tensor("out_0", [1024, 1024], F32, kind="ExternalOutput").ap())
    build(nc, *args)
    r = run_bass_kernel_spmd(nc, [given], core_ids=[0])
    return np.asarray(r.results[0]["out_0"]).reshape(1, 1024, 1024)
```

```python
import numpy as np
import concourse.bass as bass
from concourse import mybir
from concourse.alu_op_type import AluOpType as ALU
from contextlib import ExitStack

F32 = mybir.dt.float32
F32R = mybir.dt.float32r
ACT = mybir.ActivationFunctionType
AX = mybir.AxisListType

EPS = 1e-6
NEG = -1.0e30


class Queue:

    def __init__(self, sem, chained, clock, tail):
        self.sem, self.chained = sem, chained
        self.clock, self.tail = clock, tail
        self.n = 0
        self.t = 0.0
        self.own = [0]
        self.seen = {}
        self.items = []

    def put(self, fn, after=(), sig=True, free=False, cost=100.0):
        waits = []
        start = max([self.t] + [self.clock.get((id(m), v), 0.0) for m, v in after])
        self.t = start + cost
        own = [(self.sem, self.own[0])] if self.chained and not free and self.own[0] else []
        for sem, v in [*after, *own]:
            if self.seen.get(id(sem), 0) < v:
                self.seen[id(sem)] = v
                waits.append((sem, v))
        self.items.append((waits, fn, sig))
        if sig:
            self.n += 1
            self.own[0] = self.n
            self.clock[(id(self.sem), self.n)] = self.t + self.tail
        if self.chained:
            self.clock["side"] = max(self.clock.get("side", 0.0), self.t + self.tail)
        return (self.sem, self.n)

    def last(self):
        return (self.sem, self.n)

    def play(self, eng):
        for waits, fn, sig in self.items:
            best = {}
            for sem, v in waits:
                if id(sem) not in best or best[id(sem)][1] < v:
                    best[id(sem)] = (sem, v)
            for sem, v in best.values():
                eng.wait_ge(sem, v)
            ins = fn(eng)
            if sig is True:
                ins.then_inc(self.sem, 1)
            elif sig:
                ins.then_inc(sig, 16)


class Slot:

    def __init__(self, sem):
        self.sem, self.n = sem, 0

    def token(self):
        return (self.sem, self.n)


def build(nc, x, norm_w, w_in, gq, gk, rpb, conv_w, a_log, dt_bias, dn_w, w_out,
          gain2, w_in2, b_merge, sbq, sbk, ret_gain, w_sb, w_ret, w_out2,
          masks, cossin, retmask, retcol, out):
    ctx = ExitStack()
    with ctx:
        def sb(name, shape, dt=F32):
            return ctx.enter_context(nc.sbuf_tensor(name, shape, dt))

        def semaphore(name):
            return ctx.enter_context(nc.semaphore(name))

        def scratch(name, shape):
            return nc.dram_tensor(name, shape, F32, kind="Internal").ap()

        mix_d = scratch("mix_d", [1024, 1024])
        x1_d = scratch("x1_d", [1024, 1024])
        oa_d = scratch("oa_d", [1024, 1024])
        ob_d = scratch("ob_d", [1024, 1024])
        sig_d = scratch("sig_d", [2, 1024, 1024])
        dz_d = scratch("dz_d", [1024, 512])
        dnr_d = scratch("dnr_d", [4, 128, 3, 1024])

        NSLOT = 11
        WH = sb("WH", [128, NSLOT, 1024], F32R)
        NRAW = 4
        RAW = sb("RAW", [128, NRAW, 512])
        TM = sb("TM", [128, 3, 4096])
        WKW = 11184
        WK = sb("WK", [128, WKW])
        PS = ctx.enter_context(nc.psum_tensor("PS", [128, 4096], F32))
        lent = ctx.enter_context(ExitStack())
        HH = lent.enter_context(nc.sbuf_tensor("HH", [128, 8, 1024], F32R))
        HL = lent.enter_context(nc.sbuf_tensor("HL", [128, 8, 1024], F32R))

        def bank(n, w=512, o=0):
            return PS[:, n * 512 + o:n * 512 + o + w]

        clock = {}
        pe = Queue(semaphore("s_pe"), False, clock, 200.0)
        act = Queue(semaphore("s_act"), True, clock, 200.0)
        dve = Queue(semaphore("s_dve"), True, clock, 200.0)
        pool = Queue(semaphore("s_pool"), True, clock, 100.0)
        sp = Queue(semaphore("s_sp"), False, clock, 0.0)

        def width(a):
            n = 1
            for d in a.shape[1:]:
                n *= d
            return n
        slots = []

        def slot(name):
            s = Slot(semaphore(name))
            slots.append(s)
            return s

        def mm(o, l, r, start, stop, after=(), sig=False):
            passes = 2.1 if l.dtype == F32 else 1
            return pe.put(lambda e: e.matmul(o, l, r, start=start, stop=stop), after, sig,
                          cost=passes * max(64, width(r)) / 2.4)

        def tr(o, i, after=(), sig=False):
            p = i.shape[0]
            b = i.base_partition() if callable(i.base_partition) else i.base_partition
            idn = ident[b:b + p, b:b + p] if p < 128 else ident
            return pe.put(lambda e: e.transpose(o, i, idn), after, sig, cost=60)

        def af(o, i, func, after=(), par=False, **kw):
            return act.put(lambda e: e.activation(o, i, func, **kw), after, free=par, cost=70 + 0.83 * width(o))

        def tt(q, o, a, b, op, after=()):
            c = 150 + 160 * width(o) if op == ALU.pow else 70 + (1.04 if q is dve else 2.4) * width(o)
            return q.put(lambda e: e.tensor_tensor(o, a, b, op), after, cost=c)

        def ts(q, o, a, s1, s2, op0, op1=None, after=(), par=False):
            c = 70 + (1.04 if q is dve else 5.0) * width(o)
            if op1 is None:
                return q.put(lambda e: e.tensor_scalar(o, a, s1, None, op0), after, free=par, cost=c)
            return q.put(lambda e: e.tensor_scalar(o, a, s1, s2, op0, op1), after, free=par, cost=c)

        def stt(o, a, s, b, op0, op1, after=()):
            return dve.put(lambda e: e.scalar_tensor_tensor(out=o, in0=a, scalar=s, in1=b, op0=op0, op1=op1), after,
                           cost=70 + 1.04 * width(o))

        def red(o, i, op, after=(), axis=AX.X):
            return dve.put(lambda e: e.tensor_reduce(o, i, axis, op), after, cost=70 + 1.04 * width(i))

        def recip(o, i, after=()):
            return dve.put(lambda e: e.reciprocal(o, i), after, cost=70 + 6.3 * width(o))

        def mset(q, o, v, after=()):
            return q.put(lambda e: e.memset(o, v), after)

        def dma(q, s, o, i, after=()):
            if q is sp:
                sp.put(lambda e: e.dma_start(o, i), after, s.sem)
                sp.n -= 1
            else:
                kept = q.own[0]
                q.put(lambda e: e.dma_start(o, i), after, s.sem, cost=1040)
                q.n -= 1
                q.own[0] = kept
            s.n += 16
            clock[(id(s.sem), s.n)] = q.t + 2000.0 + width(o) * 128 * 4 / 200.0
            return s.token()

        class Area:
            def __init__(self, at, end=WKW):
                self.at, self.end = at, end

            def take(self, n):
                a = self.at
                self.at += n
                assert self.at <= self.end, self.at
                return WK[:, a:a + n]

        keep = Area(0)
        ident = keep.take(128)
        one = keep.take(1)
        half = keep.take(1)
        nw = keep.take(8)
        nw2 = keep.take(8)
        naq, nak, sq_, sk_ = (keep.take(1) for _ in range(4))
        ss = keep.take(128)
        rs = keep.take(128)
        dummy = keep.take(2)
        base = keep.at
        tail = WK[:, WKW - 512:WKW]

        c_x = [slot(f"c_x{i}") for i in range(8)]

        def x_load(t):
            dma(sp, c_x[t], TM[:, 1 + t // 4, (t % 4) * 1024:(t % 4 + 1) * 1024], x[t * 128:(t + 1) * 128, :])

        c_const = slot("c_const")
        c_const2 = slot("c_const2")
        x_load(0)
        dma(sp, c_const, ident, masks[0])
        dma(sp, c_const, nw, norm_w)
        dma(pool, c_const2, nw2, gain2)
        for b in (0, 64):
            dma(pool, c_const2, naq[b:b + 64, :], gq)
            dma(pool, c_const2, nak[b:b + 64, :], gk)
        dma(pool, c_const2, sq_, sbq)
        dma(pool, c_const2, sk_, sbk)
        t_const, t_const2 = c_const.token(), c_const2.token()
        mset(dve, one, 1.0)
        t_one = mset(dve, half, -0.5)

        def rsqrt(cols, n, after=()):
            a, r = ss[:, cols[0]:cols[1]], rs[:, cols[0]:cols[1]]
            ts(pool, a, a, 1.0 / n, EPS, ALU.mult, ALU.add, after=[*after, t_one])
            return tt(pool, r, a, half.to_broadcast([128, cols[1] - cols[0]]), ALU.pow)

        def seg(w, k):
            return w[k * 128:(k + 1) * 128, :]

        blocks = []
        w_segs = w_in[:, 0:4096].rearrange("r (s c) -> r s c", c=512)
        w2_segs = w_in2.rearrange("r (s c) -> r s c", c=1024)

        def add_block(width, src, gain=None):
            blocks.append((width, src, gain))

        na_order = ["na0", "na1", "dn0", "na2", "dn1", "dn2", "na3", "dn3", "dz"]
        for b in na_order:
            n = int(b[-1]) if b[-1].isdigit() else 0
            if b == "dz":
                add_block(512, lambda k: w_segs[k * 128:(k + 1) * 128, 7, :], nw)
            elif b[:2] == "na":
                add_block(512, lambda k, p=n: w_segs[k * 128:(k + 1) * 128, 0:4, p * 128:(p + 1) * 128], nw)
            elif b == "dn0":
                add_block(400, lambda k: (w_segs[k * 128:(k + 1) * 128, 4:7, 0:128],
                                          w_in[k * 128:(k + 1) * 128, 4096:4112]), nw)
            else:
                add_block(384, lambda k, h=n: w_segs[k * 128:(k + 1) * 128, 4:7, h * 128:(h + 1) * 128], nw)
        for cb in range(2):
            add_block(512, lambda k, cb=cb: w_out[k * 128:(k + 1) * 128, cb * 512:(cb + 1) * 512])
        sb_order = [0, 1, 2, (0, 0), 3, 4, 5, 6, (0, 1), 7]
        for h in sb_order:
            if isinstance(h, int):
                add_block(512, lambda k, h=h: w2_segs[k * 128:(k + 1) * 128, 0:4, h * 128:(h + 1) * 128], nw2)
            else:
                add_block(512, lambda k, g=h: w2_segs[k * 128:(k + 1) * 128, 8 + g[0], g[1] * 512:(g[1] + 1) * 512], nw2)
        ret_order = [(0, 4), (0, 6), (1, 4), "m0", (1, 6), (2, 4), (2, 6), (3, 4), (3, 6), "m1"]
        for b in ret_order:
            if isinstance(b, str):
                add_block(512, lambda k, c=512 * int(b[1]): w2_segs[k * 128:(k + 1) * 128, 9, c:c + 512], nw2)
            else:
                add_block(512, lambda k, h=b[0], s=b[1]: w2_segs[k * 128:(k + 1) * 128, s:s + 2, h * 256:(h + 1) * 256], nw2)
        for w in (w_sb, w_ret, w_out2):
            for cb in range(2):
                add_block(512, lambda k, w=w, cb=cb: w[k * 128:(k + 1) * 128, cb * 512:(cb + 1) * 512])

        tiles = [(b, k) for b in range(len(blocks)) for k in range(8)]
        c_raw = [slot(f"c_raw{i}") for i in range(NRAW)]
        raw_free = [[] for _ in range(NRAW)]
        wh_free = [[] for _ in range(NSLOT)]
        ready = {}
        arrival = {}
        prepped = [0]
        loaded = [0]

        def load_next():
            n = loaded[0]
            if n >= len(tiles):
                return
            b, k = tiles[n]
            width, src, _ = blocks[b]
            s = src(k)
            at = 0
            for s in s if isinstance(s, tuple) else (s,):
                w = s.shape[1] if len(s.shape) == 2 else s.shape[1] * s.shape[2]
                d = RAW[:, n % NRAW, at:at + w]
                if len(s.shape) == 3:
                    d = d.rearrange("p (s c) -> p s c", c=s.shape[2])
                dma(sp, c_raw[n % NRAW], d, s, after=raw_free[n % NRAW])
                at += w
            arrival[n] = c_raw[n % NRAW].token()
            loaded[0] += 1

        def prep_next():
            n = prepped[0]
            if n >= len(tiles):
                return
            b, k = tiles[n]
            width, _, gain = blocks[b]
            r, w = RAW[:, n % NRAW, 0:width], WH[:, n % NSLOT, :]
            after = [arrival[n], t_const2 if gain is nw2 else t_const, *wh_free[n % NSLOT]]
            if gain is None:
                hi = af(w[:, 0:width], r, ACT.Copy, after=after, par=True)
                lo = tt(dve, w[:, 512:512 + width], r, w[:, 0:width].bitcast(F32), ALU.subtract, after=[hi])
            else:
                g = gain[:, k:k + 1]
                hi = af(w[:, 0:width], r, ACT.Copy, after=after, par=True, scale=g)
                lo = stt(w[:, 512:512 + width], r, g, w[:, 0:width].bitcast(F32), ALU.mult, ALU.subtract, after=[hi])
            ready[n] = lo
            raw_free[n % NRAW] = [lo]
            prepped[0] += 1
            load_next()

        for _ in range(NRAW):
            load_next()
        x_load(1)

        side = []

        class Stream:
            def __init__(self, gen):
                self.gen, self.wake = gen, 0.0
                self.own = [[q.n] for q in (act, dve, pool)]

            def step(self):
                ran = False
                main = [q.own for q in (act, dve, pool)]
                act.own, dve.own, pool.own = self.own
                while self.wake <= pe.t:
                    clock["side"] = 0.0
                    try:
                        said = next(self.gen)
                    except StopIteration:
                        side.remove(self)
                        ran = True
                        break
                    if said == "idle":
                        break
                    if said == "next":
                        ran = True
                        continue
                    ran = True
                    self.wake = clock["side"] if said is None else clock[(id(said[0]), said[1])]
                act.own, dve.own, pool.own = main
                return ran

        def spawn(g):
            side.append(Stream(g))

        def pump(idle=False):
            ran = [s.step() for s in sorted(side, key=lambda s: s.wake)]
            if idle and not any(ran):
                later = [s.wake for s in side if s.wake > pe.t]
                assert later, "streams wait for each other"
                pe.t = min(later)

        def drain():
            while side:
                pump(True)

        def fence(but=()):
            marks = [q.last() for q in (pe, act, dve, pool)] + [
                s.token() for s in slots if s.n and s not in c_raw and s not in but]
            marks = [m for m in marks if m[1]]
            return marks

        cur = [0]
        mb = [0]
        mfree = [[] for _ in range(8)]
        ring_banks = list(range(8))

        open_bank = [None]

        def next_bank():
            mb[0] += 1
            if ring_banks[mb[0] % len(ring_banks)] == open_bank[0]:
                mb[0] += 1
            return ring_banks[mb[0] % len(ring_banks)]

        def use_banks(banks, after=()):
            for b in banks:
                if b not in ring_banks:
                    mfree[b] = list(after)
            ring_banks[:] = banks

        def token_groups(consume, after_tile, width=512):
            b = cur[0]
            cur[0] += 1
            assert blocks[b][0] == width
            while prepped[0] < 8 * b + 8:
                prep_next()
            for t in range(8):
                tile_tokens = after_tile(t)
                open_bank[0] = m = next_bank()
                ps = bank(m, width)
                for k in range(8):
                    n = 8 * b + k
                    w = WH[:, n % NSLOT, :]
                    aft = [ready[n]]
                    if k == 0:
                        aft += mfree[m] + tile_tokens
                    hh, hl = HH[:, k, t * 128:(t + 1) * 128], HL[:, k, t * 128:(t + 1) * 128]
                    mm(ps, hh, w[:, 0:width], k == 0, False, after=aft)
                    mm(ps, hh, w[:, 512:512 + width], False, False)
                    tok = mm(ps, hl, w[:, 0:width], False, k == 7, sig=(k == 7 or t == 7))
                    if t == 7:
                        wh_free[n % NSLOT] = [tok]
                        prep_next() if prepped[0] < 8 * b + 16 and prepped[0] - NSLOT < 8 * b + k + 1 else None
                    pump()
                mfree[m] = consume(t, ps, tok)
                open_bank[0] = None
                if t < 7 and prepped[0] < 8 * b + 8 + NSLOT - 8:
                    prep_next()

        def channel_groups(consume, extra=0):
            b = cur[0]
            cur[0] += 1
            while prepped[0] < 8 * b + 8:
                prep_next()
            parts = [(c, c * 128, 128) for c in range(3)] + ([(3, 384, extra)] if extra else [])
            groups = [(*p, th) for p in parts for th in range(2)]
            for g, (c, at, n_c, th) in enumerate(groups):
                end = g == len(groups) - 1
                open_bank[0] = m = next_bank()
                ps = bank(m)[0:n_c, :]
                for k in range(8):
                    n = 8 * b + k
                    w = WH[:, n % NSLOT, :]
                    wh, wl = w[:, at:at + n_c], w[:, 512 + at:512 + at + n_c]
                    hh, hl = HH[:, k, th * 512:(th + 1) * 512], HL[:, k, th * 512:(th + 1) * 512]
                    aft = [ready[n]]
                    if k == 0:
                        aft += mfree[m]
                    mm(ps, wh, hh, k == 0, False, after=aft)
                    mm(ps, wh, hl, False, False)
                    tok = mm(ps, wl, hh, False, k == 7, sig=(k == 7 or end))
                    if end:
                        wh_free[n % NSLOT] = [tok]
                        prep_next() if prepped[0] < 8 * b + 16 and prepped[0] - NSLOT < 8 * b + k + 1 else None
                    pump()
                mfree[m] = consume(c, th, ps, tok)
                open_bank[0] = None
                if not end and prepped[0] < 8 * b + 8 + NSLOT - 8:
                    prep_next()

        def to_stationary(t, src, after):
            dst = slice(t * 128, (t + 1) * 128)
            for half_ in range(2):
                m = next_bank()
                ps = bank(m)
                for j in range(4):
                    k = half_ * 4 + j
                    tok = tr(ps[:, j * 128:(j + 1) * 128], src[:, k * 128:(k + 1) * 128],
                             after=[*after, *mfree[m], t_const], sig=(j == 3))
                hh, hl = HH[:, half_ * 4:half_ * 4 + 4, dst], HL[:, half_ * 4:half_ * 4 + 4, dst]
                p4 = ps.rearrange("p (k c) -> p k c", c=128)
                hi = af(hh, p4, ACT.Copy, after=[tok], par=True)
                lo = tt(dve, hl, p4, hh.bitcast(F32), ALU.subtract, after=[hi])
                mfree[m] = [lo]
            ht[t] = lo
            return lo

        def staged(t):
            while t not in ht:
                pump(True)
            return [ht[t]]

        act.put(lambda e: e.preload_act_table_set("natural_log_exp_and_others"), sig=False)

        ht = {}
        tm_free = [[] for _ in range(3)]
        use_banks(list(range(6)))

        def norm_in():
            for t in range(8):
                X = TM[:, 1 + t // 4, (t % 4) * 1024:(t % 4 + 1) * 1024]
                s = af(PS[:, 3072:4096], X, ACT.Square, after=[c_x[t].token()], accum_out=ss[:, 112 + t:113 + t])
                r = rsqrt((112 + t, 113 + t), 1024, after=[s])
                a = ts(dve, X, X, rs[:, 112 + t:113 + t], None, ALU.mult, after=[r])
                yield
                tm_free[1] = tm_free[2] = [to_stationary(t, X, [a])]
                yield "next"

        spawn(norm_in())
        for i_ in range(8):
            pe.t += 1000.0
            pump()
            prep_next()
            if i_ >= 3:
                x_load(i_ - 1)
        x_load(7)

        ts(dve, naq, naq, 0.125, None, ALU.mult, after=[t_const2])
        t_gain = ts(dve, sq_, sq_, 128.0 ** -0.5, None, ALU.mult)

        DNFIX = WKW - 512 - 1036
        area = Area(DNFIX, WKW - 512)
        tri = area.take(256).rearrange("p (d c) -> p d c", d=2)
        onesq = area.take(128)
        dnw = area.take(128)
        cw = area.take(60).rearrange("p (g j) -> p g j", j=5)
        cst = area.take(16)
        G, g_, beta, kdf, eGL, bg = (area.take(64) for _ in range(6))
        gtmp = area.take(64)
        c_dn = slot("c_dn")
        mset(dve, onesq, 1.0)
        t_dn = (c_dn.sem, 5 * 16)

        area = Area(base, WKW - 512)
        tab = [area.take(23 * 64).rearrange("p (j c) -> p j c", c=64) for _ in range(2)]
        qT = area.take(1024)
        kT = area.take(1024)
        S = [area.take(576) for _ in range(2)]
        PT = [area.take(640) for _ in range(2)]
        nm = area.take(2)
        sums = area.take(2)
        rinv = area.take(2)
        sqt = area.take(256)
        stg = [area.take(512) for _ in range(3)]
        assert area.at <= DNFIX
        c_tab = [slot("c_tab0"), slot("c_tab1")]
        c_mix = [slot(f"c_mix{i}") for i in range(3)]
        w_start = []
        tab_free = [[], []]

        def load_table(h):
            T = tab[h % 2]
            tok = None
            for ro in range(2):
                src = rpb[h, 1 - ro:15 - ro, :, :].rearrange("j w c -> w j c")
                tok = dma(pool, c_tab[h % 2], T[ro * 64:(ro + 1) * 64, 0:14, :], src, after=tab_free[h % 2])
            for ro in range(2):
                Fh = T[ro * 64:(ro + 1) * 64, 0:14, :]
                a = pool.put(lambda e, Fh=Fh: e.affine_select(
                    out=Fh[:, :, 0:48], in_=Fh[:, :, 0:48], pattern=[[0, 14], [1, 48]], compare_op=ALU.is_ge,
                    fill=NEG, base=8, channel_multiplier=-1), [tok], cost=830)
                a = pool.put(lambda e, Fh=Fh: e.affine_select(
                    out=Fh[:, :, 16:64], in_=Fh[:, :, 16:64], pattern=[[0, 14], [-1, 48]], compare_op=ALU.is_ge,
                    fill=NEG, base=7 - 16, channel_multiplier=1), cost=830)
            a = pool.put(lambda e: e.tensor_copy(T[:, 14:23, :], T[:, 2:11, :]), cost=2040)
            a = mset(pool, T[64:128, 14, :], NEG)
            a = mset(pool, T[0:64, 22, :], NEG)
            return a

        def transposed(dst, src, gain, after, bk, free):
            for g in range(2):
                for j in range(4):
                    tok = tr(bank(bk)[:, j * 128:(j + 1) * 128], src(g * 4 + j), after=[*after, *free], sig=(j == 3))
                if gain is None:
                    free = [af(dst[:, g * 512:(g + 1) * 512], bank(bk), ACT.Copy, after=[tok])]
                else:
                    free = [af(dst[:, g * 512:(g + 1) * 512], bank(bk), ACT.Copy, after=[tok, t_gain], scale=gain)]
                yield free

        def exp_ln_set():
            act.put(lambda e: e.preload_act_table_set("natural_log_exp_and_others"), sig=False, cost=1300)

        def silu_in_place(z, e, after=()):
            a = af(z, z, ACT.Silu, after=after)
            if e:
                exp_ln_set()
            return a

        state = {"pe_na": [[], []], "table": {}}
        done = {}

        def na_side(p, buf, ev):
            B = TM[:, buf, :].rearrange("p (t c) -> p t c", c=512)
            qk = B[:, :, 0:256].rearrange("p t (g d) -> p t g d", d=64)
            c0 = (p % 3) * 32
            r = rsqrt((c0, c0 + 32), 64, after=[ev])
            sc = rs[:, c0:c0 + 32].rearrange("p (t g) -> p t g", g=4)
            for t in range(8):
                a = tt(dve, qk[:, t], qk[:, t], sc[:, t].unsqueeze(2).to_broadcast([128, 4, 64]), ALU.mult, after=[r])
            yield
            while p and not (done.get(("na", p - 1, 0)) and done.get(("na", p - 1, 1))):
                yield "idle"
            free = [*state.get("pt_free0", []), *state["pe_na"][0], *state["pe_na"][1]]
            for dst, o, g in ((qT, 0, naq), (kT, 128, nak)):
                for f in transposed(dst, lambda t, o=o: B[:, t, o:o + 128], g, [a, *w_start], 4, free):
                    free = f
                    yield
            state["pt_free0"] = free
            sz = silu_in_place(B[:, :, 384:512], True, after=[pe.last()])
            state[("qk", p)] = [free[0], sz]
            done[("naqk", p)] = True

        def na_head(p, buf, h):
            B = TM[:, buf, :].rearrange("p (t c) -> p t c", c=512)
            while not done.get(("naqk", p)):
                yield "idle"
            qk_tok, sz = state[("qk", p)]
            hd = 2 * p + h
            tok_tab = state["table"][hd]
            yield tok_tab
            T = tab[h]
            P = slice(h * 64, h * 64 + 64)
            Sb, Pb = S[h], PT[h]
            c0 = (2 + 3 * h) * 512
            ptb = 4 + 3 * h

            def key(n):
                return n + str(h)

            for i in range(8):
                inner = 2 <= i <= 5
                k0 = i - 2 if inner else (0 if i < 2 else 4)
                nk = 576 if inner else 512
                q = qT[P, i * 128:(i + 1) * 128]
                tok = mm(PS[:, c0:c0 + 512], q, kT[P, k0 * 128:k0 * 128 + 512], True, True,
                         after=[qk_tok, *state.get(key("s_free"), [])], sig=True)
                if inner:
                    tok = mm(PS[:, c0 + 512:c0 + 576], q, kT[P, k0 * 128 + 512:k0 * 128 + 576], True, True, sig=True)
                j0 = 14 if inner else 2 * k0 - 2 * i + 7 - 1
                tb = T[:, j0:j0 + nk // 64, :].rearrange("p j c -> p (j c)")
                b = dve.put(lambda e, Sb=Sb, nk=nk, tb=tb, c0=c0: e.tensor_tensor_reduce(
                    out=Sb[:, 0:nk], in0=PS[:, c0:c0 + nk], in1=tb, scale=-1.0, scalar=3.0e38, op0=ALU.add,
                    op1=ALU.min, accum_out=nm[:, h:h + 1]), [tok, tok_tab, *state.get(key("s"), []), *state.get(key("e"), [])],
                    cost=70 + 1.04 * nk)
                if i == 7:
                    tab_free[h] = [b]
                ex = af(Sb[:, 0:nk], Sb[:, 0:nk], ACT.Exp, after=[b], bias=nm[:, h:h + 1], scale=-1.0,
                        accum_out=sums[:, h:h + 1])
                state[key("e")] = [ex]
                yield
                for j in range(4):
                    tok = tr(bank(ptb)[:, j * 128:(j + 1) * 128], Sb[:, j * 128:(j + 1) * 128],
                             after=[ex, b, *state.get("pt_free" + str(h), [])], sig=(j == 3))
                if inner:
                    tok = tr(PS[0:64, c0 + 640:c0 + 768], Sb[:, 512:576], sig=True)
                state[key("s")] = [tok]
                c = af(Pb[:, 0:512], bank(ptb), ACT.Copy, after=[tok, *state.get(key("pt"), [])])
                state["pt_free" + str(h)] = [c]
                if inner:
                    c = af(Pb[0:64, 512:640], PS[0:64, c0 + 640:c0 + 768], ACT.Copy, par=True)
                yield
                V = B[:, :, 256 + h * 64:256 + h * 64 + 64]
                O = PS[:, c0 + 896:c0 + 960]
                for j in range(4):
                    tok = mm(O, Pb[:, j * 128:(j + 1) * 128], V[:, k0 + j, :], j == 0, (j == 3) and not inner,
                             after=[c, b], sig=(j == 3))
                if inner:
                    tok = mm(O, Pb[0:64, 512:640], V[0:64, k0 + 4, :], False, True, sig=True)
                state[key("pt")] = [tok]
                recip(rinv[:, h:h + 1], sums[:, h:h + 1], after=[ex])
                o = stt(B[:, i, 128 + h * 64:128 + h * 64 + 64], O, rinv[:, h:h + 1],
                        B[:, i, 384 + h * 64:384 + h * 64 + 64], ALU.mult, ALU.mult, after=[tok, sz])
                state[key("s_free")] = [o]
                yield
            if hd + 2 < 8:
                state["table"][hd + 2] = load_table(hd + 2)
            state["pe_na"][h] = [pe.last(), o]
            done[("na", p, h)] = True
            if done.get(("na", p, 1 - h)):
                w = dma(pool, c_mix[buf], mix_d.rearrange("(t p) c -> p t c", p=128)[:, :, p * 128:(p + 1) * 128],
                        B[:, :, 128:256], after=[o])
                tm_free[buf] = [w, pe.last(), o]
                done[("naw", p)] = True

        def na_consume(buf, p):
            B = TM[:, buf, :].rearrange("p (t c) -> p t c", c=512)

            def f(t, ps, tok):
                a = af(B[:, t, :], ps, ACT.Copy, after=[tok, *tm_free[buf]])
                q = B[:, t, 0:256]
                tt(dve, sqt, q, q, ALU.mult, after=[a, *w_start])
                c0 = (p % 3) * 32 + t * 4
                red(ss[:, c0:c0 + 4], sqt.rearrange("p (g d) -> p g d", d=64), ALU.add)
                return [a]
            return f

        c_stg = [slot(f"c_stg{i}") for i in range(3)]
        stg_free = [list(w_start) for _ in range(3)]
        n_stg = [0]
        spilled = {}

        def spill(ps, tok, dst, name):
            i = n_stg[0] % 3
            n_stg[0] += 1
            a = af(stg[i], ps, ACT.Copy, after=[tok, *stg_free[i]])
            w = dma(pool, c_stg[i], dst, stg[i], after=[a])
            stg_free[i] = [w]
            spilled.setdefault(name, []).append(w)
            return [a]

        def gates_side(tok):
            gv = gt_in.rearrange("p t (d k h) -> p d k h t", d=2, k=2)

            def col(a, d):
                return a[:, d * 32:(d + 1) * 32].rearrange("p (h t) -> p h t", t=8)

            for d in range(2):
                a = af(col(beta, d), gv[:, d, 0], ACT.Exp, scale=-1.0, after=[tok])
            al = af(cst[:, 0:8], cst[:, 0:8], ACT.Exp, after=[t_dn])
            yield
            ts(dve, beta, beta, 1.0, None, ALU.add, after=[a])
            recip(beta, beta)
            for d in range(2):
                db = cst[:, 8 + 4 * d:12 + 4 * d].unsqueeze(2).to_broadcast([128, 4, 8])
                a = tt(dve, col(g_, d), gv[:, d, 1], db, ALU.add, after=[t_dn, al, tok])
            yield
            a = af(gtmp, g_, ACT.Abs, after=[a])
            a = af(gtmp, gtmp, ACT.Exp, scale=-1.0)
            a = af(gtmp, gtmp, ACT.Ln, bias=1.0)
            yield
            stt(g_, g_, 0.0, gtmp, ALU.max, ALU.add, after=[a])
            for d in range(2):
                ab = cst[:, 4 * d:4 * d + 4].unsqueeze(2).to_broadcast([128, 4, 8])
                tt(dve, col(g_, d), col(g_, d), ab, ALU.mult)
            gg = ts(dve, g_, g_, -1.0, None, ALU.mult)
            yield
            m = next_bank()
            ps = bank(m)
            for d in range(2):
                mm(ps[:, 32 * d:32 * d + 32], tri[:, d, :], g_[:, 32 * d:32 * d + 32], True, True,
                   after=[gg, t_dn, *mfree[m]])
            tok = mm(ps[:, 64:128], onesq, g_, True, True, sig=True)
            a = af(G, ps[:, 0:64], ACT.Copy, after=[tok])
            a = af(bg, G, ACT.Exp)
            b = af(eGL, ps[:, 64:128], ACT.Exp)
            c = tt(dve, kdf, ps[:, 64:128], G, ALU.subtract, after=[b])
            mfree[m] = [b, c]
            yield
            tt(dve, bg, bg, beta, ALU.mult)
            b = af(kdf, kdf, ACT.Exp, after=[c])
            t_gates[:] = [b, dve.last()]

        t_gates = []
        gt_in = tail[:, 0:128].rearrange("p (t c) -> p t c", c=16)

        def gates_in(th, ps, tok):
            i = n_stg[0] % 3
            n_stg[0] += 1
            G16 = stg[i][0:16, :]
            a = af(G16, ps, ACT.Copy, after=[tok, *stg_free[i]])
            late_gates.append((th, i, G16, a))
            return [a]

        late_gates = []

        def gates_turned():
            for th, i, G16, a in late_gates:
                m = next_bank()
                for j in range(4):
                    tok = tr(bank(m)[:, j * 16:(j + 1) * 16], G16[:, j * 128:(j + 1) * 128], after=[a, *mfree[m]],
                             sig=(j == 3))
                b = af(gt_in[:, th * 4:th * 4 + 4, :], bank(m, 64).rearrange("p (t c) -> p t c", c=16), ACT.Copy, after=[tok])
                mfree[m] = [b]
                stg_free[i] = [tok]
            yield from gates_side(b)

        OB = [1, 0, 2, 1]
        c_r = [slot("c_r0"), slot("c_r1")]
        dn_st = {}

        def transposed_ring(dst, src, after):
            for g in range(2):
                m = next_bank()
                for j in range(4):
                    tok = tr(bank(m)[:, j * 128:(j + 1) * 128], src(g * 4 + j), after=[*after, *mfree[m]], sig=(j == 3))
                a = af(dst[:, g * 512:(g + 1) * 512], bank(m), ACT.Copy, after=[tok])
                mfree[m] = [a]
                yield a

        def load_raw(h, RB, after):
            R = RB.rearrange("p (g t) -> p g t", t=1028)
            mset(pool, R[:, :, 0:2], 0.0, after=after)
            pad = mset(pool, R[:, :, 1026:1028], 0.0)
            return [pad, dma(pool, c_r[h % 2], R[:, :, 2:1026], dnr_d[h], after=[*after, *spilled[("dn", h)]])]

        def dn_prepare(h, RB, raw, after):
            ob = OB[h]
            R = RB.rearrange("p (g t) -> p g t", t=1028)
            C = TM[:, ob, 0:3072].rearrange("p (g t) -> p g t", t=1024)
            yield raw[1]
            for c in range(3):
                w = cw[:, c * 4 + h, :]
                a = af(C[:, c, :], R[:, c, 0:1024], ACT.Copy, after=[*raw, t_dn, *after], scale=w[:, 0:1])
                for j in range(1, 5):
                    a = stt(C[:, c, :], R[:, c, j:j + 1024], w[:, j:j + 1], C[:, c, :], ALU.mult, ALU.add, after=[a])
                    yield
            s = silu_in_place(C, True, after=[a])
            yield
            qt = RB[:, 0:1024].rearrange("p (t c) -> p t c", c=128)
            kt0 = RB[:, 1024:2048].rearrange("p (t c) -> p t c", c=128)
            e = RB[:, 2048:3072].rearrange("p (t c) -> p t c", c=128)
            kt = TM[:, ob, 2048:3072].rearrange("p (t c) -> p t c", c=128)
            vt = TM[:, ob, 3072:4096].rearrange("p (t c) -> p t c", c=128)
            for c, dst in ((0, qt), (1, kt0), (2, vt)):
                for f in transposed_ring(dst.rearrange("p t c -> p (t c)"), lambda t, c=c: C[:, c, t * 128:(t + 1) * 128], [s]):
                    yield
            for n, src in ((0, qt), (1, kt0)):
                b = af(e, src, ACT.Square, after=[dve.last()])
                yield
                a = red(ss[:, 96 + n * 8:104 + n * 8], e, ALU.add, after=[b])
                yield
            a = rsqrt((96, 112), 1.0, after=[a])
            yield
            a = ts(dve, rs[:, 96:104], rs[:, 96:104], 128.0 ** -0.5, None, ALU.mult, after=[a])
            a = tt(dve, qt, qt, rs[:, 96:104].unsqueeze(2).to_broadcast([128, 8, 128]), ALU.mult)
            a = tt(dve, kt, kt0, rs[:, 104:112].unsqueeze(2).to_broadcast([128, 8, 128]), ALU.mult, after=[f])
            yield
            for c, src in ((0, qt), (1, kt)):
                for f in transposed_ring(C[:, c, :], lambda t, src=src: src[:, t, :], [a]):
                    yield
            dn_st[("in", h)] = [f, a]
            done[("prep", h)] = True

        def prepare_first():
            while not done.get(("naw", 1)) or not done.get(("naw", 2)):
                yield "idle"
            RB = TM[:, 2, 0:3084]
            raw = load_raw(0, RB, tm_free[2])
            yield
            yield from dn_prepare(0, RB, raw, tm_free[1])

        def first_tile_hook(t):
            tok = staged(t)
            if 7 in ht and not state["table"]:
                state["table"][0] = load_table(0)
                state["table"][1] = load_table(1)
                dma(pool, c_dn, tri, masks[15:17].rearrange("m p c -> p m c"))
                dma(pool, c_dn, dnw, dn_w.to_broadcast([128, 128]))
                dma(pool, c_dn, cw, conv_w)
                dma(pool, c_dn, cst[:, 0:8], a_log.to_broadcast([128, 8]))
                dma(pool, c_dn, cst[:, 8:16], dt_bias.to_broadcast([128, 8]))
            return tok

        for b in na_order:
            n = int(b[-1]) if b[-1].isdigit() else 0
            if b == "dz":
                token_groups(lambda t, ps, tok: spill(ps, tok, dz_d[t * 128:(t + 1) * 128, :], "dz"), lambda t: [])
            elif b[:2] == "dn":
                channel_groups(lambda c, th, ps, tok, h=n: gates_in(th, ps, tok) if c == 3 else spill(
                    ps, tok, dnr_d[h, :, c, th * 512:(th + 1) * 512], ("dn", h)), 0 if n else 16)
                if n == 0:
                    for _ in gates_turned():
                        pass
                    spawn(prepare_first())
            else:
                buf = n % 3
                while n == 3 and not done.get(("naw", 0)):
                    pump(True)
                token_groups(na_consume(buf, n), staged if n else first_tile_hook)
                if n == 0:
                    use_banks([0, 1])
                    for b_ in range(2, 8):
                        w_start.extend(mfree[b_])
                spawn(na_side(n, buf, dve.last()))
                spawn(na_head(n, buf, 0))
                spawn(na_head(n, buf, 1))
        drain()

        area = Area(base, DNFIX)
        late_mark = fence()
        mark = fence(c_mix)
        use_banks([2], mark)
        OAS = [area.take(1024).rearrange("p (t c) -> p t c", c=128)]
        sets = [[area.take(512) for _ in range(7)] for _ in range(2)]
        St = area.take(256).rearrange("p (d c) -> p d c", d=2)
        Vn = area.take(256).rearrange("p (d c) -> p d c", d=2)
        lent.close()
        H0 = lent.enter_context(nc.sbuf_tensor("H0", [128, 8192], F32))
        H1 = lent.enter_context(nc.sbuf_tensor("H1", [128, 8192], F32))
        RBS = [H0[:, 0:3084], H0[:, 3084:6168]]
        mk32 = H0[:, 6168:6168 + 14 * 128].rearrange("p (m c) -> p m c", c=128)
        sets.append([H1[:, i * 512:(i + 1) * 512] for i in range(7)])
        MK = H1[:, 3584:3584 + 14 * 64].bitcast(mybir.dt.bfloat16).rearrange("p (l d c) -> p l d c", l=7, d=2)
        c_mk = slot("c_mk")
        mset(dve, St, 0.0, after=mark)
        act.put(lambda e: e.activation(OAS[0][:, 0, 0:1], St[:, 0, 0:1], ACT.Copy), [*mark, dve.last()])
        dma(pool, c_mk, mk32, masks[1:15].rearrange("m p c -> p m c"), after=mark)
        dn_mark = [dve.last(), act.last()]
        dn_st["raw"] = [None, load_raw(1, RBS[1], mark)]
        dn_st["raw"][0] = load_raw(2, RBS[0], mark)
        mkt = []

        def masks_in():
            yield c_mk.token()
            mkt.append(act.put(lambda e: e.activation(MK.rearrange("p l d c -> p (l d) c"), mk32, ACT.Copy),
                               [c_mk.token()], cost=1560))

        spawn(masks_in())
        dn_st["free7"] = []
        c_dz = [slot("c_dz0"), slot("c_dz1")]
        ZT, SQ, OA2 = (H1[:, 4480 + i * 1024:5504 + i * 1024].rearrange("p (t c) -> p t c", c=128) for i in range(3))
        OAS.append(OA2)
        out_free = {1: late_mark}

        def prepare_lane():
            for h in range(1, 4):
                raw = dn_st["raw"][h % 2]
                while h == 3 and not done.get(("dn", 0)):
                    yield "idle"
                yield from dn_prepare(h, RBS[h % 2], raw, out_free[1] if h == 3 else late_mark)
                if h + 2 < 4:
                    dn_st["raw"][h % 2] = load_raw(h + 2, RBS[h % 2], [pe.last(), act.last(), dve.last()])

        def half_inverse(h, ob, j, ss_):
            before = 4 * h + j - 3
            while not done.get(("prep", h)) or (before >= 0 and not done.get(("rec", before // 4, before % 4))):
                yield "idle"
            AT, X, XT, Y, aT, E, TB = sets[ss_]
            b0, b1 = ((3, 4), (5, 6), (0, 1))[ss_]
            A, Bk = bank(b0), bank(b1)
            u4 = lambda a: a.rearrange("p (u c) -> p u c", c=128)
            d4 = lambda a: a.rearrange("p (d s c) -> p d s c", d=2, s=2)
            chunks = [2 * j, 2 * j + 1, 6 - 2 * j, 7 - 2 * j]
            cols = [d * 32 + h * 8 + c for d, c in zip((0, 0, 1, 1), chunks)]
            kT_ = TM[:, ob, 1024:2048]
            qT_ = TM[:, ob, 0:1024]
            kt = TM[:, ob, 2048:3072]
            vt = TM[:, ob, 3072:4096]
            cs = lambda a, c: a[:, c * 128:(c + 1) * 128]
            src = dn_st[("in", h)]
            fr = [*dn_st.get(("set", ss_), dn_mark), *t_gates]
            for u in range(4):
                a = af(u4(TB)[:, u, :], tri[:, u // 2, :], ACT.Copy, after=fr, par=u > 0, scale=g_[:, cols[u]:cols[u] + 1])
                b = af(u4(Y)[:, u, :], ident, ACT.Copy, par=True, scale=beta[:, cols[u]:cols[u] + 1])
            yield
            gr = mm(A, onesq, TB, True, True, after=[b, *fr], sig=True)
            br = mm(Bk, onesq, Y, True, True, sig=True)
            yield
            for u in range(4):
                a = ts(dve, u4(E)[:, u, :], u4(A)[:, u, :], G[:, cols[u]:cols[u] + 1], 0.0, ALU.subtract, ALU.min,
                       after=[gr, *fr], par=u > 0)
            e = af(E, E, ACT.Exp, after=[a])
            qe = af(TB, A, ACT.Exp)
            tri4 = tri.unsqueeze(2).to_broadcast([128, 2, 2, 128])
            yield
            e = tt(pool, d4(E), d4(E), tri4, ALU.mult, after=[e])
            beta_row = af(X, Bk, ACT.Copy, after=[br])
            yield
            for u in range(4):
                kk = mm(u4(A)[:, u, :], cs(kT_, chunks[u]), cs(kT_, chunks[u]), True, True, after=[qe, e, *src],
                        sig=(u == 3))
            for u in range(4):
                kq = mm(u4(Bk)[:, u, :], cs(kT_, chunks[u]), cs(qT_, chunks[u]), True, True, after=[beta_row],
                        sig=(u == 3))
            yield
            a = tt(dve, aT, Bk, E, ALU.mult, after=[kq, e])
            tt(dve, AT, A, E, ALU.mult, after=[kk])
            at = stt(AT, AT, -1.0, X, ALU.mult, ALU.mult, after=[beta_row])
            yield
            while not mkt:
                yield "idle"
            mk = lambda l: MK[:, l].unsqueeze(2).to_broadcast([128, 2, 2, 128])
            tt(pool, d4(XT), d4(AT), MK[:, 6].unsqueeze(2).to_broadcast([128, 2, 2, 128]), ALU.mult, after=[*mkt, at])
            a = tt(pool, u4(XT), u4(XT), ident.unsqueeze(1).to_broadcast([128, 4, 128]), ALU.add)
            am = tt(pool, d4(E), d4(AT), mk(0), ALU.mult)
            yield
            for u in range(4):
                t_ = tr(u4(A)[:, u, :], u4(XT)[:, u, :], after=[a], sig=(u == 3))
            a = xe = af(X, A, ACT.Copy, after=[t_])
            yield
            lx = []
            for l in range(6):
                for u in range(4):
                    y = mm(u4(A)[:, u, :], u4(E)[:, u, :], u4(X)[:, u, :], True, True, after=[a, xe, am] if u == 0 else (), sig=(u == 3))
                if l < 5:
                    am = tt(pool, d4(E), d4(AT), mk(l + 1), ALU.mult, after=[y])
                if l:
                    o_, i_, z_ = late_xt
                    lx = [tt(dve, o_, o_, i_, ALU.add, after=[z_])]
                yield
                ym = af(Y, A, ACT.Copy, after=[y])
                yield
                if l < 5:
                    for u in range(4):
                        z = mm(u4(A)[:, u, :], u4(XT)[:, u, :], u4(Y)[:, u, :], True, True, after=[ym, *lx], sig=(u == 3))
                    xa = tt(dve, X, X, A, ALU.add, after=[z])
                for u in range(4):
                    z = mm(u4(Bk)[:, u, :], u4(Y)[:, u, :], u4(XT)[:, u, :], True, True, after=[ym, *lx], sig=(u == 3))
                if l < 5:
                    a = xa
                    late_xt = (XT, Bk, z)
                else:
                    a = tt(dve, XT, XT, Bk, ALU.add, after=[z])
                yield
            for u in range(4):
                af(u4(Y)[:, u, :], cs(vt, chunks[u]), ACT.Copy, after=[z, *src], par=u > 0, scale=beta[:, cols[u]:cols[u] + 1])
                kb = af(u4(E)[:, u, :], cs(kt, chunks[u]), ACT.Copy, after=[a], par=True, scale=bg[:, cols[u]:cols[u] + 1])
            for d in range(2):
                c0 = chunks[2 * d]
                qg = tt(dve, AT[:, d * 256:(d + 1) * 256], TB[:, d * 256:(d + 1) * 256],
                        qT_[:, c0 * 128:(c0 + 2) * 128], ALU.mult, after=[z])
            yield
            for u in range(4):
                uu = mm(u4(A)[:, u, :], u4(XT)[:, u, :], u4(Y)[:, u, :], True, True, after=[kb, a], sig=(u == 3))
            for u in range(4):
                ww = mm(u4(Bk)[:, u, :], u4(E)[:, u, :], u4(XT)[:, u, :], True, True, sig=(u == 3))
            yield
            ue = af(X, A, ACT.Copy, after=[uu])
            we = af(Y, Bk, ACT.Copy, after=[ww], scale=-1.0)
            for u in range(4):
                kd = af(u4(XT)[:, u, :], cs(kt, chunks[u]), ACT.Copy, after=[ww], par=u > 0, scale=kdf[:, cols[u]:cols[u] + 1])
            yield
            dn_st[("out", h, j)] = [ue, we, kd, qg]
            done[("pre", h, j)] = True

        def recursion(h, ob):
            OA = OAS[h % 2]
            D3 = bank(7)
            ws = D3[:, 0:256].rearrange("p (d c) -> p d c", d=2)
            oo = D3[:, 256:512].rearrange("p (d c) -> p d c", d=2)
            mset(dve, St, 0.0, after=dn_mark)
            s_tok = [dve.last()]
            for j in range(4):
                while not done.get(("pre", h, j)):
                    yield "idle"
                AT, X, XT, Y, aT, E, TB = sets[(4 * h + j) % 3]
                u4 = lambda a: a.rearrange("p (u c) -> p u c", c=128)
                pre = dn_st[("out", h, j)]
                for s in range(2):
                    us = (s, 3 - s)
                    chs = (2 * j + s, 7 - 2 * j - s)
                    for d in range(2):
                        w = mm(ws[:, d, :], u4(Y)[:, us[d], :], St[:, d, :], True, True,
                               after=[*pre, *s_tok, *dn_st["free7"]], sig=(d == 1))
                    yield
                    v = tt(dve, Vn, ws, u4(X)[:, s:4 - s:3 - 2 * s, :], ALU.add, after=[w])
                    yield
                    for d in range(2):
                        mm(oo[:, d, :], u4(AT)[:, us[d], :], St[:, d, :], True, False, after=[v])
                        mm(oo[:, d, :], u4(aT)[:, us[d], :], Vn[:, d, :], False, True)
                    for d in range(2):
                        w = mm(ws[:, d, :], u4(XT)[:, us[d], :], Vn[:, d, :], True, True, sig=(d == 1))
                    yield
                    for d in range(2):
                        cl = d * 32 + h * 8 + chs[d]
                        a = stt(St[:, d, :], St[:, d, :], eGL[:, cl:cl + 1], ws[:, d, :], ALU.mult, ALU.add, after=[w])
                    s_tok = [a]
                    for d in range(2):
                        o = OA[:, chs[d], :]
                        if j < 2:
                            a = dve.put(lambda e, o=o, d=d: e.tensor_copy(o, oo[:, d, :]),
                                        [w, *dn_st.get(("oa", h - 2), dn_mark)])
                        else:
                            a = tt(dve, o, o, oo[:, d, :], ALU.add)
                    dn_st["free7"] = [a]
                    yield
                dn_st[("set", (4 * h + j) % 3)] = [pe.last(), a]
                done[("rec", h, j)] = True
            out_free[ob] = [pe.last(), a]
            done[("dn", h)] = True

        def finish(h):
            zt, e = ZT, SQ
            OA = OAS[h % 2]
            while h and not done.get(("dnall", h - 1)):
                yield "idle"
            lz = dma(pool, c_dz[h % 2], zt, dz_d.rearrange("(t p) c -> p t c", p=128)[:, :, h * 128:(h + 1) * 128],
                     after=[*spilled["dz"], *mark, *dn_st.get("z_free", [])])
            yield lz
            lz = silu_in_place(zt, True, after=[lz])
            yield
            while not done.get(("dn", h)):
                yield "idle"
            a = af(e, OA, ACT.Square, after=[*out_free[OB[h]], *dn_st.get("sq_free", [])])
            yield
            a = red(ss[:, 48:56], e, ALU.add, after=[a, *dn_st.get("rs_free", [])])
            dn_st["sq_free"] = [a]
            yield
            r = rsqrt((48, 56), 128, after=[a])
            yield
            tt(dve, OA, OA, rs[:, 48:56].unsqueeze(2).to_broadcast([128, 8, 128]), ALU.mult, after=[r])
            dn_st["rs_free"] = [dve.last()]
            a = tt(dve, OA, OA, dnw.unsqueeze(1).to_broadcast([128, 8, 128]), ALU.mult)
            q = dve if h == 3 else pool
            a = tt(q, OA, OA, zt, ALU.mult, after=[lz, a])
            dn_st["z_free"] = [a]
            w = dma(pool, c_mix[2], mix_d.rearrange("(t p) c -> p t c", p=128)[:, :, 512 + h * 128:512 + (h + 1) * 128],
                    OA, after=[a])
            dn_st[("oa", h)] = [w]
            done[("dnall", h)] = True

        def lane(s):
            for n in range(s, 16, 3):
                yield from half_inverse(n // 4, OB[n // 4], n % 4, s)

        def rec_lane():
            for h in range(4):
                while h >= 2 and not done.get(("dnall", h - 2)):
                    yield "idle"
                yield from recursion(h, OB[h])

        for s_ in range(3):
            spawn(lane(s_))
        spawn(rec_lane())
        spawn(prepare_lane())
        for h in range(4):
            spawn(finish(h))
        drain()

        lent.close()
        HH = lent.enter_context(nc.sbuf_tensor("HH2", [128, 8, 1024], F32R))
        HL = lent.enter_context(nc.sbuf_tensor("HL2", [128, 8, 1024], F32R))
        area = Area(base)
        mark = fence()
        use_banks(list(range(8)), mark)
        ring = [area.take(1024) for _ in range(4)]
        h2 = [area.take(1024) for _ in range(3)]
        junk = area.take(1024)
        c_ring = [slot(f"c_ring{i}") for i in range(4)]
        c_x1 = slot("c_x1out")
        ring_free = [list(mark) for _ in range(4)]
        nring = [0]

        def feed(src):
            i = nring[0] % 4
            nring[0] += 1
            tok = dma(sp, c_ring[i], ring[i], src, after=ring_free[i])
            return ring[i], tok, i

        def stage_in(src_d):
            fed = {}
            for t in range(8):
                for n in range(t, min(8, t + 4)):
                    if n not in fed:
                        fed[n] = feed(src_d[n * 128:(n + 1) * 128, :])
                buf, tok, i = fed[t]
                yield tok
                to_stationary(t, buf, [tok])
                ring_free[i] = [pe.last()]
                yield

        def xt(t):
            return TM[:, t // 4, (t % 4) * 1024:(t % 4 + 1) * 1024]

        act.put(lambda e: e.activation(dummy[:, 0:1], half, ACT.Copy), mark)
        mset(dve, dummy[:, 1:2], 0.0, after=mark)
        ht.clear()
        spawn(stage_in(mix_d))
        c_xr = [slot(f"c_xr{i}") for i in range(8)]
        for t in range(8):
            dma(pool, c_xr[t], xt(t), x[t * 128:(t + 1) * 128, :], after=mark)
        h2_free = [list(mark) for _ in range(3)]
        todo = []
        ht2 = {}

        def wo_consume(cb):
            def f(t, ps, tok):
                o = xt(t)[:, cb * 512:(cb + 1) * 512]
                a = tt(dve, o, ps, o, ALU.add, after=[tok, c_xr[t].token()])
                if cb:
                    todo.append((t, a, tok))
                return [a]
            return f

        def norm_mid():
            for t in range(8):
                while not todo:
                    yield "idle"
                t_, a, tok = todo.pop(0)
                dma(pool, c_x1, x1_d[t * 128:(t + 1) * 128, :], xt(t), after=[a])
                s = af(junk, xt(t), ACT.Square, after=[a], accum_out=ss[:, t:t + 1])
                r = rsqrt((t, t + 1), 1024, after=[s])
                b = ts(dve, h2[t % 3], xt(t), rs[:, t:t + 1], None, ALU.mult, after=[r, *h2_free[t % 3]])
                yield
                ht2[t] = to_stationary(t, h2[t % 3], [b])
                h2_free[t % 3] = [pe.last()]
                yield

        token_groups(wo_consume(0), staged)
        spawn(norm_mid())
        token_groups(wo_consume(1), staged)
        drain()
        ht = ht2

        area = Area(base, WKW - 512)
        mark = fence()
        lanes = [dict(qT=area.take(1024), kT=area.take(1024), L=area.take(1024), P=area.take(1025)) for _ in range(2)]
        sqt = area.take(256)
        sm = area.take(128)
        sbufs = [area.take(512) for _ in range(3)]
        c_sb = slot("c_sb")
        c_oa = [slot(f"c_oa{i}") for i in range(3)]
        mset(dve, sqt, 0.0, after=mark)
        mset(pool, tail, 0.0, after=mark)
        act.put(lambda e: e.activation(lanes[0]["L"][:, 0:1], sqt[:, 0:1], ACT.Copy), [*mark, dve.last()])
        dma(pool, c_sb, sm, masks[17], after=mark)
        w_start = [dve.last(), act.last(), pool.last(), c_sb.token()]
        use_banks([0, 1], mark)
        for b_ in range(2, 8):
            w_start += mfree[b_]
        tm_free = [list(mark) for _ in range(3)]
        state = {}

        def norm_consume(buf, dh, ng, cols):
            B = TM[:, buf, :].rearrange("p (t c) -> p t c", c=512)

            def f(t, ps, tok):
                a = af(B[:, t, :], ps, ACT.Copy, after=[tok, *tm_free[buf]])
                q = B[:, t, 0:256]
                tt(dve, sqt, q, q, ALU.mult, after=[a, *w_start])
                red(ss[:, cols + t * ng:cols + t * ng + ng], sqt.rearrange("p (g d) -> p g d", d=dh), ALU.add)
                return [a]
            return f

        def sb_side(h, buf, ev):
            ln = h % 2
            W = lanes[ln]
            qT, kT, L, Pm = W["qT"], W["kT"], W["L"], W["P"]
            z0, tb = (2, 4) if ln == 0 else (5, 7)
            st = lambda n: state.get((n, ln), [])
            B = TM[:, buf, :].rearrange("p (t c) -> p t c", c=512)
            qk = B[:, :, 0:256].rearrange("p t (g d) -> p t g d", d=128)
            c0 = (h % 3) * 16
            r = rsqrt((c0, c0 + 16), 128, after=[ev])
            sc = rs[:, c0:c0 + 16].rearrange("p (t g) -> p t g", g=2)
            for t in range(8):
                a = tt(dve, qk[:, t], qk[:, t], sc[:, t].unsqueeze(2).to_broadcast([128, 2, 128]), ALU.mult, after=[r])
            yield
            while h >= 2 and not done.get(("sb", h - 2)):
                yield "idle"
            free = st("tb")
            for dst, o, g in ((qT, 0, sq_), (kT, 128, sk_)):
                for f in transposed(dst, lambda t, o=o: B[:, t, o:o + 128], g, [a, *w_start, *st("qk")], tb, free):
                    free = f
                    yield
            state[("tb", ln)] = free
            qk_tok = free[0]
            sz = silu_in_place(B[:, :, 384:512], True, after=[pe.last()])
            for i in range(8):
                nk = (i + 1) * 128
                zp = PS[:, z0 * 512:z0 * 512 + nk]
                for c in range(0, nk, 512):
                    w = min(512, nk - c)
                    tok = mm(PS[:, z0 * 512 + c:z0 * 512 + c + w], qT[:, i * 128:(i + 1) * 128], kT[:, c:c + w], True, True,
                             after=[qk_tok, *st("z")], sig=True)
                l = L[:, 0:nk]
                a = af(l, zp, ACT.Abs, after=[tok, *st("L")])
                a = af(l, l, ACT.Exp, scale=-1.0)
                a = af(l, l, ACT.Ln, bias=1.0)
                yield
                pm = Pm[:, 0:nk]
                stt(pm, zp, 0.0, l, ALU.max, ALU.add, after=[a, *st("P")])
                b = tt(dve, l, zp, pm, ALU.subtract)
                state[("z", ln)] = [b]
                tt(dve, Pm[:, nk - 128:nk], Pm[:, nk - 128:nk], sm, ALU.mult)
                if i == 0:
                    mset(dve, Pm[:, 1024:1025], 0.0)
                yield
                dve.put(lambda e, nk=nk: e.tensor_tensor_scan(
                    Pm[:, 1:nk][:, ::-1], one.to_broadcast([128, nk - 1]), Pm[:, 1:nk][:, ::-1], 0.0,
                    ALU.mult, ALU.add), cost=70 + 2.1 * nk)
                b = tt(dve, L[:, 0:nk - 1], L[:, 0:nk - 1], Pm[:, 1:nk], ALU.subtract)
                yield
                a = af(l, l, ACT.Exp, after=[b])
                yield
                a = tt(dve, L[:, nk - 128:nk], L[:, nk - 128:nk], sm, ALU.mult, after=[a])
                yield
                for g in range(0, i + 1, 4):
                    n = min(4, i + 1 - g)
                    for jj in range(n):
                        tok = tr(bank(tb)[:, jj * 128:(jj + 1) * 128], L[:, (g + jj) * 128:(g + jj + 1) * 128],
                                 after=[a, *st("tb")], sig=(jj == n - 1))
                    f = af(Pm[:, g * 128:(g + n) * 128], bank(tb, n * 128), ACT.Copy, after=[tok, a])
                    state[("tb", ln)] = [f]
                    yield
                state[("L", ln)] = [tok]
                O = bank(tb, 128)
                for jj in range(i + 1):
                    tok = mm(O, Pm[:, jj * 128:(jj + 1) * 128], B[:, jj, 256:384], jj == 0, jj == i,
                             after=[f], sig=(jj == i))
                state[("P", ln)] = [tok]
                o = tt(dve, B[:, i, 128:256], O, B[:, i, 384:512], ALU.mult, after=[tok, sz])
                state[("tb", ln)] = [o]
                yield
            state[("qk", ln)] = [pe.last()]
            w = dma(pool, c_oa[buf], oa_d.rearrange("(t p) c -> p t c", p=128)[:, :, h * 128:(h + 1) * 128],
                    B[:, :, 128:256], after=[o])
            tm_free[buf] = [w, pe.last(), o]
            done[("sb", h)] = True

        brow = tail
        c_br = slot("c_br")
        c_sg = [slot(f"c_sg{i}") for i in range(3)]
        sgf = [[] for _ in range(3)]
        n_s = [0]
        br_free = [[pool.last()]]

        def m_consume(g, cb, br):
            def f(t, ps, tok):
                i = n_s[0] % len(sbufs)
                n_s[0] += 1
                s = sbufs[i]
                a = tt(dve, s, ps, brow, ALU.add, after=[tok, br, *w_start, *sgf[i]])
                br_free[0] = [a]
                w = dma(pool, c_sg[i], sig_d[g, t * 128:(t + 1) * 128, cb * 512:(cb + 1) * 512], s, after=[a])
                sgf[i] = [w]
                return [a]
            return f

        def merge_gate(g, cb):
            br = dma(pool, c_br, brow, b_merge[g:g + 1, cb * 512:(cb + 1) * 512].to_broadcast([128, 512]),
                     after=br_free[0])
            token_groups(m_consume(g, cb, br), lambda t: [])

        for h in sb_order:
            if not isinstance(h, int):
                merge_gate(*h)
                continue
            buf = h % 3
            while h >= 3 and not done.get(("sb", h - 3)):
                pump(True)
            token_groups(norm_consume(buf, 128, 2, (h % 3) * 16), lambda t: [ht[t]])
            spawn(sb_side(h, buf, dve.last()))

        def plain_consume(buf):
            B = TM[:, buf, :].rearrange("p (t c) -> p t c", c=512)

            def f(t, ps, tok):
                return [af(B[:, t, :], ps, ACT.Copy, after=[tok, *tm_free[buf]])]
            return f

        while not done.get(("sb", 5)):
            pump(True)
        token_groups(plain_consume(2), lambda t: [])
        first_q = act.last()
        while not done.get(("sb", 6)):
            pump(True)
        token_groups(plain_consume(0), lambda t: [])
        first_v = act.last()
        drain()

        area = Area(base, WKW - 512)
        mark = fence()
        CS = area.take(2048).rearrange("p (s t c) -> p s t c", s=2, c=128)
        RQ = area.take(2048).rearrange("p (d t) -> p d t", d=2)
        RK = area.take(2048).rearrange("p (d t) -> p d t", d=2)
        tq = [area.take(256).rearrange("p (g c) -> p g c", g=2) for _ in range(4)]
        Sr = [area.take(512).rearrange("p (d e) -> p d e", d=2) for _ in range(2)]
        aTr = area.take(128)
        rm = area.take(512).rearrange("p (h c) -> p h c", h=4)
        rc = area.take(8)
        grow = area.take(256)
        sbufs = [area.take(512) for _ in range(2)]
        c_rt = slot("c_rt")
        c_gr = slot("c_gr")
        c_ob = slot("c_ob")
        mset(dve, aTr, 0.0, after=mark)
        mset(pool, tq[2], 0.0, after=mark)
        act.put(lambda e: e.activation(Sr[0][:, 0, 0:1], aTr[:, 0:1], ACT.Copy), [*mark, dve.last()])
        dma(pool, c_rt, CS, cossin.rearrange("s (t p) c -> p s t c", p=128), after=mark)
        dma(pool, c_rt, rm, retmask.rearrange("h p c -> p h c"), after=mark)
        dma(pool, c_rt, rc, retcol, after=mark)
        w_start = [dve.last(), act.last(), pool.last(), c_rt.token()]
        tm_free = [list(mark) for _ in range(3)]
        state = {"b4": [], "b5": [], "b6": [], "qk": []}
        gam = [1.0 - 2.0 ** (-5.0 - h) for h in range(4)]

        def ret_side(h, bx, by, ev):
            BX = TM[:, bx, :].rearrange("p (t c) -> p t c", c=512)
            BY = TM[:, by, :].rearrange("p (t c) -> p t c", c=512)
            for t in range(8):
                v = BX[:, t, :].rearrange("p (g s c) -> p g s c", g=2, s=2)
                t1, t2 = v[:, :, 0, :], v[:, :, 1, :]
                c = CS[:, 0, t, :].unsqueeze(1).to_broadcast([128, 2, 128])
                s = CS[:, 1, t, :].unsqueeze(1).to_broadcast([128, 2, 128])
                tt(dve, tq[0], t1, c, ALU.mult, after=[*ev, *w_start])
                a = tt(dve, tq[1], t2, s, ALU.mult)
                b = tt(pool, tq[2], t1, s, ALU.mult, after=[*ev, *w_start])
                b = tt(pool, tq[3], t2, c, ALU.mult)
                tt(dve, t1, tq[0], tq[1], ALU.subtract, after=[b])
                b = tt(pool, t2, tq[2], tq[3], ALU.add, after=[a])
                yield
            rope = [b, dve.last()]
            while h and not done.get(("ret", h - 1)):
                yield "idle"
            gr = dma(pool, c_gr, grow, ret_gain[h:h + 1, :].to_broadcast([128, 256]), after=[*w_start, *state.get("grow", [])])
            free = state["b4"]
            for dst, o in ((RQ, 0), (RK, 256)):
                for dh in range(2):
                    for f in transposed(dst[:, dh, :], lambda t, o=o, dh=dh: BX[:, t, o + dh * 128:o + dh * 128 + 128],
                                        None, [*rope, *w_start, *state["qk"]], 4, free):
                        free = f
                        yield
            state["b4"] = free
            tr_done = [pe.last(), free[0]]
            while not done.get(("vz", h)):
                yield "idle"
            tr_done = [*tr_done, *done[("vz", h)]]
            kd = ts(dve, BX[:, :, 256:512], BX[:, :, 256:512], rc[:, 4 + h:5 + h], None, ALU.mult, after=tr_done)
            sz = silu_in_place(BY[:, :, 256:512], False, after=tr_done)
            yield
            s_tok = [mset(dve, Sr[0], 0.0, after=w_start)]
            for c in range(8):
                cc = slice(c * 128, (c + 1) * 128)
                S0, S1 = Sr[c % 2], Sr[(c + 1) % 2]
                b5 = bank(5, 128)
                for dh in range(2):
                    tok = mm(b5, RK[:, dh, cc], RQ[:, dh, cc], dh == 0, dh == 1, after=[*tr_done, *state["b5"]],
                             sig=(dh == 1))
                yield
                a = tt(dve, aTr, b5, rm[:, h, :], ALU.mult, after=[tok, *state.get("a", [])])
                yield
                o = bank(6, 256)
                for dh in range(2):
                    mm(o, RQ[:, dh, cc], S0[:, dh, :], dh == 0, False, after=[*s_tok, *state["b6"]])
                tok = mm(o, aTr, BY[:, c, 0:256], False, True, after=[a], sig=True)
                state["a"] = [tok]
                state["b5"] = [a]
                if c < 7:
                    for dh in range(2):
                        u = mm(bank(7)[:, dh * 256:(dh + 1) * 256], BX[:, c, 256 + dh * 128:256 + (dh + 1) * 128],
                               BY[:, c, 0:256], True, True, after=[kd, *s_tok], sig=(dh == 1))
                yield
                oe = ts(dve, BX[:, c, 0:256], o, rc[:, h:h + 1], None, ALU.mult, after=[tok])
                state["b6"] = [oe]
                if c < 7:
                    a = stt(S1, S0, gam[h] ** 128, bank(7).rearrange("p (d e) -> p d e", d=2), ALU.mult, ALU.add, after=[u])
                    s_tok = [a]
                yield
            state["qk"] = [pe.last()]
            pe_done = pe.last()
            O = BX[:, :, 0:256]
            e = BX[:, :, 256:512]
            tt(dve, e, O, O, ALU.mult, after=[pe_done])
            a = red(ss[:, h % 2 * 8:h % 2 * 8 + 8], e, ALU.add)
            r = rsqrt((h % 2 * 8, h % 2 * 8 + 8), 256, after=[a])
            yield
            tt(dve, O, O, rs[:, h % 2 * 8:h % 2 * 8 + 8].unsqueeze(2).to_broadcast([128, 8, 256]), ALU.mult, after=[r])
            a = tt(dve, O, O, grow.unsqueeze(1).to_broadcast([128, 8, 256]), ALU.mult, after=[gr])
            state["grow"] = [a]
            a = tt(dve, O, O, BY[:, :, 256:512], ALU.mult, after=[sz])
            w = dma(pool, c_ob, ob_d.rearrange("(t p) c -> p t c", p=128)[:, :, h * 256:(h + 1) * 256], O, after=[a])
            tm_free[bx] = [w, pe_done, a]
            tm_free[by] = [pe_done, a]
            done[("ret", h)] = True

        sgf = [list(mark) for _ in range(2)]
        spawn(ret_side(0, 2, 0, [first_q]))
        done[("vz", 0)] = [first_v]
        for h in range(1, 4):
            bx, by = (2 * h + 2) % 3, 2 * h % 3
            while h >= 2 and not done.get(("ret", h - 2)):
                pump(True)
            token_groups(plain_consume(bx), lambda t: [])
            spawn(ret_side(h, bx, by, [act.last()]))
            if h == 1:
                merge_gate(1, 0)
            while not done.get(("ret", h - 1)):
                pump(True)
            token_groups(plain_consume(by), lambda t: [])
            done[("vz", h)] = [act.last()]
        merge_gate(1, 1)
        ring = [TM[:, 1, i * 1024:(i + 1) * 1024] for i in range(4)]
        ring_free = [[*tm_free[1], *(s.token() for s in c_oa)] for _ in range(4)]
        nring[0] = 0
        c_ring[:] = [slot(f"c_ringb{i}") for i in range(4)]
        ht.clear()
        spawn(stage_in(oa_d))
        drain()

        area = Area(base)
        mark = fence()
        use_banks(list(range(8)), mark)
        ring_free = [x + mark for x in ring_free]
        sgt = [area.take(512) for _ in range(4)]
        ot = [area.take(512) for _ in range(4)]
        c_st = [slot(f"c_st{i}") for i in range(4)]
        c_ot = [slot(f"c_ot{i}") for i in range(4)]
        sg_free = [list(mark) for _ in range(4)]
        ot_free = [list(mark) for _ in range(4)]
        n_g = [0]

        def merged(t):
            return TM[:, t // 4 * 2, (t % 4) * 1024:(t % 4 + 1) * 1024]

        def feed_small(src):
            i = n_g[0] % 4
            n_g[0] += 1
            tok = dma(pool, c_st[i], sgt[i], src, after=sg_free[i])
            return sgt[i], tok, i

        fed = {}

        def restage(src, cb, leave=None):
            def hook(t):
                for n in ((0, 1) if t == 0 else (t + 1,)):
                    if n < 8:
                        fed[n] = feed_small(src[n * 128:(n + 1) * 128, cb * 512:(cb + 1) * 512])
                while t not in ht:
                    pump(True)
                now = [ht[t]]
                if leave is not None and t:
                    leave.append(t - 1)
                return now
            return hook

        def swap_in(src_d, left, new):
            ahead = {}
            for t in range(8):
                for n in range(t, min(8, t + 3)):
                    if n not in ahead:
                        ahead[n] = feed(src_d[n * 128:(n + 1) * 128, :])
                while t not in left:
                    yield "idle"
                buf, tok, i = ahead[t]
                new[t] = to_stationary(t, buf, [tok])
                ring_free[i] = [pe.last()]
                yield

        def swap_merged(left, new):
            for t in range(8):
                while t not in left:
                    yield "idle"
                yield mdone[t]
                new[t] = to_stationary(t, merged(t), [mdone[t]])
                yield

        def branch_consume(g, cb):
            def f(t, ps, tok):
                s, st, i = fed.pop(t)
                m = merged(t)[:, cb * 512:(cb + 1) * 512]
                st = af(s, s, ACT.Sigmoid, after=[st])
                if g == 0:
                    a = b = tt(dve, m, ps, s, ALU.mult, after=[tok, st, *mark])
                else:
                    a = tt(dve, s, ps, s, ALU.mult, after=[tok, st])
                    b = tt(dve, m, m, s, ALU.add)
                sg_free[i] = [b]
                mdone[t] = b
                return [a]
            return f

        mdone = {}
        token_groups(branch_consume(0, 0), restage(sig_d[0], 0))
        left, new = [], {}
        spawn(swap_in(ob_d, left, new))
        token_groups(branch_consume(0, 1), restage(sig_d[0], 1, left))
        left.append(7)
        ht = new
        token_groups(branch_consume(1, 0), restage(sig_d[1], 0))
        left, new = [], {}
        spawn(swap_merged(left, new))
        token_groups(branch_consume(1, 1), restage(sig_d[1], 1, left))
        left.append(7)
        ht = new

        def final_consume(cb):
            def f(t, ps, tok):
                s, st, i = fed.pop(t)
                o = ot[n_o[0] % 4]
                j = n_o[0] % 4
                n_o[0] += 1
                a = tt(dve, o, ps, s, ALU.add, after=[tok, st, *ot_free[j]])
                sg_free[i] = [a]
                w = dma(pool, c_ot[j], out[t * 128:(t + 1) * 128, cb * 512:(cb + 1) * 512], o, after=[a])
                ot_free[j] = [w]
                return [a]
            return f

        n_o = [0]
        token_groups(final_consume(0), restage(x1_d, 0))
        token_groups(final_consume(1), restage(x1_d, 1))

        ends = [s.token() for s in slots]

        block = ctx.enter_context(nc.Block())

        @block.sync
        def _(eng):
            sp.play(eng)
            for sem, v in ends:
                eng.wait_ge(sem, v)

        @block.tensor
        def _(eng):
            pe.play(eng)

        @block.scalar
        def _(eng):
            act.play(eng)

        @block.vector
        def _(eng):
            dve.play(eng)

        @block.gpsimd
        def _(eng):
            pool.play(eng)


def constants():
    i = np.arange(128)
    eye = np.eye(128, dtype=np.float32)
    planes = [eye]
    for b in (2, 4, 8, 16, 32, 64):
        pair = (i[:, None] // (2 * b)) == (i[None, :] // (2 * b))
        low = pair & (i[:, None] // b % 2 == 1) & (i[None, :] // b % 2 == 0)
        planes += [low.T.astype(np.float32), low.astype(np.float32)]
    pair = (i[:, None] // 2) == (i[None, :] // 2)
    low = pair & (i[:, None] % 2 == 1) & (i[None, :] % 2 == 0)
    planes += [low.T.astype(np.float32), low.astype(np.float32)]
    planes += [(i[:, None] <= i[None, :]).astype(np.float32), (i[:, None] >= i[None, :]).astype(np.float32)]
    planes += [(i[:, None] > i[None, :]).astype(np.float32)]
    masks = np.stack(planes)
    inv = (10000.0 ** (-np.arange(0, 256, 2, dtype=np.float32) / np.float32(256))).astype(np.float32)
    ang = np.arange(1024, dtype=np.float32)[:, None] * inv[None, :]
    cs = np.stack([np.cos(ang), np.sin(ang)]).astype(np.float32)
    rm = np.zeros((4, 128, 128), np.float32)
    rc = np.zeros((128, 8), np.float32)
    for h in range(4):
        lg = np.log1p(-np.exp2(-5.0 - h))
        s, t = i[:, None], i[None, :]
        rm[h] = np.where(s // 64 <= t // 64, np.exp(lg * (np.abs(t - s) - (t + 1.0))), 0.0) / 16.0
        rc[:, h] = np.exp(lg * (i + 1.0))
        rc[:, 4 + h] = np.exp(lg * (127.0 - i)) / 16.0
    return masks, cs, rm, rc


def kernel(**inputs):
    import concourse.bacc as bacc
    from concourse.bass_utils import run_bass_kernel_spmd

    a = {k: np.asarray(v)[0] for k, v in inputs.items()}
    masks, cs, rm, rc = constants()
    pad = np.pad(a["rpb"], ((0, 0), (0, 0), (48, 48)))
    tabs = np.stack([pad[:, :, 63 - w:127 - w] for w in range(64)], axis=2)
    arrays = {
        "x": a["x"],
        "norm_w": a["norm_w"].reshape(8, 128).T,
        "w_in": a["w_in"],
        "gq": a["qk_gain_q"][:, None],
        "gk": a["qk_gain_k"][:, None],
        "rpb": tabs,
        "conv_w": a["conv_w"].reshape(5, 12, 128).transpose(2, 1, 0),
        "a_log": a["a_log"].reshape(1, 8),
        "dt_bias": a["dt_bias"].reshape(1, 8),
        "dn_w": a["dn_norm_w"][None, :],
        "w_out": a["w_out"],
        "gain2": a["norm_gain_2"].reshape(8, 128).T,
        "w_in2": a["w_in_2"],
        "b_merge": a["b_merge_2"],
        "sbq": a["sb_q_gain_2"][:, None],
        "sbk": a["sb_k_gain_2"][:, None],
        "ret_gain": a["ret_out_gain_2"],
        "w_sb": a["w_branch_sb_2"],
        "w_ret": a["w_branch_ret_2"],
        "w_out2": a["w_out_2"],
        "masks": masks, "cossin": cs, "retmask": rm, "retcol": rc,
    }
    nc = bacc.Bacc("TRN2", target_bir_lowering=False, num_devices=1)
    given, args = {}, []
    for name, v in arrays.items():
        v = np.ascontiguousarray(v)
        given[f"in_{name}"] = v
        args.append(nc.dram_tensor(f"in_{name}", v.shape, mybir.dt.from_np(v.dtype), kind="ExternalInput").ap())
    args.append(nc.dram_tensor("out_0", [1024, 1024], F32, kind="ExternalOutput").ap())
    build(nc, *args)
    r = run_bass_kernel_spmd(nc, [given], core_ids=[0])
    return np.asarray(r.results[0]["out_0"]).reshape(1, 1024, 1024)
```
